# Optimizing a Trainium2 kernel written in Bass

```python
import math
import jax, jax.numpy as jnp
from jax import lax
import numpy as np

D_MODEL = 1024
BATCH = 1
SEQ = 1024
DEPTH = 1

ATT_HEADS = 8
ATT_KV_HEADS = 2
ATT_HEAD_DIM = 64
ATT_WIDTH = ATT_HEADS * ATT_HEAD_DIM
WINDOW = 128
ATT_BLOCK = 128
N_BUCKETS = 32
MAX_DISTANCE = 128
ML_HEADS = 4
ML_DQK = 64
ML_DV = 128
ML_WIDTH = ML_HEADS * ML_DV
ML_CHUNK = 64
CONV_K = 4
D_MIX = ATT_WIDTH + ML_WIDTH
IN_SPLITS = [ATT_WIDTH, ATT_KV_HEADS * ATT_HEAD_DIM, ATT_KV_HEADS * ATT_HEAD_DIM,
             ML_HEADS * ML_DQK, ML_HEADS * ML_DQK, ML_WIDTH, ML_WIDTH, ML_HEADS, ML_HEADS]
N_IN = sum(IN_SPLITS)
SPLIT_POINTS = [int(v) for v in np.cumsum(IN_SPLITS)[:-1]]
N_GROUPS = 4
EXPERTS_PER_GROUP = 4
N_EXPERTS = N_GROUPS * EXPERTS_PER_GROUP
TOP_K = 2
D_FF_EXPERT = 512
EPS = 1e-6

kernel_name = "hymba_swa_mlstm_hier_moe"

def rms_norm(x, g):
    xf = x.astype(jnp.float32)
    y = xf * lax.rsqrt(jnp.mean(xf * xf, axis=-1, keepdims=True) + EPS)
    return (y * g.astype(jnp.float32)).astype(x.dtype)

def t5_bucket(dist):
    max_exact = N_BUCKETS // 2
    d = jnp.maximum(dist, 1).astype(jnp.float32)
    large = max_exact + (jnp.log(d / max_exact) / math.log(MAX_DISTANCE / max_exact)
                         * (N_BUCKETS - max_exact)).astype(jnp.int32)
    large = jnp.minimum(large, N_BUCKETS - 1)
    return jnp.where(dist < max_exact, dist, large)

def swa_sink_attention(q, k, v, q_g, k_g, sink, rel_bias):
    B, S, _ = q.shape
    nb = S // ATT_BLOCK
    G = ATT_HEADS // ATT_KV_HEADS
    q = rms_norm(q.reshape(B, S, ATT_HEADS, ATT_HEAD_DIM), q_g)
    k = rms_norm(k.reshape(B, S, ATT_KV_HEADS, ATT_HEAD_DIM), k_g)
    v = v.reshape(B, S, ATT_KV_HEADS, ATT_HEAD_DIM)
    qb = q.reshape(B, nb, ATT_BLOCK, ATT_KV_HEADS, G, ATT_HEAD_DIM)
    pad = ((0, 0), (ATT_BLOCK, 0), (0, 0), (0, 0))
    kp = jnp.pad(k, pad).reshape(B, nb + 1, ATT_BLOCK, ATT_KV_HEADS, ATT_HEAD_DIM)
    vp = jnp.pad(v, pad).reshape(B, nb + 1, ATT_BLOCK, ATT_KV_HEADS, ATT_HEAD_DIM)
    kb = jnp.concatenate([kp[:, :-1], kp[:, 1:]], axis=2)
    vb = jnp.concatenate([vp[:, :-1], vp[:, 1:]], axis=2)
    scores = jnp.einsum('bnqkgd,bnskd->bnkgqs', qb, kb).astype(jnp.float32) * (ATT_HEAD_DIM ** -0.5)
    qi = jnp.arange(ATT_BLOCK)[:, None]
    kj = jnp.arange(2 * ATT_BLOCK)[None, :]
    dist = qi + ATT_BLOCK - kj
    in_window = (dist >= 0) & (dist < WINDOW)
    key_pos = jnp.arange(nb)[:, None, None] * ATT_BLOCK + kj[None] - ATT_BLOCK
    valid = in_window[None] & (key_pos >= 0)
    bucket = t5_bucket(jnp.clip(dist, 0, WINDOW - 1))
    bias = rel_bias.astype(jnp.float32)[bucket]
    bias = bias.transpose(2, 0, 1).reshape(ATT_KV_HEADS, G, ATT_BLOCK, 2 * ATT_BLOCK)
    logits = jnp.where(valid[None, :, None, None], scores + bias, -jnp.inf)
    sink_l = sink.astype(jnp.float32).reshape(ATT_KV_HEADS, G)[:, :, None, None]
    m = jnp.maximum(jnp.max(logits, axis=-1, keepdims=True), sink_l)
    p = jnp.exp(logits - m)
    probs = p / (jnp.sum(p, axis=-1, keepdims=True) + jnp.exp(sink_l - m))
    out = jnp.einsum('bnkgqs,bnskd->bnqkgd', probs.astype(vb.dtype), vb)
    return out.reshape(B, S, ATT_WIDTH)

def causal_conv_silu(x, w, b):
    K = w.shape[0]
    S = x.shape[1]
    xp = jnp.pad(x, ((0, 0), (K - 1, 0), (0, 0)))
    y = xp[:, 0:S] * w[0]
    for j in range(1, K):
        y = y + xp[:, j:j + S] * w[j]
    return jax.nn.silu(y + b)

def mlstm_chunkwise(q, k, v, i_pre, f_pre):
    B, S = q.shape[0], q.shape[1]
    nc = S // ML_CHUNK

    def to_chunks(a):
        a = a.reshape(B, nc, ML_CHUNK, ML_HEADS, *a.shape[3:])
        return jnp.moveaxis(a, (1, 3), (0, 2))

    qc = to_chunks(q.astype(jnp.float32))
    kc = to_chunks(k.astype(jnp.float32) * (ML_DQK ** -0.5))
    vc = to_chunks(v.astype(jnp.float32))
    lic = to_chunks(i_pre.astype(jnp.float32))
    lfc = to_chunks(jax.nn.log_sigmoid(f_pre.astype(jnp.float32)))
    causal = jnp.tril(jnp.ones((ML_CHUNK, ML_CHUNK), dtype=bool))

    def step(carry, inp):
        C, n, m = carry
        qt, kt, vt, li, lf = inp
        b = jnp.cumsum(lf, axis=-1)
        log_d = jnp.where(causal, b[..., :, None] - b[..., None, :] + li[..., None, :], -jnp.inf)
        m_inter = b + m[..., None]
        m_row = jnp.maximum(m_inter, jnp.max(log_d, axis=-1))
        d = jnp.exp(log_d - m_row[..., None])
        inter_scale = jnp.exp(m_inter - m_row)
        s = jnp.einsum('bhtd,bhsd->bhts', qt, kt) * d
        num = inter_scale[..., None] * jnp.einsum('bhvd,bhtd->bhtv', C, qt) + jnp.einsum('bhts,bhsv->bhtv', s, vt)
        den = inter_scale * jnp.einsum('bhd,bhtd->bht', n, qt) + jnp.sum(s, axis=-1)
        h = num / jnp.maximum(jnp.abs(den), jnp.exp(-m_row))[..., None]
        b_last = b[..., -1]
        log_w = b_last[..., None] - b + li
        m_next = jnp.maximum(b_last + m, jnp.max(log_w, axis=-1))
        w = jnp.exp(log_w - m_next[..., None])
        decay = jnp.exp(b_last + m - m_next)
        C_next = decay[..., None, None] * C + jnp.einsum('bhs,bhsv,bhsd->bhvd', w, vt, kt)
        n_next = decay[..., None] * n + jnp.einsum('bhs,bhsd->bhd', w, kt)
        return (C_next, n_next, m_next), h

    init = (jnp.zeros((B, ML_HEADS, ML_DV, ML_DQK), jnp.float32),
            jnp.zeros((B, ML_HEADS, ML_DQK), jnp.float32),
            jnp.zeros((B, ML_HEADS), jnp.float32))
    _, h = lax.scan(step, init, (qc, kc, vc, lic, lfc))
    h = jnp.moveaxis(h, (0, 2), (1, 3))
    return h.reshape(B, S, ML_HEADS, ML_DV)

def hier_moe(x, w_rg, b_rg, w_re, b_re, w_gate, w_up, w_down):
    B, S, D = x.shape
    t = x.reshape(-1, D)
    g_logits = (t @ w_rg).astype(jnp.float32) + b_rg.astype(jnp.float32)
    g_prob = jax.nn.softmax(g_logits, axis=-1)
    grp = jnp.argmax(g_logits, axis=-1)
    p_grp = jnp.take_along_axis(g_prob, grp[:, None], axis=-1)
    e_logits = ((t @ w_re).astype(jnp.float32) + b_re.astype(jnp.float32)).reshape(-1, N_GROUPS, EXPERTS_PER_GROUP)
    e_in = jnp.take_along_axis(e_logits, grp[:, None, None], axis=1)[:, 0]
    e_prob = jax.nn.softmax(e_in, axis=-1)
    top_p, top_i = lax.top_k(e_prob, TOP_K)
    top_p = top_p / jnp.sum(top_p, axis=-1, keepdims=True)
    weights = p_grp * top_p
    expert_ids = grp[:, None] * EXPERTS_PER_GROUP + top_i
    combine = jnp.sum(jax.nn.one_hot(expert_ids, N_EXPERTS, dtype=jnp.float32) * weights[..., None], axis=1)
    y = jnp.zeros(t.shape, jnp.float32)
    for e in range(N_EXPERTS):
        h = jax.nn.silu(t @ w_gate[e]) * (t @ w_up[e])
        y = y + combine[:, e:e + 1] * (h @ w_down[e]).astype(jnp.float32)
    return y.astype(x.dtype).reshape(B, S, D)

def setup_inputs(seed: int = 0) -> dict:
    key = jax.random.key(seed)
    ks = jax.random.split(key, 20)
    f32 = jnp.float32
    nrm = lambda k, shape, s: jax.random.normal(k, shape, f32) * s
    gate_b = jnp.concatenate([
        nrm(ks[9], (DEPTH, ML_HEADS), 0.1),
        jnp.linspace(3.0, 6.0, ML_HEADS, dtype=f32)[None, :] + nrm(ks[10], (DEPTH, ML_HEADS), 0.1)], axis=-1)
    return {
        "x": nrm(ks[0], (BATCH, SEQ, D_MODEL), 1.0),
        "rel_bias": nrm(ks[1], (N_BUCKETS, ATT_HEADS), 0.5),
        "norm_mix_g": 1.0 + nrm(ks[2], (DEPTH, D_MODEL), 0.02),
        "w_in": nrm(ks[3], (DEPTH, D_MODEL, N_IN), D_MODEL ** -0.5),
        "q_norm_g": 1.0 + nrm(ks[4], (DEPTH, ATT_HEAD_DIM), 0.02),
        "k_norm_g": 1.0 + nrm(ks[5], (DEPTH, ATT_HEAD_DIM), 0.02),
        "attn_sink": nrm(ks[6], (DEPTH, ATT_HEADS), 0.5),
        "conv_w": nrm(ks[7], (DEPTH, CONV_K, 2 * ML_HEADS * ML_DQK), CONV_K ** -0.5),
        "conv_b": nrm(ks[8], (DEPTH, 2 * ML_HEADS * ML_DQK), 0.02),
        "gate_b": gate_b,
        "mlstm_norm_g": 1.0 + nrm(ks[11], (DEPTH, ML_WIDTH), 0.02),
        "w_out": nrm(ks[12], (DEPTH, D_MIX, D_MODEL), D_MIX ** -0.5),
        "norm_ffn_g": 1.0 + nrm(ks[13], (DEPTH, D_MODEL), 0.02),
        "w_router_group": nrm(ks[14], (DEPTH, D_MODEL, N_GROUPS), D_MODEL ** -0.5),
        "b_router_group": nrm(ks[15], (DEPTH, N_GROUPS), 0.01),
        "w_router_expert": nrm(ks[16], (DEPTH, D_MODEL, N_EXPERTS), D_MODEL ** -0.5),
        "b_router_expert": nrm(ks[17], (DEPTH, N_EXPERTS), 0.01),
        "w_gate": nrm(ks[18], (DEPTH, N_EXPERTS, D_MODEL, D_FF_EXPERT), D_MODEL ** -0.5),
        "w_up": nrm(jax.random.fold_in(ks[18], 1), (DEPTH, N_EXPERTS, D_MODEL, D_FF_EXPERT), D_MODEL ** -0.5),
        "w_down": nrm(ks[19], (DEPTH, N_EXPERTS, D_FF_EXPERT, D_MODEL), D_FF_EXPERT ** -0.5),
    }

def reference(x, rel_bias, norm_mix_g, w_in, q_norm_g, k_norm_g, attn_sink, conv_w, conv_b, gate_b,
              mlstm_norm_g, w_out, norm_ffn_g, w_router_group, b_router_group, w_router_expert,
              b_router_expert, w_gate, w_up, w_down):
    B, S, _ = x.shape
    for l in range(DEPTH):
        hn = rms_norm(x, norm_mix_g[l])
        proj = hn @ w_in[l]
        q_a, k_a, v_a, q_m, k_m, v_m, o_m, i_m, f_m = jnp.split(proj, SPLIT_POINTS, axis=-1)
        att = swa_sink_attention(q_a, k_a, v_a, q_norm_g[l], k_norm_g[l], attn_sink[l], rel_bias)
        qk_m = causal_conv_silu(jnp.concatenate([q_m, k_m], axis=-1), conv_w[l], conv_b[l])
        q_m, k_m = jnp.split(qk_m, 2, axis=-1)
        i_pre = i_m + gate_b[l, :ML_HEADS]
        f_pre = f_m + gate_b[l, ML_HEADS:]
        h_m = mlstm_chunkwise(q_m.reshape(B, S, ML_HEADS, ML_DQK), k_m.reshape(B, S, ML_HEADS, ML_DQK),
                              v_m.reshape(B, S, ML_HEADS, ML_DV), i_pre, f_pre).astype(x.dtype)
        h_m = rms_norm(h_m, mlstm_norm_g[l].reshape(ML_HEADS, ML_DV)).reshape(B, S, ML_WIDTH) * jax.nn.sigmoid(o_m)
        x = x + jnp.concatenate([att, h_m], axis=-1) @ w_out[l]
        x = x + hier_moe(rms_norm(x, norm_ffn_g[l]), w_router_group[l], b_router_group[l],
                         w_router_expert[l], b_router_expert[l], w_gate[l], w_up[l], w_down[l])
    return x


_drawn_inputs = setup_inputs


def setup_inputs(seed=0):
    import zlib

    import numpy as np

    out = dict(_drawn_inputs(seed))
    spreads = {}
    factors = {'q_norm_g': 6.43,
     'k_norm_g': 6.996,
     'attn_sink': 64.0,
     'conv_b': 2.866,
     'mlstm_norm_g': 10.103,
     'b_router_group': 62.3,
     'b_router_expert': 14.593,
     'norm_ffn_g': 3.235}
    for name, (base, spread) in spreads.items():
        noise = np.random.default_rng([zlib.crc32(name.encode()), seed]).standard_normal(out[name].shape)
        drawn = base * np.exp(spread * noise) if base else spread * noise
        out[name] = __import__('jax').numpy.asarray(drawn.astype(out[name].dtype))
    for name, factor in factors.items():
        out[name] = (out[name] * factor).astype(out[name].dtype)
    return out
```

```python
import concourse.bass as bass
from concourse import mybir
from contextlib import ExitStack


def hymba_layer_program(nc, x, rel_bias, norm_mix_g, w_in, q_norm_g, k_norm_g, attn_sink, conv_w, conv_b,
                        gate_b, mlstm_norm_g, w_out, norm_ffn_g, w_router_group, b_router_group,
                        w_router_expert, b_router_expert, w_gate, w_up, w_down, bucket_onehot, out):
    F32 = mybir.dt.float32
    I32 = mybir.dt.int32
    U32 = mybir.dt.uint32
    ALU = mybir.AluOpType
    ACT = mybir.ActivationFunctionType
    AX = mybir.AxisListType.X

    P = 128
    S, D = x.shape[1], x.shape[2]
    TILES = S // P
    KC = D // P
    HEADS, HD = attn_sink.shape[1], q_norm_g.shape[1]
    KVH = 2
    G = HEADS // KVH
    AW = HEADS * HD
    KVW = KVH * HD
    MH = gate_b.shape[1] // 2
    CH = conv_w.shape[2]
    TAPS = conv_w.shape[1]
    CC = CH // P
    DQK = CH // 2 // MH
    MW = mlstm_norm_g.shape[1]
    DV = MW // MH
    VE = DV + 1
    PAIRS = MH // 2
    NG = w_router_group.shape[2]
    NE = w_router_expert.shape[2]
    EPG = NE // NG
    FF = w_gate.shape[3]
    FC = FF // P
    HALF = D // 2
    EPS = 1e-6
    NEG = -1.0e30
    NBK = rel_bias.shape[0]
    RLEN = 3 * P
    MAXT = 2 * S // P + NE
    TROWS = NE * S + 2 * P
    OUTR = S + P

    x2 = x.rearrange("b s d -> (b s) d")
    ctx = ExitStack()
    with ctx:
        def sb(name, shape, dt=F32):
            return ctx.enter_context(nc.sbuf_tensor(name, shape, dt))

        def pb(name):
            return ctx.enter_context(nc.psum_tensor(name, [P, 512], F32))

        def sems(names):
            return [ctx.enter_context(nc.semaphore(n)) for n in names.split()]

        bias_rows = nc.dram_tensor("bias_rows", (HEADS, RLEN), F32, kind="Internal").ap()
        ffn_in = nc.dram_tensor("ffn_in", (OUTR, D), F32, kind="Internal").ap()
        table = nc.dram_tensor("table", (TROWS, 2), I32, kind="Internal").ap()

        KVG = 2 * KVW + 2 * MH
        NIN = w_in.shape[2]
        c_q, c_cv = KVG, KVG + AW
        c_vm = c_cv + CH
        c_om = c_vm + MW
        wbuf = sb("wbuf", [P, KC * NIN])
        wi = wbuf[:, :].rearrange("p (k n) -> p k n", k=KC)
        wo = sb("wo", [P, KC, D])
        ring = wbuf[:, 0:3 * FC * 2 * FF].rearrange("p (a n) -> p a n", a=3 * FC)
        wr = sb("wr", [P, KC, NG + NE])
        ident = sb("ident", [P, P])
        tri = sb("tri", [P, P])
        selh = sb("selh", [MH, MH, P])
        selp = sb("selp", [MH, PAIRS, P])
        gmix = sb("gmix", [P, D])
        gffn = sb("gffn", [P, D])
        gq = sb("gq", [P, HD])
        gk = sb("gk", [P, HD])
        sink = sb("sink", [P, HEADS])
        cw = sb("cw", [P, TAPS, CC])
        cb = sb("cb", [P, CC])
        gb = sb("gb", [64, 1])
        gml = sb("gml", [P, MW])
        bias = sb("bias", [P, HEADS, 2 * P])
        rbt = sb("rbt", [NBK, HEADS + P])
        rbias = sb("rbias", [P, NG + NE])
        mhalf = sb("mhalf", [P, 16])
        eps_d, eps_hd, eps_dv = (sb(f"eps_{n}", [P, 16]) for n in ("d", "hd", "dv"))
        tick = sb("tick", [1, 32])
        ones_s = sb("ones_s", [MH, P])
        xin = sb("xin", [P, 2, D])
        ssx = sb("ssx", [P, 1])
        rsx = sb("rsx", [P, 1])
        hn = sb("hn", [P, D])
        hnT = sb("hnT", [P, KC, P])
        kvg = sb("kvg", [P, KVG])
        q_sb = sb("q_sb", [P, AW])
        sqk = sb("sqk", [P, KVW + AW])
        ssqk = sb("ssqk", [P, KVH + HEADS])
        rqk = sb("rqk", [P, KVH + HEADS])
        qn = sb("qn", [P, G, KVH, HD])
        kn = sb("kn", [P, KVH, HD])
        gt = sb("gt", [P, 64])
        qT = sb("qT", [P, G, P])
        kTw = sb("kTw", [P, 2, P])
        vw = sb("vw", [P, 2, KVW])
        lg = sb("lg", [P, G, 2 * P])
        pr = lg
        PT = sb("PT", [P, G, 2, P])
        junk = PT[:, :, :, :].rearrange("p a b c -> p (a b c)")
        amx = sb("amx", [P, HEADS])
        anm = sb("anm", [P, HEADS])
        aes = sb("aes", [P, HEADS])
        asum = sb("asum", [P, HEADS])
        arc = sb("arc", [P, HEADS])
        pbias = sb("pbias", [P, 1])
        cin = sb("cin", [P, CC, TAPS - 1 + P])
        cy = sb("cy", [P, CC, P])
        ce = sb("ce", [P, CC, P])
        qk = sb("qk", [P, 2, CC, P])
        vm = sb("vm", [P, 2, MH, VE])
        eo = sb("eo", [P, MW])
        osg = eo
        giz = sb("giz", [MH, P])
        gfz = sb("gfz", [64, 3, P])
        glf = sb("glf", [MH, P])
        gbm = sb("gbm", [MH, 4, P])
        mprev = sb("mprev", [MH, 1])
        GT = sb("GT", [P, P])
        gT = sb("gT", [P, 68])
        darg = sb("darg", [P, MH, P])
        flip = darg[:, 0, :]
        dmat = sd = darg
        qg = sb("qg", [P, PAIRS, P])
        dec = sb("dec", [P, PAIRS])
        kw = sb("kw", [P, MH, DQK])
        Cst = sb("Cst", [P, PAIRS, VE])
        hden = sb("hden", [P, MH])
        hm = sb("hm", [P, MH, DV])
        hsq = darg
        hss = sb("hss", [P, MH])
        hrs = sb("hrs", [P, MH])
        mix = hn
        mixT = sb("mixT", [P, KC, P])
        ssh = sb("ssh", [P, 1])
        rsh = sb("rsh", [P, 1])
        h2 = sb("h2", [P, D])
        h2T = mixT
        brow = h2[0:HEADS, 0:RLEN]
        rl = sb("rl", [P, TILES, NG + NE])

        pay = sb("pay", [P, TILES, 2, 2], I32)
        desti = sb("desti", [P, TILES, 2], I32)
        stage = [sb(f"stage{n}", [P, 2], I32) for n in range(3)]
        row_a, row_b, row_c = stage[2], sb("row_b", [P, 2], I32), sb("row_c", [P, 2], I32)
        xg = hn
        yb = lg[:, :, :].rearrange("p a b -> p (a b)")
        CUM, ROWS, EXPERT = 0, NE, NE + MAXT + 2
        tabi = sb("tabi", [1, 2 * (MAXT + 2) + NE], I32)
        NI = MAXT + 2
        ints = sb("ints", [P, NI + TILES], I32)
        route_e = sb("route_e", [P, TILES * (NG + 1)])
        Mall = sqk[:, 0:TILES * NE]
        onesm = kvg[:, 0:P]
        strict = darg[:, 0, :]
        mh = q_sb

        T0, T1, J0, J1, S0, S1, O0, X0 = [pb(f"bank_{n}") for n in "t0 t1 j0 j1 s0 s1 o0 x0".split()]
        TB = [T0, T1]

        (ld_x0, ld_x1, ld_w0, ld_w1, ld_w2, ld_w3, ld_w4, ld_wo, ld_c, ld_rb, ld_bias, st_brow, st_h, st_h2,
         st_tab, st_zero) = sems("ld_x0 ld_x1 ld_wkvg ld_wq ld_wconv ld_wvm ld_wom ld_wo ld_consts ld_relbias "
                                 "ld_bias st_brow st_h st_ffn st_table st_zero")
        LDX = [ld_x0, ld_x1]
        (pool_const, pe_brow, dve_brow, pe_bias, dve_bias) = sems("pool_const pe_brow dve_brow pe_bias dve_bias")
        (pe_qkT, pe_hnT, pe_s0, pe_s1, pe_kvg, pe_g, pe_pT0, pe_pT1, pe_q, pe_pv0, pe_o, pe_kT, pe_cin, pe_st,
         pe_vm, pe_h, pe_u, pe_om, pe_mixT, pe_y0, pe_y1, pe_h2T, pe_r) = sems(
            "pe_qkT pe_hnT pe_s0 pe_s1 pe_kvg pe_g pe_pT0 pe_pT1 pe_q pe_pv0 pe_o pe_kT pe_cin pe_st "
            "pe_vm pe_h pe_u pe_om pe_mixT pe_y0 pe_y1 pe_h2T pe_r")
        (act_v, act_qT, act_ssx, act_ln, act_hnT, act_p0, act_g, act_kvg, act_pT0, act_D, act_p1, act_q,
         act_pT1, act_cin, act_vm, act_mixT, act_ey, act_om, act_ssh, act_h2T) = sems(
            "act_v act_qT act_ssx act_ln act_hnT act_p0 act_g act_kvg act_pT0 act_D act_p1 act_q "
            "act_pT1 act_cin act_vm act_mixT act_ey act_om act_ssh act_h2T")
        (dve_kg, dve_az, dve_hn, dve_nm0, dve_L0, dve_L1, dve_nm1, dve_ca, dve_hnT, dve_gT, dve_darg, dve_qg,
         dve_pT0, dve_pT1, dve_kw, dve_att, dve_sd, dve_qkn, dve_C, dve_hm, dve_mix, dve_osg, dve_mixT, dve_h,
         dve_h0, dve_hn2, dve_h2T, dve_rl, dve_qk, dve_cy, dve_sqk, dve_hss) = sems(
            "dve_kg dve_az dve_hn dve_nm0 dve_L0 dve_L1 dve_nm1 dve_ca dve_hnT dve_gT dve_darg dve_qg "
            "dve_pT0 dve_pT1 dve_kw dve_att dve_sd dve_qkn dve_C dve_hm dve_mix dve_osg dve_mixT dve_h "
            "dve_h0 dve_hn2 dve_h2T dve_rl dve_qk dve_cy dve_sqk dve_hss")
        (pool_rx, pool_rqk, pool_rhm, pool_rh) = sems("pool_rx pool_rqk pool_rhm pool_rh")
        (dve_chain, act_chain, pool_chain) = sems("dve_chain act_chain pool_chain")
        (dve_M, pe_pos, dve_pay, st_rows, dve_tab, dve_rt, act_rt) = sems(
            "dve_masks pe_positions dve_payload st_rows dve_tables dve_logits act_route")
        ld_g = sems(" ".join(f"ld_gate{j}" for j in range(FC)))
        ld_u = sems(" ".join(f"ld_up{j}" for j in range(FC)))
        ld_d = sems(" ".join(f"ld_down{j}" for j in range(FC)))
        (ld_i0, ld_i1, ld_i2, ld_row, st_y, pool_row, pe_mx, pe_gup, pe_hT, pe_dnp, act_silu, act_mx, act_y,
         dve_mh, dve_mx, dve_hT, dve_y) = sems(
            "ld_idx0 ld_idx1 ld_idx2 ld_rows st_y pool_row pe_mx pe_gateup pe_hT pe_down act_silu act_mx act_y "
            "dve_mh dve_mx dve_hT dve_y")

        block = ctx.enter_context(nc.Block())

        def wait(eng, sem, value):
            if not (isinstance(value, int) and value <= 0):
                eng.wait_ge(sem, value)

        class Chain:

            def __init__(self, eng, sem):
                self.eng, self.sem, self.base, self.n, self.start = eng, sem, 0, 0, 0
                self.wait = eng.wait_ge

            def begin_tiles(self):
                self.start = self.n

            def at(self, base):
                self.base, self.n = self.start + base, 0

            def __call__(self, ins):
                self.n += 1
                ins.then_inc(self.sem, 1)
                self.wait(self.sem, self.base + self.n)

        def tiles(eng, body, chain=None, per_tile=0, per_first=0):
            def one(t, u, main, nxt, base):
                if chain is not None:
                    chain.at(base)
                body(t, u, main, nxt)
                if chain is not None and nxt:
                    assert chain.n == (per_tile if main else per_first), (chain.n, main)
            if chain is not None:
                chain.begin_tiles()
            one(-1, 1, False, True, 0)
            with eng.Fori(0, (TILES - 2) // 2) as pair:
                for u in range(2):
                    one(2 * pair + u, u, True, True, per_first + (2 * pair + u) * per_tile)
            one(TILES - 2, 0, True, True, per_first + (TILES - 2) * per_tile)
            one(TILES - 1, 1, True, False, per_first + (TILES - 1) * per_tile)

        def load_expert(sp, e, last):
            wg = w_gate[0].rearrange("e (p k) n -> e p k n", p=P)
            wu = w_up[0].rearrange("e (p k) n -> e p k n", p=P)
            wd = w_down[0].rearrange("e (c p) n -> e p c n", p=P)
            ei = slice(e, e + 1) if isinstance(e, int) else bass.ds(e, 1)
            for j in range(FC):
                if last is not None:
                    sp.wait_ge(pe_gup, FC * last + (j + 1))
                for w, sem, at in ((wg, ld_g, j), (wu, ld_u, FC + j)):
                    sp.dma_start(ring[:, at, :].rearrange("p (k n) -> p k n", k=2),
                                 w[ei, :, 2 * j:2 * j + 2, :].rearrange("e p k n -> (e p) k n")).then_inc(sem[j], 16)
            for j in range(FC):
                if last is not None:
                    sp.wait_ge(pe_dnp, FC * last + (j + 1))
                sp.dma_start(ring[:, 2 * FC + j, :],
                             wd[ei, :, j, :].rearrange("e p n -> (e p) n")).then_inc(ld_d[j], 16)

        @block.sync
        def _(sp):
            sp.dma_start(xin[:, 0, :], x2[0:P, :]).then_inc(ld_x0, 16)
            sp.dma_start(gmix[:, :], norm_mix_g[0, :].partition_broadcast(P)).then_inc(ld_c, 16)
            w_v = w_in[0].rearrange("(k p) n -> p k n", p=P)
            a0 = AW + 2 * KVW
            sp.dma_start(wi[:, :, 0:2 * KVW], w_v[:, :, AW:a0]).then_inc(ld_w0, 16)
            sp.dma_start(wi[:, :, 2 * KVW:KVG], w_v[:, :, NIN - 2 * MH:NIN]).then_inc(ld_w0, 16)
            sp.dma_start(wi[:, :, c_q:c_cv], w_v[:, :, 0:AW]).then_inc(ld_w1, 16)
            for src, dst in ((q_norm_g[0, :].partition_broadcast(P), gq[:, :]),
                             (k_norm_g[0, :].partition_broadcast(P), gk[:, :]),
                             (attn_sink[0, :].partition_broadcast(P), sink[:, :]),
                             (mlstm_norm_g[0, :].partition_broadcast(P), gml[:, :]),
                             (norm_ffn_g[0, :].partition_broadcast(P), gffn[:, :]),
                             (b_router_group[0, :].partition_broadcast(P), rbias[:, 0:NG]),
                             (b_router_expert[0, :].partition_broadcast(P), rbias[:, NG:]),
                             *((conv_w[0, k].rearrange("(c p) -> p c", p=P), cw[:, k, :]) for k in range(TAPS)),
                             (conv_b[0].rearrange("(c p) -> p c", p=P), cb[:, :]),
                             (gate_b[0, 0:MH].rearrange("(h o) -> h o", o=1), gb[0:MH, :]),
                             (gate_b[0, MH:].rearrange("(h o) -> h o", o=1), gb[32:32 + MH, :])):
                with nc.allow_non_contiguous_dma("small constants"):
                    sp.dma_start(dst, src).then_inc(ld_c, 16)
            sp.dma_start(rbt[:, 0:HEADS], rel_bias).then_inc(ld_rb, 16)
            sp.dma_start(rbt[:, HEADS:], bucket_onehot).then_inc(ld_rb, 16)
            sp.dma_start(wi[:, :, c_cv:c_vm], w_v[:, :, a0:a0 + CH]).then_inc(ld_w2, 16)
            sp.dma_start(wi[:, :, c_vm:c_om], w_v[:, :, a0 + CH:a0 + CH + MW]).then_inc(ld_w3, 16)
            sp.dma_start(wi[:, :, c_om:NIN], w_v[:, :, a0 + CH + MW:a0 + CH + 2 * MW]).then_inc(ld_w4, 16)
            sp.wait_ge(dve_brow, 1)
            sp.dma_start(bias_rows, brow[:, :]).then_inc(st_brow, 16)
            sp.wait_ge(st_brow, 16)
            sp.dma_start(bias[:, :, :], bass.AP(tensor=bias_rows.tensor, offset=0,
                                                ap=[[1, P], [RLEN, HEADS], [1, 2 * P]])).then_inc(ld_bias, 16)
            sp.dma_start(xin[:, 1, :], x2[P:2 * P, :]).then_inc(ld_x1, 16)
            sp.dma_start(wo[:, :, :], w_out[0].rearrange("(k p) n -> p k n", p=P)).then_inc(ld_wo, 16)
            sp.dma_start(wr[:, :, 0:NG], w_router_group[0].rearrange("(p k) n -> p k n", p=P)).then_inc(ld_wo, 16)
            sp.dma_start(wr[:, :, NG:], w_router_expert[0].rearrange("(p k) n -> p k n", p=P)).then_inc(ld_wo, 16)
            sp.wait_ge(pool_const, 6)
            tv = table[0:NE * S, :].rearrange("(a p j) c -> a p j c", p=P, j=P)
            padv = lg[:, :, :].rearrange("p a b -> p (a b)")[:, 0:2 * P].bitcast(I32)
            for a in range(NE * S // (P * P)):
                sp.dma_start(tv[a].rearrange("p j c -> p (j c)"), padv).then_inc(st_tab, 16)
            sp.dma_start(table[NE * S:, :].rearrange("(p j) c -> p (j c)", p=2), padv[0:2, :]).then_inc(st_tab, 16)
            sp.dma_start(out[S:, :], junk).then_inc(st_zero, 16)
            sp.dma_start(ffn_in[S:, :], junk).then_inc(st_zero, 16)
            wait(sp, st_tab, 16 * (NE * S // (P * P) + 1))
            sp.wait_ge(st_zero, 32)

            def body(t, u, main, nxt):
                if not main:
                    return
                sp.wait_ge(dve_h, t + 1)
                sp.dma_start(out[bass.ds(t * P, P), :] if not isinstance(t, int) else out[t * P:t * P + P, :],
                             xin[:, u, :]).then_inc(st_h, 16)
                sp.wait_ge(dve_hn2, t + 1)
                sp.dma_start(ffn_in[bass.ds(t * P, P), :] if not isinstance(t, int)
                             else ffn_in[t * P:t * P + P, :], h2[:, :]).then_inc(st_h2, 16)
                if not (isinstance(t, int) and t + 2 >= TILES):
                    sp.wait_ge(st_h, 16 * t + 16)
                    sp.dma_start(xin[:, u, :], x2[bass.ds((t + 2) * P, P), :]).then_inc(LDX[u], 16)
            tiles(sp, body)
            sp.wait_ge(pe_om, TILES)
            load_expert(sp, 0, None)
            sp.wait_ge(dve_tab, 1)
            with sp.Fori(1, NE) as e:
                last = sp.value_load(tabi[0:1, bass.ds(e + (CUM - 1), 1)], min_val=0, max_val=MAXT - 1)
                load_expert(sp, e, last)

        @block.gpsimd
        def _(pool):
            chain = Chain(pool, pool_chain)
            chain(pool.memset(ident[:, :], 0.0))
            chain(pool.affine_select(out=ident[:, :], in_=ident[:, :], compare_op=ALU.not_equal, fill=1.0,
                                     base=0, pattern=[[-1, P]], channel_multiplier=1))
            chain(pool.memset(flip, 0.0))
            chain(pool.affine_select(out=flip, in_=flip, compare_op=ALU.not_equal, fill=1.0,
                                     base=1 - P, pattern=[[1, P]], channel_multiplier=1))
            chain(pool.memset(tri[:, :], 0.0))
            chain(pool.affine_select(out=tri[:, :], in_=tri[:, :], compare_op=ALU.is_ge, fill=NEG,
                                     base=0, pattern=[[1, P]], channel_multiplier=-1))
            pool.memset(mhalf[:, :], -0.5).then_inc(pool_const, 1)
            chain(pool.memset(selh[:, :, :], 0.0))
            chain(pool.affine_select(out=selh[:, :, :], in_=selh[:, :, :], compare_op=ALU.not_equal, fill=1.0,
                                     base=0, pattern=[[-1, MH], [0, P]], channel_multiplier=1))
            chain(pool.memset(selp[:, :, :], 0.0))
            sv = selp[:, :, :].rearrange("h c (a b) -> h c a b", a=2)
            chain(pool.affine_select(out=sv, in_=sv, compare_op=ALU.not_equal, fill=1.0, base=0,
                                     pattern=[[-2, PAIRS], [-1, 2], [0, P // 2]], channel_multiplier=1))
            pool.memset(ones_s[:, :], 1.0).then_inc(pool_const, 1)
            pool.memset(brow[:, :], NEG).then_inc(pool_const, 1)
            padi = lg[:, :, :].rearrange("p a b -> p (a b)")[:, 0:2 * P].bitcast(I32).rearrange(
                "p (j c) -> p j c", c=2)
            chain(pool.memset(padi, 0))
            pool.iota(padi[:, :, 0], pattern=[[1, P]], base=S, channel_multiplier=0).then_inc(pool_const, 1)
            pool.memset(junk, 0.0).then_inc(pool_const, 1)
            pool.iota(ints[:, 0:NI], pattern=[[1, NI]], base=0, channel_multiplier=0)
            pool.iota(ints[:, NI:], pattern=[[P, TILES]], base=0, channel_multiplier=1)
            for e, n in ((eps_d, D), (eps_hd, HD), (eps_dv, DV)):
                pool.memset(e[:, :], n * EPS)
            for z in (GT[:, :], gt[:, :], mprev[:, :], Cst[:, :, :], kTw[:, 1, :], vw[:, 1, :],
                      cin[:, :, 0:TAPS - 1]):
                chain(pool.memset(z, 0.0))
            chain(pool.memset(pbias[:, :], NEG))
            pool.memset(vm[:, :, :, DV:VE], 1.0).then_inc(pool_const, 1)

            def pwait(sem, value):
                pool.wait_ge(sem, value)
                if not isinstance(value, int):
                    ticks.append(len(ticks))
                    pool.tensor_tensor(tick[:, len(ticks):len(ticks) + 1], mhalf[0:1, 0:1], mhalf[0:1, 0:1], ALU.mult)
            ticks = []

            def rsqrt(root, ss, done, add):
                chain(pool.tensor_tensor(root, ss, add[:, 0:root.shape[1]], ALU.add))
                pool.tensor_tensor(root, root, mhalf[:, 0:root.shape[1]], ALU.pow).then_inc(done, 1)

            def body(t, u, main, nxt):
                if nxt:
                    pool.wait_ge(act_ssx, t + 2)
                    rsqrt(rsx[:, :], ssx[:, :], pool_rx, eps_d)
                    pool.wait_ge(dve_sqk, t + 2)
                    rsqrt(rqk[:, :], ssqk[:, :], pool_rqk, eps_hd)
                if main:
                    pool.wait_ge(dve_hss, t + 1)
                    rsqrt(hrs[:, :], hss[:, :], pool_rhm, eps_dv)
                    pool.wait_ge(act_ssh, t + 1)
                    rsqrt(rsh[:, :], ssh[:, :], pool_rh, eps_d)
            tiles(pool, body, chain, 4, 2)

            pool.wait_ge(dve_pay, 1)
            for t in range(TILES):
                for c in range(2):
                    pool.indirect_dma_start(
                        out=table, out_offset=bass.IndirectOffsetOnAxis(
                            ap=desti[:, t, c:c + 1].bitcast(U32), axis=0),
                        in_=pay[:, t, c, :], in_offset=None).then_inc(st_rows, 16)
            pool.wait_ge(st_rows, 16 * 2 * TILES)
            pool.wait_ge(dve_tab, 1)

            def load_rows(dst, t, sem):
                r = pool.value_load(tabi[0:1, bass.ds(t + ROWS, 1)], min_val=0, max_val=TROWS - P)
                pool.dma_start(dst[:, :], table[bass.ds(r, P), :]).then_inc(sem, 16)

            def gather(rows):
                pool.indirect_dma_start(
                    out=xg[:, :], out_offset=None, in_=ffn_in,
                    in_offset=bass.IndirectOffsetOnAxis(ap=rows[:, 0:1].bitcast(U32), axis=0)).then_inc(ld_row, 16)

            def scatter_add():
                pool.indirect_dma_start(
                    out=out, out_offset=bass.IndirectOffsetOnAxis(ap=row_c[:, 0:1].bitcast(U32), axis=0),
                    in_=yb[:, :], in_offset=None, compute_op=ALU.add).then_inc(st_y, 16)

            for n, sem in enumerate((ld_i0, ld_i1, ld_i2)):
                load_rows(stage[n], n, sem)
            pool.wait_ge(st_h2, 16 * TILES)
            pool.wait_ge(pe_h2T, TILES)
            pool.wait_ge(ld_i0, 16)
            pool.tensor_copy(row_c[:, :], stage[0][:, :]).then_inc(pool_row, 1)
            gather(stage[0])
            pool.wait_ge(ld_i1, 16)
            pool.tensor_copy(row_b[:, :], stage[1][:, :]).then_inc(pool_row, 1)
            pool.wait_ge(pe_mx, 1)
            pool.wait_ge(ld_row, 16)
            gather(stage[1])
            pool.wait_ge(st_h, 16 * TILES)
            end = pool.value_load(tabi[0:1, CUM + NE - 1:CUM + NE], min_val=NE - 1, max_val=MAXT - 1)
            with pool.Fori(1, end + 1) as t:
                pwait(ld_i2, 16 * t)
                pwait(pe_mx, t + 1)
                pwait(ld_row, 16 * (t + 1))
                gather(row_a)
                pwait(act_y, t)
                pwait(dve_y, t)
                scatter_add()
                pwait(st_y, 16 * t)
                pwait(ld_row, 16 * (t + 2))
                pwait(pool_row, 2 * t)
                pool.tensor_copy(row_c[:, :], row_b[:, :]).then_inc(pool_row, 1)
                pwait(pool_row, 2 * t + 1)
                pool.tensor_copy(row_b[:, :], row_a[:, :]).then_inc(pool_row, 1)
                pwait(pool_row, 2 * t + 2)
                load_rows(row_a, t + 2, ld_i2)
            pwait(act_y, end + 1)
            pwait(dve_y, end + 1)
            scatter_add()
            pwait(st_y, 16 * end + 16)
            pwait(ld_i2, 16 * end + 16)
            pwait(ld_row, 16 * end + 32)

        @block.scalar
        def _(act):
            chain = Chain(act, act_chain)

            def cp(dst, src):
                return act.activation(dst, src, ACT.Copy)

            def body(t, u, main, nxt):
                v = 1 - u
                if main:
                    act.wait_ge(act_kvg, t + 1)
                    wait(act, pe_o, t)
                    cp(vw[:, u, :], kvg[:, KVW:2 * KVW]).then_inc(act_v, 1)
                    act.wait_ge(pe_qkT, t + 1)
                    wait(act, pe_s1, t)
                    cp(qT[:, :, :].rearrange("p a b -> p (a b)"), T0[:, :]).then_inc(act_qT, 1)
                if nxt:
                    act.wait_ge(LDX[v], 8 * t + (16 + 8 * u))
                    wait(act, dve_hn, t + 1)
                    wait(act, pe_o, t)
                    wait(act, st_zero, 32)
                    act.activation(junk, xin[:, v, :], ACT.Square, accum_out=ssx[:, :]).then_inc(act_ssx, 1)
                if main:
                    act.wait_ge(dve_az, t + 1)
                    chain(act.activation(gfz[32:32 + MH, 1, :], gfz[32:32 + MH, 0, :], ACT.Exp, scale=-1.0))
                    act.activation(gfz[32:32 + MH, 1, :], gfz[32:32 + MH, 1, :], ACT.Ln, bias=1.0).then_inc(act_ln, 1)
                if nxt:
                    act.wait_ge(pe_hnT, t + 2)
                    wait(act, pe_om, t + 1)
                    cp(hnT[:, 0:4, :].rearrange("p a b -> p (a b)"), T0[:, :]).then_inc(act_hnT, 1)

                def exps(g, nm_done, p_used, done):
                    act.wait_ge(nm_done, t + 1)
                    for s, w in p_used:
                        wait(act, s, w)
                    for j in range(G):
                        h = g * G + j
                        act.activation(pr[:, j, :], lg[:, j, :], ACT.Exp, bias=anm[:, h:h + 1],
                                       accum_out=asum[:, h:h + 1])
                    act.activation(aes[:, g * G:g * G + G], aes[:, g * G:g * G + G], ACT.Exp).then_inc(done, 1)

                if main:
                    exps(0, dve_nm0, [], act_p0)
                    act.wait_ge(dve_ca, t + 1)
                    act.activation(gbm[:, 3, :], gbm[:, 2, :], ACT.Exp, bias=mprev[:, :])
                    act.activation(GT[32:32 + MH, :], GT[0:MH, :], ACT.Exp, bias=gbm[:, 2, P - 1:P])
                    act.activation(GT[64:64 + MH, :], gbm[:, 1, :], ACT.Exp, scale=-1.0).then_inc(act_g, 1)
                if nxt:
                    act.wait_ge(pe_kvg, t + 2)
                    wait(act, dve_qkn, t + 1)
                    if main:
                        act.wait_ge(act_v, t + 1)
                    cp(kvg[:, :], J0[:, 0:KVG])
                    act.activation(sqk[:, 0:KVW], J0[:, 0:KVW], ACT.Square).then_inc(act_kvg, 1)
                if main:
                    act.wait_ge(pe_pT0, t + 1)
                    wait(act, pe_o, t)
                    cp(PT[:, 0:2, :, :].rearrange("p a b c -> p (a b c)"), T0[:, :]).then_inc(act_pT0, 1)
                    act.wait_ge(dve_darg, t + 1)
                    act.wait_ge(dve_gT, t + 1)
                    wait(act, dve_sd, t)
                    for h in range(MH):
                        ins = act.activation(dmat[:, h, :], darg[:, h, :], ACT.Exp, bias=gT[:, h:h + 1])
                    ins.then_inc(act_D, 1)
                    exps(1, dve_nm1, [], act_p1)
                if nxt:
                    act.wait_ge(pe_q, t + 2)
                    wait(act, dve_qkn, t + 1)
                    cp(q_sb[:, :], J1[:, :])
                    act.activation(sqk[:, KVW:], J1[:, :], ACT.Square).then_inc(act_q, 1)
                if main:
                    act.wait_ge(pe_pT1, t + 1)
                    act.wait_ge(pe_pv0, t + 1)
                    cp(PT[:, 0:2, :, :].rearrange("p a b c -> p (a b c)"), T0[:, :]).then_inc(act_pT1, 1)
                if nxt:
                    act.wait_ge(pe_cin, t + 2)
                    wait(act, dve_cy, t + 1)
                    cp(cin[:, :, TAPS - 1:], J0[:, :].rearrange("p (a b) -> p a b", a=CC)).then_inc(act_cin, 1)
                    act.wait_ge(pe_vm, t + 2)
                    wait(act, pe_h, t)
                    cp(vm[:, v, :, 0:DV], J1[:, :].rearrange("p (a b) -> p a b", a=MH)).then_inc(act_vm, 1)
                    act.wait_ge(dve_cy, t + 2)
                    wait(act, dve_qk, t + 1)
                    act.activation(ce[:, :, :], cy[:, :, :], ACT.Exp, scale=-1.0).then_inc(act_ey, 1)
                if main:
                    act.wait_ge(pe_mixT, t + 1)
                    wait(act, pe_r, t)
                    cp(mixT[:, 0:4, :].rearrange("p a b -> p (a b)"), T0[:, :]).then_inc(act_mixT, 1)
                    act.wait_ge(dve_h, t + 1)
                    act.wait_ge(pe_o, t + 1)
                    act.activation(junk, xin[:, u, :], ACT.Square, accum_out=ssh[:, :]).then_inc(act_ssh, 1)
                if nxt:
                    act.wait_ge(pe_om, t + 2)
                    wait(act, dve_mix, t + 1)
                    act.activation(eo[:, :], J0[:, :], ACT.Exp, scale=-1.0).then_inc(act_om, 1)
                if main:
                    act.wait_ge(pe_h2T, t + 1)
                    act.wait_ge(pe_y1, t + 1)
                    cp(h2T[:, 0:4, :].rearrange("p a b -> p (a b)"), T0[:, :]).then_inc(act_h2T, 1)
            tiles(act, body, chain, 1, 0)

            sg = ce[:, :, :].rearrange("p a b -> p (a b)")
            mxT = h2T

            def silu(t):
                act.wait_ge(pe_gup, FC * (t + 1))
                wait(act, dve_mh, t)
                act.activation(sg, J0[:, :], ACT.Silu).then_inc(act_silu, 1)

            def rows_T(t):
                act.wait_ge(pe_mx, t + 1)
                if not (isinstance(t, int) and t == 0):
                    act.wait_ge(pe_gup, FC * t)
                cp(mxT[:, 0:4, :].rearrange("p a b -> p (a b)"), T0[:, :]).then_inc(act_mx, 1)

            def weigh(t):
                act.wait_ge(pe_dnp, FC * (t + 1))
                act.wait_ge(pool_row, 2 * t + 1)
                if isinstance(t, int):
                    wait(act, st_y, 16 * t)
                else:
                    act.wait_ge(st_y, 16 * t)
                act.activation(yb[:, 0:HALF], S1[:, :], ACT.Copy, scale=row_c[:, 1:2].bitcast(F32)).then_inc(act_y, 1)

            act.wait_ge(dve_rt, 1)
            act.activation(route_e[:, :], route_e[:, :], ACT.Exp).then_inc(act_rt, 1)
            act.wait_ge(dve_tab, 1)
            rows_T(0)
            silu(0)
            rows_T(1)
            act.wait_ge(st_h, 16 * TILES)
            end = act.value_load(tabi[0:1, CUM + NE - 1:CUM + NE], min_val=NE - 1, max_val=MAXT - 1)
            with act.Fori(1, end + 1) as t:
                silu(t)
                rows_T(t + 1)
                weigh(t - 1)
            weigh(end)

        @block.tensor
        def _(pe):
            def transposes(src, dst):
                for b in range(2):
                    for i in range(4):
                        ins = pe.transpose(TB[b][:, i * P:(i + 1) * P], src[:, (4 * b + i) * P:(4 * b + i + 1) * P],
                                           ident[:, :])
                ins.then_inc(dst, 1)

            def project(bank, c0, n, done, w_ready, w_count, t):
                wait(pe, w_ready, w_count)
                for k in range(KC):
                    ins = pe.matmul(bank[:, 0:n], hnT[:, k, :], wi[:, k, c0:c0 + n], start=(k == 0),
                                    stop=(k == KC - 1))
                ins.then_inc(done, 1)

            pe.wait_ge(ld_rb, 32)
            pe.matmul(X0[0:HEADS, 0:P], rbt[:, 0:HEADS], rbt[:, HEADS:], start=True, stop=True).then_inc(pe_brow, 1)
            pe.wait_ge(pool_const, 6)
            pe.wait_ge(dve_brow, 1)
            pe.wait_ge(ld_bias, 16)
            for b, bank in enumerate((S0, S1, O0, X0)):
                ins = pe.matmul(bank[:, :], flip, bias[:, 2 * b:2 * b + 2, :].rearrange("p h k -> p (h k)"),
                                start=True, stop=True)
            ins.then_inc(pe_bias, 1)

            def body(t, u, main, nxt):
                v = 1 - u
                if main:
                    pe.wait_ge(dve_qkn, t + 1)
                    wait(pe, act_h2T, t)
                    wait(pe, dve_h2T, t)
                    qf = qn[:, :, :, :].rearrange("p j g d -> p j (g d)")
                    for j in range(G):
                        pe.transpose(T0[:, j * P:(j + 1) * P], qf[:, j, :], ident[:, :])
                    pe.transpose(T1[:, 0:P], kn[:, :, :].rearrange("p g d -> p (g d)"), ident[:, :])
                    pe.transpose(T1[0:64, P:2 * P], gt[:, :], ident[:, :]).then_inc(pe_qkT, 1)
                if nxt:
                    pe.wait_ge(dve_hn, t + 2)
                    if main:
                        pe.wait_ge(act_qT, t + 1)
                        pe.wait_ge(dve_kg, t + 1)
                    transposes(hn, pe_hnT)

                def scores(g, done):
                    for j in range(G):
                        b = (S0, S1)[j // 2]
                        for w, slot in ((0, v), (1, u)):
                            c = (j % 2) * 2 * P + w * P
                            ins = pe.matmul(b[:, c:c + P], qT[64 * g:64 * g + 64, j, :],
                                            kTw[64 * g:64 * g + 64, slot, :], start=True, stop=True)
                    ins.then_inc(done, 1)

                def probs_T(done):
                    for j in range(G):
                        for w in range(2):
                            c = (j % 2) * 2 * P + w * P
                            ins = pe.transpose(TB[j // 2][:, c:c + P], pr[:, j, w * P:(w + 1) * P], ident[:, :])
                    ins.then_inc(done, 1)

                def values(g, done):
                    for j in range(G):
                        h = g * G + j
                        for w, slot in ((0, v), (1, u)):
                            ins = pe.matmul(O0[:, h * HD:(h + 1) * HD], PT[:, j, w, :],
                                            vw[:, slot, g * HD:(g + 1) * HD], start=(w == 0), stop=(w == 1))
                    ins.then_inc(done, 1)

                if main:
                    if not nxt:
                        pe.wait_ge(act_qT, t + 1)
                        pe.wait_ge(dve_kg, t + 1)
                    pe.wait_ge(dve_bias, 1)
                    wait(pe, dve_hm, t)
                    scores(0, pe_s0)
                if nxt:
                    pe.wait_ge(act_hnT, t + 2)
                    pe.wait_ge(dve_hnT, t + 2)
                    wait(pe, act_om, t + 1)
                    project(J0, 0, KVG, pe_kvg, ld_w0, 32, t)
                if main:
                    pe.wait_ge(act_g, t + 1)
                    wait(pe, dve_rl, t)
                    pe.transpose(X0[:, 0:P], GT[:, :], ident[:, :])
                    for h in range(MH):
                        pe.matmul(T0[:, h * P:(h + 1) * P], selh[:, h, :], gbm[:, 2, :], start=True, stop=True)
                    for c in range(PAIRS):
                        ins = pe.matmul(T1[:, c * P:(c + 1) * P], selp[:, c, :], gbm[:, 3, :], start=True, stop=True)
                    ins.then_inc(pe_g, 1)
                if nxt:
                    wait(pe, dve_h, t)
                    project(J1, c_q, AW, pe_q, ld_w1, 16, t)
                if main:
                    pe.wait_ge(act_p0, t + 1)
                    pe.wait_ge(dve_darg, t + 1)
                    pe.wait_ge(dve_qg, t + 1)
                    probs_T(pe_pT0)
                    pe.wait_ge(dve_L0, t + 1)
                    scores(1, pe_s1)
                if nxt:
                    wait(pe, ld_w2, 16)
                    pe.wait_ge(act_kvg, t + 2)
                    for c in range(CC):
                        for k in range(KC):
                            ins = pe.matmul(J0[:, c * P:(c + 1) * P], wi[:, k, c_cv + c * P:c_cv + (c + 1) * P],
                                            hnT[:, k, :], start=(k == 0), stop=(k == KC - 1))
                    ins.then_inc(pe_cin, 1)
                if main:
                    pe.wait_ge(act_v, t + 1)
                    pe.wait_ge(act_pT0, t + 1)
                    pe.wait_ge(dve_pT0, t + 1)
                    wait(pe, dve_att, t)
                    values(0, pe_pv0)
                    pe.wait_ge(act_p1, t + 1)
                    probs_T(pe_pT1)
                    pe.wait_ge(dve_qk, t + 1)
                    pe.wait_ge(dve_gT, t + 1)
                    for c in range(PAIRS):
                        ins = pe.transpose(X0[:, P + c * P:P + (c + 1) * P], qk[:, u, PAIRS + c, :], ident[:, :])
                    ins.then_inc(pe_kT, 1)
                    pe.wait_ge(dve_L1, t + 1)
                    for h in range(MH):
                        r, c = 64 * (h % 2), h // 2
                        ins = pe.matmul((S0, S1)[h % 2][:, c * P:(c + 1) * P], qk[r:r + 64, u, PAIRS + c, :],
                                        qk[r:r + 64, u, c, :], start=True, stop=True)
                    ins.then_inc(pe_st, 1)
                if nxt:
                    pe.wait_ge(act_q, t + 2)
                    project(J1, c_vm, MW, pe_vm, ld_w3, 16, t)
                if main:
                    pe.wait_ge(act_pT1, t + 1)
                    pe.wait_ge(dve_pT1, t + 1)
                    values(1, pe_o)
                    pe.wait_ge(dve_sd, t + 1)
                    pe.wait_ge(act_vm, t + 1)
                    wait(pe, dve_C, t)
                    for h in range(MH):
                        r, c = 64 * (h % 2), h // 2
                        o = (S0, S1)[h % 2][:, c * VE:(c + 1) * VE]
                        pe.matmul(o, sd[:, h, :], vm[:, u, h, :], start=True, stop=False)
                        ins = pe.matmul(o, qg[r:r + 64, c, :], Cst[r:r + 64, c, :], start=False, stop=True)
                    ins.then_inc(pe_h, 1)
                    pe.wait_ge(dve_kw, t + 1)
                    for h in range(MH):
                        r, c = 64 * (h % 2), h // 2
                        ins = pe.matmul(X0[r:r + 64, c * VE:(c + 1) * VE], kw[:, h, :], vm[:, u, h, :],
                                        start=True, stop=True)
                    ins.then_inc(pe_u, 1)
                    pe.wait_ge(dve_mix, t + 1)
                    transposes(mix, pe_mixT)
                    pe.wait_ge(act_mixT, t + 1)
                    pe.wait_ge(dve_mixT, t + 1)
                    wait(pe, ld_wo, 48)
                    pe.wait_ge(act_cin, t + 1 + (1 if nxt else 0))
                    for half, (b, done) in enumerate(((J0, pe_y0), (J1, pe_y1))):
                        if half:
                            pe.wait_ge(act_vm, t + 1 + (1 if nxt else 0))
                        for k in range(KC):
                            ins = pe.matmul(b[:, :], mixT[:, k, :], wo[:, k, half * HALF:(half + 1) * HALF],
                                            start=(k == 0), stop=(k == KC - 1))
                        ins.then_inc(done, 1)
                if nxt:
                    if main:
                        pe.wait_ge(dve_h0, t + 1)
                    else:
                        pe.wait_ge(act_cin, 1)
                    project(J0, c_om, MW, pe_om, ld_w4, 16, t)
                if main:
                    pe.wait_ge(dve_hn2, t + 1)
                    transposes(h2, pe_h2T)
                    pe.wait_ge(act_h2T, t + 1)
                    pe.wait_ge(dve_h2T, t + 1)
                    pe.wait_ge(dve_C, t + 1)
                    for k in range(KC):
                        ins = pe.matmul(X0[:, 0:NG + NE], h2T[:, k, :], wr[:, k, :], start=(k == 0),
                                        stop=(k == KC - 1))
                    ins.then_inc(pe_r, 1)
            tiles(pe, body)

            MC = TILES * NE
            pe.wait_ge(dve_M, 1)
            pe.matmul(S0[:, 0:MC], strict, Mall, start=True, stop=True)
            pe.matmul(S1[:, 0:MC], onesm, Mall, start=True, stop=True).then_inc(pe_pos, 1)

            mxT = h2T
            mhT = qT
            pe.wait_ge(dve_tab, 1)

            def rows_T(t):
                pe.wait_ge(ld_row, 16 * (t + 1))
                wait(pe, act_mx, t)
                wait(pe, dve_mx, t)
                transposes(xg, pe_mx)

            def gate_up(t, count, mid):
                pe.wait_ge(act_mx, t + 1)
                pe.wait_ge(dve_mx, t + 1)
                wait(pe, dve_mh, t)
                for j in range(FC):
                    pe.wait_ge(ld_g[j], count)
                    pe.wait_ge(ld_u[j], count)
                    for kk in range(2):
                        k = 2 * j + kk
                        for b, at in ((J0, j), (J1, FC + j)):
                            ins = pe.matmul(b[:, :], mxT[:, k, :], ring[:, at, kk * FF:(kk + 1) * FF],
                                            start=(k == 0), stop=(k == KC - 1))
                    ins.then_inc(pe_gup, 1)
                    if j == 0:
                        mid()

            def hidden_T(t):
                pe.wait_ge(dve_mh, t + 1)
                for c in range(FC):
                    ins = pe.transpose(S0[:, c * P:(c + 1) * P], mh[:, c * P:(c + 1) * P], ident[:, :])
                ins.then_inc(pe_hT, 1)

            def down(t, count):
                pe.wait_ge(dve_hT, t + 1)
                wait(pe, act_y, t)
                wait(pe, dve_y, t)
                for c in range(FC):
                    pe.wait_ge(ld_d[c], count)
                    for half, b in enumerate((S1, O0)):
                        ins = pe.matmul(b[:, :], mhT[:, c, :],
                                        ring[:, 2 * FC + c, half * HALF:(half + 1) * HALF],
                                        start=(c == 0), stop=(c == FC - 1))
                    ins.then_inc(pe_dnp, 1)

            def count_of(t):
                return pe.value_load(tabi[0:1, bass.ds(t + EXPERT, 1)], min_val=0, max_val=NE) * 16 + 16

            rows_T(0)
            gate_up(0, 16, lambda: None)
            rows_T(1)
            end = pe.value_load(tabi[0:1, CUM + NE - 1:CUM + NE], min_val=NE - 1, max_val=MAXT - 1)
            with pe.Fori(1, end + 1) as t:
                gate_up(t, count_of(t), lambda: hidden_T(t - 1))
                rows_T(t + 1)
                down(t - 1, count_of(t - 1))
            hidden_T(end)
            down(end, 16 * NE)

        @block.vector
        def _(dve):
            chain = Chain(dve, dve_chain)
            dve.wait_ge(pool_const, 6)
            dve.wait_ge(pe_brow, 1)
            dve.tensor_copy(brow[:, P:2 * P], X0[0:HEADS, 0:P]).then_inc(dve_brow, 1)
            dve.wait_ge(ld_c, 16 * (11 + TAPS))
            chain(dve.tensor_scalar(gmix[:, :], gmix[:, :], float(D) ** 0.5, None, ALU.mult))
            chain(dve.tensor_scalar(gffn[:, :], gffn[:, :], float(D) ** 0.5, None, ALU.mult))
            chain(dve.tensor_scalar(gml[:, :], gml[:, :], float(DV) ** 0.5, None, ALU.mult))
            chain(dve.tensor_scalar(gk[:, :], gk[:, :], float(HD) ** 0.5, None, ALU.mult))
            dve.wait_ge(pe_bias, 1)
            for b, bank in enumerate((S0, S1, O0, X0)):
                ins = dve.tensor_copy(bias[:, 2 * b:2 * b + 2, :].rearrange("p h k -> p (h k)"), bank[:, :])
            ins.then_inc(dve_bias, 1)

            LINKS, LINKS_FIRST = 26, 7

            def body(t, u, main, nxt):
                v = 1 - u
                if main:
                    dve.wait_ge(pe_qkT, t + 1)
                    wait(dve, pe_s1, t - 1 if isinstance(t, int) else t)
                    dve.tensor_copy(kTw[:, u, :], T1[:, 0:P])
                    dve.tensor_scalar(giz[:, :], T1[0:MH, P:2 * P], gb[0:MH, :], None, ALU.add)
                    ins = dve.tensor_scalar(gfz[32:32 + MH, 2, :], T1[32:32 + MH, P:2 * P], gb[32:32 + MH, :], None,
                                            ALU.add)
                    ins.then_inc(dve_kg, 1)
                    dve.wait_ge(dve_kg, t + 1)
                    dve.scalar_tensor_tensor(gfz[32:32 + MH, 0, :], gfz[32:32 + MH, 2, :], -1.0,
                                             gfz[32:32 + MH, 2, :], ALU.mult, ALU.max).then_inc(dve_az, 1)
                if nxt:
                    dve.wait_ge(pool_rx, t + 2)
                    wait(dve, pe_hnT, t + 1)
                    wait(dve, pe_mixT, t)
                    dve.scalar_tensor_tensor(hn[:, :], xin[:, v, :], rsx[:, :], gmix[:, :], ALU.mult,
                                             ALU.mult).then_inc(dve_hn, 1)

                def logits(g, s_done, l_done, nm_done):
                    hs = slice(g * G, g * G + G)
                    dve.wait_ge(s_done, t + 1)
                    for b, S_ in enumerate((S0, S1)):
                        sv = S_[:, :].rearrange("p (j w k) -> p j w k", j=2, w=2)
                        lv = lg[:, 2 * b:2 * b + 2, :].rearrange("p j (w k) -> p j w k", w=2)
                        bv = bias[:, g * G + 2 * b:g * G + 2 * b + 2, :].rearrange("p j (w k) -> p j w k", w=2)
                        dve.scalar_tensor_tensor(lv[:, :, 0, :], sv[:, :, 0, :], pbias[:, :], bv[:, :, 0, :],
                                                 ALU.add, ALU.add)
                        ins = dve.tensor_tensor(lv[:, :, 1, :], sv[:, :, 1, :], bv[:, :, 1, :], ALU.add)
                    ins.then_inc(l_done, 1)
                    dve.wait_ge(l_done, t + 1)
                    chain(dve.tensor_reduce(amx[:, hs], lg[:, :, :], AX, ALU.max))
                    chain(dve.tensor_tensor(amx[:, hs], amx[:, hs], sink[:, hs], ALU.max))
                    chain(dve.tensor_scalar(anm[:, hs], amx[:, hs], -1.0, None, ALU.mult))
                    dve.tensor_tensor(aes[:, hs], sink[:, hs], anm[:, hs], ALU.add).then_inc(nm_done, 1)

                if main:
                    wait(dve, pe_pT1, t)
                    logits(0, pe_s0, dve_L0, dve_nm0)
                    dve.wait_ge(act_ln, t + 1)
                    chain(dve.tensor_scalar(gfz[32:32 + MH, 2, :], gfz[32:32 + MH, 2, :], 0.0, None, ALU.min))
                    chain(dve.tensor_tensor(glf[:, :], gfz[32:32 + MH, 2, :], gfz[32:32 + MH, 1, :], ALU.subtract))
                    chain(dve.tensor_tensor_scan(gbm[:, 0, :], ones_s[:, :], glf[:, :], 0.0, ALU.mult, ALU.add))
                    chain(dve.tensor_tensor_scan(gbm[:, 1, :], glf[:, :], giz[:, :], mprev[:, :], ALU.add, ALU.max))
                    wait(dve, pe_g, t)
                    dve.tensor_tensor(gbm[:, 2, :], gbm[:, 0, :], gbm[:, 1, :], ALU.subtract)
                    dve.tensor_tensor(GT[0:MH, :], giz[:, :], gbm[:, 0, :], ALU.subtract).then_inc(dve_ca, 1)
                if nxt:
                    dve.wait_ge(pe_hnT, t + 2)
                    wait(dve, pe_om, t + 1)
                    dve.tensor_copy(hnT[:, 4:8, :].rearrange("p a b -> p (a b)"), T1[:, :]).then_inc(dve_hnT, 1)
                if main:
                    dve.wait_ge(pe_g, t + 1)
                    dve.tensor_copy(gT[:, :], X0[:, 0:68]).then_inc(dve_gT, 1)
                    wait(dve, pe_h, t)
                    dve.tensor_tensor(darg[:, :, :], T0[:, :].rearrange("p (h s) -> p h s", h=MH),
                                      tri[:, :].unsqueeze(1).to_broadcast([P, MH, P]), ALU.add).then_inc(dve_darg, 1)
                    dve.wait_ge(dve_qk, t + 1)
                    dve.tensor_copy(dec[:, :], T1[:, P - 1:PAIRS * P:P])
                    dve.tensor_tensor(qg[:, :, :], qk[:, u, 0:PAIRS, :],
                                      T1[:, 0:PAIRS * P].rearrange("p (c s) -> p c s", c=PAIRS),
                                      ALU.mult).then_inc(dve_qg, 1)
                    dve.wait_ge(act_g, t + 1)
                    dve.tensor_copy(mprev[:, :], gbm[:, 1, P - 1:P])
                    dve.wait_ge(pe_pT0, t + 1)
                    wait(dve, pe_o, t)
                    dve.tensor_copy(PT[:, 2:4, :, :].rearrange("p a b c -> p (a b c)"), T1[:, :]).then_inc(dve_pT0, 1)
                    dve.wait_ge(pe_pT0, t + 1)
                    logits(1, pe_s1, dve_L1, dve_nm1)
                    dve.memset(pbias[:, :], 0.0)
                    dve.wait_ge(pe_kT, t + 1)
                    dve.scalar_tensor_tensor(
                        kw[:, :, :], X0[:, P:P + MH * DQK].rearrange("p (h d) -> p h d", h=MH), float(DQK) ** -0.5,
                        gT[:, 32:32 + MH].unsqueeze(2).to_broadcast([P, MH, DQK]), ALU.mult,
                        ALU.mult).then_inc(dve_kw, 1)
                    dve.wait_ge(pe_pT1, t + 1)
                    dve.wait_ge(pe_pv0, t + 1)
                    dve.tensor_copy(PT[:, 2:4, :, :].rearrange("p a b c -> p (a b c)"), T1[:, :]).then_inc(dve_pT1, 1)
                    dve.wait_ge(pe_st, t + 1)
                    dve.wait_ge(act_D, t + 1)
                    for b, S_ in enumerate((S0, S1)):
                        ins = dve.scalar_tensor_tensor(
                            sd[:, b::2, :], S_[:, 0:PAIRS * P].rearrange("p (c s) -> p c s", c=PAIRS),
                            float(DQK) ** -0.5, dmat[:, b::2, :], ALU.mult, ALU.mult)
                    ins.then_inc(dve_sd, 1)
                if nxt:
                    dve.wait_ge(act_kvg, t + 2)
                    dve.wait_ge(act_q, t + 2)
                    dve.tensor_reduce(ssqk[:, :], sqk[:, :].rearrange("p (h d) -> p h d", d=HD), AX,
                                      ALU.add).then_inc(dve_sqk, 1)
                    wait(dve, pe_qkT, t + 1)
                    dve.tensor_copy(gt[:, 0:MH], kvg[:, 2 * KVW:2 * KVW + MH])
                    dve.tensor_copy(gt[:, 32:32 + MH], kvg[:, 2 * KVW + MH:KVG])
                    dve.wait_ge(pool_rqk, t + 2)
                    qv = qn[:, :, :, :].rearrange("p j g d -> p g j d")
                    for g in range(KVH):
                        dve.tensor_tensor(qv[:, g, :, :],
                                          q_sb[:, g * G * HD:(g + 1) * G * HD].rearrange("p (j d) -> p j d", j=G),
                                          rqk[:, KVH + g * G:KVH + (g + 1) * G].unsqueeze(2).to_broadcast([P, G, HD]),
                                          ALU.mult)
                    chain(dve.tensor_tensor(kn[:, :, :], kvg[:, 0:KVW].rearrange("p (g d) -> p g d", g=KVH),
                                            rqk[:, 0:KVH].unsqueeze(2).to_broadcast([P, KVH, HD]), ALU.mult))
                    q8 = qn[:, :, :, :].rearrange("p j g d -> p (j g) d")
                    dve.tensor_tensor(q8, q8, gq[:, :].unsqueeze(1).to_broadcast([P, HEADS, HD]), ALU.mult)
                    dve.tensor_tensor(kn[:, :, :], kn[:, :, :], gk[:, :].unsqueeze(1).to_broadcast([P, KVH, HD]),
                                      ALU.mult).then_inc(dve_qkn, 1)
                    dve.wait_ge(act_cin, t + 2)
                    wait(dve, act_ey, t + 1)
                    wait(dve, dve_qk, t + 1)
                    for c in range(CC):
                        ins = dve.tensor_scalar(cy[:, c, :], cin[:, c, 0:P], cw[:, 0, c:c + 1], None, ALU.mult)
                    chain(ins)
                    for k in range(1, TAPS):
                        for c in range(CC):
                            ins = dve.scalar_tensor_tensor(cy[:, c, :], cin[:, c, k:k + P], cw[:, k, c:c + 1],
                                                           cy[:, c, :], ALU.mult, ALU.add)
                        chain(ins)
                    for c in range(CC):
                        dve.tensor_scalar(cy[:, c, :], cy[:, c, :], cb[:, c:c + 1], None, ALU.add)
                    dve.tensor_copy(cin[:, :, 0:TAPS - 1], cin[:, :, P:P + TAPS - 1]).then_inc(dve_cy, 1)
                if main:
                    dve.wait_ge(pe_o, t + 1)
                    dve.wait_ge(act_p1, t + 1)
                    chain(dve.tensor_tensor(arc[:, :], asum[:, :], aes[:, :], ALU.add))
                    chain(dve.reciprocal(arc[:, :], arc[:, :]))
                    dve.tensor_tensor(mix[:, 0:AW].rearrange("p (h d) -> p h d", h=HEADS),
                                      O0[:, :].rearrange("p (h d) -> p h d", h=HEADS),
                                      arc[:, :].unsqueeze(2).to_broadcast([P, HEADS, HD]), ALU.mult)\
                        .then_inc(dve_att, 1)
                    dve.wait_ge(pe_h, t + 1)
                    for b, S_ in enumerate((S0, S1)):
                        hv = S_[:, 0:PAIRS * VE].rearrange("p (c e) -> p c e", c=PAIRS)
                        ins = dve.tensor_tensor(hden[:, b::2], hv[:, :, DV], gT[:, 64 + b:64 + MH:2], ALU.max)
                    chain(ins)
                    for b, S_ in enumerate((S0, S1)):
                        hv = S_[:, 0:PAIRS * VE].rearrange("p (c e) -> p c e", c=PAIRS)
                        ins = dve.scalar_tensor_tensor(hden[:, b::2], hv[:, :, DV], -1.0, hden[:, b::2], ALU.mult,
                                                       ALU.max)
                    chain(ins)
                    chain(dve.reciprocal(hden[:, :], hden[:, :]))
                    for b, S_ in enumerate((S0, S1)):
                        hv = S_[:, 0:PAIRS * VE].rearrange("p (c e) -> p c e", c=PAIRS)
                        ins = dve.tensor_tensor(hm[:, b::2, :], hv[:, :, 0:DV],
                                                hden[:, b::2].unsqueeze(2).to_broadcast([P, PAIRS, DV]), ALU.mult)
                    ins.then_inc(dve_hm, 1)
                    dve.wait_ge(dve_hm, t + 1)
                    chain(dve.tensor_tensor(hsq[:, :, :], hm[:, :, :], hm[:, :, :], ALU.mult))
                    dve.tensor_reduce(hss[:, :], hsq[:, :, :], AX, ALU.add).then_inc(dve_hss, 1)
                    dve.wait_ge(act_om, t + 1)
                    chain(dve.tensor_scalar(osg[:, :], eo[:, :], 1.0, None, ALU.add))
                    chain(dve.reciprocal(osg[:, :], osg[:, :]))
                    dve.tensor_tensor(osg[:, :], osg[:, :], gml[:, :], ALU.mult).then_inc(dve_osg, 1)
                    dve.wait_ge(pe_u, t + 1)
                    for c in range(PAIRS):
                        ins = dve.scalar_tensor_tensor(Cst[:, c, :], Cst[:, c, :], dec[:, c:c + 1],
                                                       X0[:, c * VE:(c + 1) * VE], ALU.mult, ALU.add)
                    ins.then_inc(dve_C, 1)
                    dve.wait_ge(pool_rhm, t + 1)
                    dve.wait_ge(dve_osg, t + 1)
                    chain(dve.tensor_tensor(hm[:, :, :], hm[:, :, :], hrs[:, :].unsqueeze(2).to_broadcast([P, MH, DV]),
                                            ALU.mult))
                    dve.tensor_tensor(mix[:, AW:], hm[:, :, :].rearrange("p h d -> p (h d)"), osg[:, :],
                                      ALU.mult).then_inc(dve_mix, 1)
                    dve.wait_ge(pe_mixT, t + 1)
                    wait(dve, pe_r, t)
                    dve.tensor_copy(mixT[:, 4:8, :].rearrange("p a b -> p (a b)"), T1[:, :]).then_inc(dve_mixT, 1)
                if nxt:
                    dve.wait_ge(act_ey, t + 2)
                    chain(dve.tensor_scalar(ce[:, :, :], ce[:, :, :], 1.0, None, ALU.add))
                    chain(dve.reciprocal(ce[:, :, :], ce[:, :, :]))
                    dve.tensor_tensor(qk[:, v, :, :], cy[:, :, :], ce[:, :, :], ALU.mult).then_inc(dve_qk, 1)
                if main:
                    dve.wait_ge(pe_y0, t + 1)
                    dve.tensor_tensor(xin[:, u, 0:HALF], J0[:, :], xin[:, u, 0:HALF], ALU.add).then_inc(dve_h0, 1)
                    dve.wait_ge(pe_y1, t + 1)
                    dve.tensor_tensor(xin[:, u, HALF:], J1[:, :], xin[:, u, HALF:], ALU.add).then_inc(dve_h, 1)
                    dve.wait_ge(pool_rh, t + 1)
                    dve.wait_ge(dve_h, t + 1)
                    wait(dve, pe_h2T, t)
                    wait(dve, st_h2, 16 * t)
                    hv = h2[:, :].rearrange("q (k p) -> q p k", k=KC)
                    dve.scalar_tensor_tensor(hv, xin[:, u, :].rearrange("q (p k) -> q p k", k=KC), rsh[:, :],
                                             gffn[:, :].rearrange("q (p k) -> q p k", k=KC), ALU.mult,
                                             ALU.mult).then_inc(dve_hn2, 1)
                    dve.wait_ge(pe_h2T, t + 1)
                    dve.wait_ge(pe_y1, t + 1)
                    dve.tensor_copy(h2T[:, 4:8, :].rearrange("p a b -> p (a b)"), T1[:, :]).then_inc(dve_h2T, 1)
                    dve.wait_ge(pe_r, t + 1)
                    ti = slice(t, t + 1) if isinstance(t, int) else bass.ds(t, 1)
                    dve.tensor_tensor(rl[:, ti, :].rearrange("p t n -> p (t n)"), X0[:, 0:NG + NE], rbias[:, :],
                                      ALU.add).then_inc(dve_rl, 1)
            tiles(dve, body, chain, LINKS, LINKS_FIRST)

            T_ = TILES

            class Space:
                def __init__(self, bufs):
                    self.bufs, self.i, self.at = bufs, 0, 0

                def __call__(self, n):
                    if self.at + n > self.bufs[self.i].shape[1]:
                        self.i, self.at = self.i + 1, 0
                    self.at += n
                    return self.bufs[self.i][:, self.at - n:self.at]

            new = Space([lg[:, :, :].rearrange("p a b -> p (a b)"), junk, bias[:, 0:4, :].rearrange(
                "p a b -> p (a b)"), bias[:, 4:8, :].rearrange("p a b -> p (a b)")])
            dve.wait_ge(dve_rl, TILES)
            dve.wait_ge(act_p1, TILES)
            dve.wait_ge(pe_pT1, TILES)
            dve.wait_ge(pe_mixT, TILES)
            dve.wait_ge(act_ssh, TILES)

            def tt(out_, a, b, op):
                chain(dve.tensor_tensor(out_, a, b, op))

            def first_max(vals, n):
                mx, idx = new(T_), new(T_)
                chain(dve.tensor_reduce(mx, vals, AX, ALU.max))
                oh = new(T_ * n).rearrange("p (t n) -> p t n", n=n)
                bc = lambda a: a.unsqueeze(2).to_broadcast([P, T_, n])
                tt(oh, vals, bc(mx), ALU.is_equal)
                io = iota_f[:, 0:n].unsqueeze(1).to_broadcast([P, T_, n])
                chain(dve.tensor_scalar(oh, oh, -1.0e4, None, ALU.mult))
                tt(oh, oh, io, ALU.add)
                chain(dve.tensor_reduce(idx, oh, AX, ALU.min))
                chain(dve.tensor_scalar(idx, idx, 1.0e4, None, ALU.add))
                tt(oh, io, bc(idx), ALU.is_equal)
                return oh, mx

            iota_f = new(NI)
            chain(dve.tensor_copy(iota_f, ints[:, 0:NI]))
            gl = rl[:, :, 0:NG]
            ohg, gmx = first_max(gl, NG)
            eg = new(T_ * NG).rearrange("p (t n) -> p t n", n=NG)
            tt(eg, gl, gmx.unsqueeze(2).to_broadcast([P, T_, NG]), ALU.subtract)
            el = rl[:, :, NG:].rearrange("p t (g e) -> p t g e", g=NG)
            prod = new(T_ * NE).rearrange("p (t g e) -> p t g e", g=NG, e=EPG)
            tt(prod, el, ohg.unsqueeze(3).to_broadcast([P, T_, NG, EPG]), ALU.mult)
            ein = new(T_ * EPG).rearrange("p (t e) -> p t e", e=EPG)
            chain(dve.tensor_reduce(ein, prod.rearrange("p t g e -> p t e g"), AX, ALU.add))
            oh1, m1 = first_max(ein, EPG)
            e2 = new(T_ * EPG).rearrange("p (t e) -> p t e", e=EPG)
            chain(dve.scalar_tensor_tensor(e2, oh1, -3.0e38, ein, ALU.mult, ALU.add))
            oh2, m2 = first_max(e2, EPG)
            dm = new(T_)
            tt(dm, m2, m1, ALU.subtract)
            eb = route_e
            dve.tensor_copy(eb[:, 0:T_ * NG], eg.rearrange("p t n -> p (t n)"))
            dve.tensor_copy(eb[:, T_ * NG:], dm).then_inc(dve_rt, 1)
            full = []
            for oh in (oh1, oh2):
                f = new(T_ * NE)
                tt(f.rearrange("p (t g e) -> p t g e", g=NG, e=EPG),
                   ohg.unsqueeze(3).to_broadcast([P, T_, NG, EPG]),
                   oh.unsqueeze(2).to_broadcast([P, T_, NG, EPG]), ALU.mult)
                full.append(f)
            dve.wait_ge(act_v, TILES)
            dve.wait_ge(act_D, TILES)
            dve.memset(onesm, 1.0)
            dve.tensor_scalar(strict, tri[:, :], -0.5, None, ALU.is_gt)
            chain(dve.tensor_tensor(Mall, full[0], full[1], ALU.add))
            dve.tensor_tensor(strict, strict, ident[:, :], ALU.subtract).then_inc(dve_M, 1)
            dve.wait_ge(act_rt, 1)
            gs, wt = new(T_), new(2 * T_).rearrange("p (t c) -> p t c", c=2)
            chain(dve.tensor_reduce(gs, eb[:, 0:T_ * NG].rearrange("p (t n) -> p t n", n=NG), AX, ALU.add))
            e21, dn = eb[:, T_ * NG:], new(T_)
            chain(dve.tensor_scalar(dn, e21, 1.0, None, ALU.add))
            tt(dn, dn, gs, ALU.mult)
            chain(dve.reciprocal(dn, dn))
            chain(dve.tensor_copy(wt[:, :, 0], dn))
            tt(wt[:, :, 1], dn, e21, ALU.mult)
            chain(dve.tensor_copy(pay[:, :, :, 1].bitcast(F32), wt))
            for c in range(2):
                chain(dve.tensor_copy(pay[:, :, c, 0], ints[:, NI:]))
            dve.wait_ge(pe_pos, 1)
            MC = T_ * NE
            tot = new(MC)
            pos = new(MC)
            chain(dve.tensor_copy(tot, S1[:, 0:MC]))
            off = new(MC + NE)
            chain(dve.memset(off[:, 0:NE], 0.0))
            for t in range(T_):
                tt(off[:, (t + 1) * NE:(t + 2) * NE], off[:, t * NE:(t + 1) * NE], tot[:, t * NE:(t + 1) * NE], ALU.add)
            tt(pos, S0[:, 0:MC], off[:, 0:MC], ALU.add)
            eb_ = new(NE)
            chain(dve.tensor_scalar(eb_, iota_f[:, 0:NE], float(S), None, ALU.mult))
            tt(pos.rearrange("p (t e) -> p t e", e=NE), pos.rearrange("p (t e) -> p t e", e=NE),
               eb_.unsqueeze(1).to_broadcast([P, T_, NE]), ALU.add)
            dst = new(2 * T_).rearrange("p (t c) -> p t c", c=2)
            for c in range(2):
                tt(full[c], full[c], pos, ALU.mult)
                chain(dve.tensor_reduce(dst[:, :, c], full[c].rearrange("p (t e) -> p t e", e=NE), AX, ALU.add))
            dve.tensor_copy(desti[:, :, :], dst).then_inc(dve_pay, 1)
            one = slice(0, 1)
            cnt = off[one, T_ * NE:(T_ + 1) * NE]
            cmp = new(NE * (T_ - 1))[one, :].rearrange("p (e k) -> p e k", e=NE)
            thr = new(T_ - 1)[one, :]
            chain(dve.tensor_scalar(thr, iota_f[one, 1:T_], float(P), None, ALU.mult))
            tt(cmp, cnt.unsqueeze(2).to_broadcast([1, NE, T_ - 1]), thr.unsqueeze(1).to_broadcast([1, NE, T_ - 1]),
               ALU.is_gt)
            te, cum = new(NE)[one, :], new(NE)[one, :]
            chain(dve.tensor_reduce(te, cmp, AX, ALU.add))
            chain(dve.tensor_scalar(te, te, 1.0, None, ALU.add))
            on = new(NE)[one, :]
            chain(dve.memset(on, 1.0))
            chain(dve.tensor_tensor_scan(cum, on, te, 0.0, ALU.mult, ALU.add))
            NTL = MAXT + 2
            big = new(NTL * NE)[one, :].rearrange("p (t e) -> p t e", e=NE)
            et, fs = new(NTL)[one, :], new(NTL)[one, :]
            tt(big, cum.unsqueeze(1).to_broadcast([1, NTL, NE]),
               iota_f[one, 0:NTL].unsqueeze(2).to_broadcast([1, NTL, NE]), ALU.is_le)
            chain(dve.tensor_reduce(et, big, AX, ALU.add))
            tt(big, big, te.unsqueeze(1).to_broadcast([1, NTL, NE]), ALU.mult)
            chain(dve.tensor_reduce(fs, big, AX, ALU.add))
            chain(dve.tensor_copy(tabi[:, EXPERT:EXPERT + NTL], et))
            chain(dve.tensor_scalar(et, et, float(S // P), None, ALU.mult))
            tt(et, et, iota_f[one, 0:NTL], ALU.add)
            tt(et, et, fs, ALU.subtract)
            chain(dve.tensor_scalar(et, et, float(P), None, ALU.mult))
            chain(dve.tensor_scalar(et, et, float(TROWS - P), None, ALU.min))
            chain(dve.tensor_copy(tabi[:, ROWS:ROWS + NTL], et))
            dve.tensor_scalar(tabi[:, CUM:CUM + NE], cum, -1.0, None, ALU.add).then_inc(dve_tab, 1)

            mxT = h2T
            mhT = qT
            sg = ce[:, :, :].rearrange("p a b -> p (a b)")

            def hidden_T(t):
                dve.wait_ge(pe_hT, t + 1)
                if not isinstance(t, int):
                    dve.wait_ge(pe_dnp, FC * t)
                dve.tensor_copy(mhT[:, :, :].rearrange("p a b -> p (a b)"), S0[:, :]).then_inc(dve_hT, 1)

            def hidden(t):
                dve.wait_ge(act_silu, t + 1)
                wait(dve, pe_hT, t)
                dve.tensor_tensor(mh[:, :], sg, J1[:, :], ALU.mult).then_inc(dve_mh, 1)

            def rows_T(t):
                dve.wait_ge(pe_mx, t + 1)
                if not (isinstance(t, int) and t == 0):
                    dve.wait_ge(pe_gup, FC * t)
                dve.tensor_copy(mxT[:, 4:8, :].rearrange("p a b -> p (a b)"), T1[:, :]).then_inc(dve_mx, 1)

            def weigh(t):
                dve.wait_ge(pe_dnp, FC * (t + 1))
                dve.wait_ge(pool_row, 2 * t + 1)
                dve.wait_ge(st_y, 16 * t)
                dve.tensor_scalar(yb[:, HALF:], O0[:, :], row_c[:, 1:2].bitcast(F32), None, ALU.mult).then_inc(dve_y, 1)

            rows_T(0)
            hidden(0)
            rows_T(1)
            dve.wait_ge(st_h, 16 * TILES)
            end = dve.value_load(tabi[0:1, CUM + NE - 1:CUM + NE], min_val=NE - 1, max_val=MAXT - 1)
            with dve.Fori(1, end + 1) as t:
                hidden_T(t - 1)
                hidden(t)
                rows_T(t + 1)
                weigh(t - 1)
            hidden_T(end)
            weigh(end)


_INS = ["x", "rel_bias", "norm_mix_g", "w_in", "q_norm_g", "k_norm_g", "attn_sink", "conv_w", "conv_b", "gate_b",
        "mlstm_norm_g", "w_out", "norm_ffn_g", "w_router_group", "b_router_group", "w_router_expert",
        "b_router_expert", "w_gate", "w_up", "w_down"]


def bucket_one_hot(buckets, window):
    import math
    import numpy as np
    exact = buckets // 2
    m = np.zeros((buckets, window), np.float32)
    for dist in range(window):
        b = dist if dist < exact else min(buckets - 1, exact + int(
            math.log(dist / exact) / math.log(window / exact) * (buckets - exact)))
        m[b, window - 1 - dist] = 1.0
    return m


def kernel(**inputs):
    import numpy as _np
    import concourse.bacc as _bacc
    from concourse import mybir as _mybir
    from concourse.bass_utils import run_bass_kernel_spmd as _run

    nc = _bacc.Bacc("TRN2", target_bir_lowering=False, num_devices=1)
    arrays, args = {}, []
    for name in _INS:
        a = _np.ascontiguousarray(inputs[name])
        arrays[f"in_{name}_dram"] = a
        args.append(nc.dram_tensor(f"in_{name}_dram", a.shape, _mybir.dt.from_np(a.dtype), kind="ExternalInput").ap())
    a = bucket_one_hot(inputs["rel_bias"].shape[0], 128)
    arrays["bucket_dram"] = a
    args.append(nc.dram_tensor("bucket_dram", a.shape, _mybir.dt.float32, kind="ExternalInput").ap())
    _, seq, width = inputs["x"].shape
    args.append(nc.dram_tensor("out_0_dram", (seq + 128, width), _mybir.dt.float32, kind="ExternalOutput").ap())
    hymba_layer_program(nc, *args)
    r = _run(nc, [arrays], core_ids=[0])
    return r.results[0]["out_0_dram"][:seq].reshape(1, seq, width)
```

```python
import concourse.bass as bass
from concourse import mybir
from contextlib import ExitStack


def hymba_layer_program(nc, x, rel_bias, norm_mix_g, w_in, q_norm_g, k_norm_g, attn_sink, conv_w, conv_b,
                        gate_b, mlstm_norm_g, w_out, norm_ffn_g, w_router_group, b_router_group,
                        w_router_expert, b_router_expert, w_gate, w_up, w_down, bucket_onehot, out):
    F32 = mybir.dt.float32
    I32 = mybir.dt.int32
    U32 = mybir.dt.uint32
    F32R = mybir.dt.float32r
    ALU = mybir.AluOpType
    ACT = mybir.ActivationFunctionType
    AX = mybir.AxisListType.X

    P = 128
    S, D = x.shape[1], x.shape[2]
    TILES = S // P
    KC = D // P
    HEADS, HD = attn_sink.shape[1], q_norm_g.shape[1]
    KVH = 2
    G = HEADS // KVH
    AW = HEADS * HD
    KVW = KVH * HD
    MH = gate_b.shape[1] // 2
    CH = conv_w.shape[2]
    TAPS = conv_w.shape[1]
    CC = CH // P
    DQK = CH // 2 // MH
    MW = mlstm_norm_g.shape[1]
    DV = MW // MH
    VE = DV + 1
    PAIRS = MH // 2
    NG = w_router_group.shape[2]
    NE = w_router_expert.shape[2]
    EPG = NE // NG
    FF = w_gate.shape[3]
    FC = FF // P
    HALF = D // 2
    EPS = 1e-6
    NEG = -1.0e30
    NBK = rel_bias.shape[0]
    RLEN = 3 * P
    MAXT = 2 * S // P + NE
    TCOLS = NE * S // P + 2
    OUTR = S + P

    x2 = x.rearrange("b s d -> (b s) d")
    ctx = ExitStack()
    with ctx:
        def sb(name, shape, dt=F32):
            return ctx.enter_context(nc.sbuf_tensor(name, shape, dt))

        def pb(name):
            return ctx.enter_context(nc.psum_tensor(name, [P, 512], F32))

        def sems(names):
            return [ctx.enter_context(nc.semaphore(n)) for n in names.split()]

        bias_rows = nc.dram_tensor("bias_rows", (HEADS, RLEN), F32, kind="Internal").ap()
        ffn_in = nc.dram_tensor("ffn_in", (OUTR, D), F32, kind="Internal").ap()
        table = nc.dram_tensor("table", (P * TCOLS, 2), I32, kind="Internal").ap()
        table_v = table.rearrange("(p a) c -> p a c", p=P)

        KVG = 2 * KVW + 2 * MH
        NIN = w_in.shape[2]
        c_q, c_cv = KVG, KVG + AW
        c_vm = c_cv + CH
        c_om = c_vm + MW
        phase1 = ExitStack()

        def sb1(name, shape):
            return phase1.enter_context(nc.sbuf_tensor(name, shape, F32))

        wbuf = sb1("w_proj", [P, KC * (NIN + D)])
        mixT = sb1("mixT", [P, KC, P])
        hnT = sb1("hnT", [P, KC, P])
        qT = sb1("qT", [P, G, P])
        osgT = sb1("osg", [P, FC, P])
        osg = osgT[:, :, :].rearrange("p a b -> p (a b)")
        phase1.close()
        PIECES, PW = 3 * FC, 2 * FF
        VP = 2 * FC
        slot_a = sb("slot_a", [P, 2 * PW])
        whi, wlo = sb("w_high", [P, PIECES * PW], F32R), sb("w_low", [P, PIECES * PW], F32R)
        sb("between", [P, KC * (NIN + D) - 2 * (PIECES + 1) * PW])
        mxh, mxl = sb("rows_high", [P, KC, P], F32R), sb("rows_low", [P, KC, P], F32R)
        mhh, mhl = sb("hidden_high", [P, FC, P], F32R), sb("hidden_low", [P, FC, P], F32R)
        wi = wbuf[:, 0:KC * NIN].rearrange("p (k n) -> p k n", k=KC)
        wo = wbuf[:, KC * NIN:].rearrange("p (k n) -> p k n", k=KC)
        wr = sb("wr", [P, KC, NG + NE])
        ident = sb("ident", [P, P])
        tri = sb("tri", [P, P])
        selh = sb("selh", [MH, MH, P])
        selp = sb("selp", [MH, PAIRS, P])
        gmix = sb("gmix", [P, D])
        gffn = sb("gffn", [P, D])
        gq = sb("gq", [P, HD])
        gk = sb("gk", [P, HD])
        sink = sb("sink", [P, HEADS])
        cw = sb("cw", [P, TAPS, CC])
        cb = sb("cb", [P, CC])
        gb = sb("gb", [64, 1])
        gml = sb("gml", [P, MW // P])
        bias = sb("bias", [P, HEADS, 2 * P])
        rbt = sb("rbt", [NBK, HEADS + P])
        rbias = sb("rbias", [P, NG + NE])
        mhalf = sb("mhalf", [P, 16])
        eps_d, eps_hd, eps_dv = (sb(f"eps_{n}", [P, 16]) for n in ("d", "hd", "dv"))
        tick = sb("tick", [1, 32])
        ones_s = sb("ones_s", [MH, P])
        warm = sb("warm", [1, 2])
        xin = sb("xin", [P, 2, D])
        ssx = sb("ssx", [P, 1])
        rsx = sb("rsx", [P, 1])
        hn = sb("hn", [P, D])
        kvg = sb("kvg", [P, KVG])
        q_sb = sb("q_sb", [P, AW])
        sqk = sb("sqk", [P, KVW + AW])
        ssqk = sb("ssqk", [P, KVH + HEADS])
        rqk = sb("rqk", [P, KVH + HEADS])
        qn = sb("qn", [P, G, KVH, HD])
        kn = sb("kn", [P, KVH, HD])
        gt = sb("gt", [P, 64])
        kTw = sb("kTw", [P, 2, P])
        vw = sb("vw", [P, 2, KVW])
        lg = sb("lg", [P, G, 2 * P])
        pr = lg
        PT = sb("PT", [P, G, 2, P])
        junk = PT[:, :, :, :].rearrange("p a b c -> p (a b c)")
        amx = sb("amx", [P, HEADS])
        anm = sb("anm", [P, HEADS])
        aes = sb("aes", [P, HEADS])
        asum = sb("asum", [P, HEADS])
        arc = sb("arc", [P, HEADS])
        pbias = sb("pbias", [P, 1])
        cin = sb("cin", [P, CC, TAPS - 1 + P])
        cy = sb("cy", [P, CC, P])
        qk = sb("qk", [P, 2, CC, P])
        vm = sb("vm", [P, 2, MH, VE])
        giz = sb("giz", [MH, P])
        gfz = sb("gfz", [64, 3, P])
        glf = sb("glf", [MH, P])
        gbm = sb("gbm", [MH, 4, P])
        mprev = sb("mprev", [MH, 1])
        GT = sb("GT", [P, P])
        gT = sb("gT", [P, 68])
        darg = sb("darg", [P, MH, P])
        flip = darg[:, 0, :]
        dmat = sd = darg
        qg = sb("qg", [P, PAIRS, P])
        dec = sb("dec", [P, PAIRS])
        kw = sb("kw", [P, MH, DQK])
        Cst = sb("Cst", [P, PAIRS, VE])
        hden, hd2, hrr, hsn = (sb(f"h_{n}", [P, MH]) for n in ("den", "den_sq", "scale", "num_sq"))
        hss = sb("hss", [P, MH])
        hrs = sb("hrs", [P, MH])
        mix = hn
        ssh = sb("ssh", [P, 1])
        rsh = sb("rsh", [P, 1])
        h2 = sb("h2", [P, D])
        h2T = mixT
        brow = h2[0:HEADS, 0:RLEN]
        rl = sb("rl", [P, TILES, NG + NE])

        pay = sb("pay", [P, TILES, 2, 2], I32)
        desti = sb("desti", [P, TILES, 2], I32)
        xg = hn
        yb = lg[:, :, :].rearrange("p a b -> p (a b)")
        NI = MAXT + 2
        FIRST, LAST, ROWS = 0, NE, 2 * NE
        tabi = sb("tabi", [1, 2 * NE + NI], I32)
        rows = sb("rows", [P, TCOLS, 2], I32)
        row_g, row_s = sb("row_g", [P, 1], I32), sb("row_s", [P, 1], I32)
        wt_t = sb("wt_t", [P, 2], F32)
        slot = [slot_a[:, 0:PW], slot_a[:, PW:], gmix[:, :], xin[:, 0, :],
                vm[:, :, :, :].rearrange("p a h e -> p (a h e)")[:, 0:PW],
                qk[:, :, :, :].rearrange("p a b c -> p (a b c)"), gffn[:, :], xin[:, 1, :], h2[:, :], junk,
                *(bias[:, 4 * n:4 * n + 4, :].rearrange("p a b -> p (a b)") for n in range(2))]
        ints = sb("ints", [P, NI + TILES], I32)
        route_e = sb("route_e", [P, TILES * (NG + 1)])
        iota_f, iota_m = sb("iota_f", [P, NI]), sb("iota_m", [P, NG])
        off_e = sb("off_e", [P, TILES + 1, NE])
        Mall = sqk[:, 0:TILES * NE]
        onesm = kvg[:, 0:P]
        strict = darg[:, 0, :]
        mh = q_sb

        T0, T1, J0, J1, S0, S1, O0, X0 = [pb(f"bank_{n}") for n in "t0 t1 j0 j1 s0 s1 o0 x0".split()]
        TB = [T0, T1]

        (ld_xn, ld_x0, ld_x1, ld_gn, ld_w0, ld_w1, ld_w2, ld_w3, ld_w4, ld_wo, ld_c, ld_rb, ld_bias, st_brow, st_h, st_h2,
         st_tab, st_zero) = sems("ld_xnorm ld_x0 ld_x1 ld_gain ld_wkvg ld_wq ld_wconv ld_wvm ld_wom ld_wo ld_consts ld_relbias "
                                 "ld_bias st_brow st_h st_ffn st_table st_zero")
        LDX = [ld_x0, ld_x1]
        (pool_const, pe_brow, dve_brow, pe_bias, dve_bias) = sems("pool_const pe_brow dve_brow pe_bias dve_bias")
        (pe_qkT, pe_hnT, pe_s0, pe_s1, pe_kvg, pe_g, pe_pT0, pe_pT1, pe_q, pe_pv0, pe_o, pe_cin, pe_st,
         pe_vm, pe_h, pe_u, pe_om, pe_mixT, pe_y0, pe_y1, pe_h2T, pe_r) = sems(
            "pe_qkT pe_hnT pe_s0 pe_s1 pe_kvg pe_g pe_pT0 pe_pT1 pe_q pe_pv0 pe_o pe_cin pe_st "
            "pe_vm pe_h pe_u pe_om pe_mixT pe_y0 pe_y1 pe_h2T pe_r")
        (act_v, act_qT, act_ssx, act_ln, act_hnT, act_p0, act_g, act_kvg, act_pT0, act_D, act_p1, act_q,
         act_pT1, act_cin, act_vm, act_mixT, act_qk, act_om, act_ssh, act_h2T, act_ssn) = sems(
            "act_v act_qT act_ssx act_ln act_hnT act_p0 act_g act_kvg act_pT0 act_D act_p1 act_q "
            "act_pT1 act_cin act_vm act_mixT act_qk act_om act_ssh act_h2T act_ssn")
        (dve_kg, dve_az, dve_hn, dve_nm0, dve_L0, dve_L1, dve_nm1, dve_ca, dve_hnT, dve_gT, dve_darg, dve_qg,
         dve_pT0, dve_pT1, dve_kw, dve_att, dve_sd, dve_qkn, dve_C, dve_mix, dve_mixT, dve_h,
         dve_h0, dve_hn2, dve_h2T, dve_rl, dve_cy, dve_sqk, dve_hss) = sems(
            "dve_kg dve_az dve_hn dve_nm0 dve_L0 dve_L1 dve_nm1 dve_ca dve_hnT dve_gT dve_darg dve_qg "
            "dve_pT0 dve_pT1 dve_kw dve_att dve_sd dve_qkn dve_C dve_mix dve_mixT dve_h "
            "dve_h0 dve_hn2 dve_h2T dve_rl dve_cy dve_sqk dve_hss")
        (pool_rx, pool_rqk, pool_rhm, pool_rh, pool_wo, dve_const, dve_den) = sems("pool_rx pool_rqk pool_rhm pool_rh pool_wo dve_const dve_den")
        (dve_chain, act_chain, pool_chain) = sems("dve_chain act_chain pool_chain")
        (dve_M, pe_pos, dve_pay, st_rows, dve_tab, dve_rt, act_rt) = sems(
            "dve_masks pe_positions dve_payload st_rows dve_tables dve_logits act_route")
        ld_slot = sems(" ".join(f"ld_slot{j}" for j in range(PIECES)))
        (ld_rows, ld_g, st_y, act_hi, lo_a, lo_b, pe_mx, pe_gup, pe_hT, pe_dnp, act_silu, act_mx, act_hT, act_y,
         dve_mh, dve_mx, dve_hT, dve_y, pool_rowg, dve_wt, dve_rows) = sems(
            "ld_rows ld_gathered st_y act_hi lo_a lo_b pe_mx pe_gateup pe_hT pe_down act_silu act_mx act_hT act_y "
            "dve_mh dve_mx dve_hT dve_y pool_rowg dve_wt dve_rows")

        block = ctx.enter_context(nc.Block())

        def wait(eng, sem, value):
            if not (isinstance(value, int) and value <= 0):
                eng.wait_ge(sem, value)

        class Chain:

            def __init__(self, eng, sem):
                self.eng, self.sem, self.base, self.n, self.start = eng, sem, 0, 0, 0
                self.wait = eng.wait_ge

            def begin_tiles(self):
                self.start = self.n

            def at(self, base):
                self.base, self.n = self.start + base, 0

            def __call__(self, ins):
                self.n += 1
                ins.then_inc(self.sem, 1)
                self.wait(self.sem, self.base + self.n)

        def tiles(eng, body, chain=None, per_tile=0):
            base = 0

            def one(t, u, main, nxt, ahead, at):
                if chain is not None:
                    chain.at(at)
                body(t, u, main, nxt, ahead)
                return 0 if chain is None else chain.n
            if chain is not None:
                chain.begin_tiles()
            base += one(-2, 0, False, False, True, base)
            base += one(-1, 1, False, True, True, base)
            with eng.Fori(0, (TILES - 2) // 2) as pair:
                for u in range(2):
                    t = 2 * pair + u
                    n = one(t, u, True, True, True, t * per_tile + base)
                    assert n == per_tile, n
            base += (TILES - 2) * per_tile
            base += one(TILES - 2, 0, True, True, False, base)
            one(TILES - 1, 1, True, False, False, base)

        def order(i):
            return (i % 2) * FC + i // 2 if i < 2 * FC else i

        def lo_ready(e, i):
            return (lo_a, e * VP + (i + 1)) if i < VP else (lo_b, e * (PIECES - VP) + (i - VP + 1))

        def split_free(i):
            return (pe_gup, i // 2 + 1) if i < 2 * FC else (pe_dnp, i - 2 * FC + 1)

        @block.sync
        def _(sp):
            sp.dma_start(hn[:, :], x2[0:P, :]).then_inc(ld_xn, 16)
            sp.dma_start(gmix[:, :], norm_mix_g[0, :].partition_broadcast(P)).then_inc(ld_gn, 16)
            sp.dma_start(rbt[:, 0:HEADS], rel_bias).then_inc(ld_rb, 16)
            sp.dma_start(rbt[:, HEADS:], bucket_onehot).then_inc(ld_rb, 16)
            w_v = w_in[0].rearrange("(k p) n -> p k n", p=P)
            a0 = AW + 2 * KVW
            sp.dma_start(wi[:, :, 0:2 * KVW], w_v[:, :, AW:a0]).then_inc(ld_w0, 16)
            sp.dma_start(wi[:, :, 2 * KVW:KVG], w_v[:, :, NIN - 2 * MH:NIN]).then_inc(ld_w0, 16)
            sp.dma_start(wi[:, :, c_q:c_cv], w_v[:, :, 0:AW]).then_inc(ld_w1, 16)
            for src, dst in ((q_norm_g[0, :].partition_broadcast(P), gq[:, :]),
                             (k_norm_g[0, :].partition_broadcast(P), gk[:, :]),
                             (attn_sink[0, :].partition_broadcast(P), sink[:, :]),
                             (mlstm_norm_g[0].rearrange("(c p) -> p c", p=P), gml[:, :]),
                             (norm_ffn_g[0, :].partition_broadcast(P), gffn[:, :]),
                             (b_router_group[0, :].partition_broadcast(P), rbias[:, 0:NG]),
                             (b_router_expert[0, :].partition_broadcast(P), rbias[:, NG:]),
                             *((conv_w[0, k].rearrange("(c p) -> p c", p=P), cw[:, k, :]) for k in range(TAPS)),
                             (conv_b[0].rearrange("(c p) -> p c", p=P), cb[:, :]),
                             (gate_b[0, 0:MH].rearrange("(h o) -> h o", o=1), gb[0:MH, :]),
                             (gate_b[0, MH:].rearrange("(h o) -> h o", o=1), gb[32:32 + MH, :])):
                with nc.allow_non_contiguous_dma("small constants"):
                    sp.dma_start(dst, src).then_inc(ld_c, 16)
            sp.wait_ge(pe_hnT, 1)
            sp.dma_start(hn[:, :], x2[P:2 * P, :]).then_inc(ld_xn, 16)
            sp.dma_start(wi[:, :, c_cv:c_vm], w_v[:, :, a0:a0 + CH]).then_inc(ld_w2, 16)
            sp.dma_start(wi[:, :, c_vm:c_om], w_v[:, :, a0 + CH:a0 + CH + MW]).then_inc(ld_w3, 16)
            sp.dma_start(wi[:, :, c_om:NIN], w_v[:, :, a0 + CH + MW:a0 + CH + 2 * MW]).then_inc(ld_w4, 16)
            sp.wait_ge(dve_brow, 1)
            sp.dma_start(bias_rows, brow[:, :]).then_inc(st_brow, 16)
            sp.wait_ge(st_brow, 16)
            sp.dma_start(bias[:, :, :], bass.AP(tensor=bias_rows.tensor, offset=0,
                                                ap=[[1, P], [RLEN, HEADS], [1, 2 * P]])).then_inc(ld_bias, 16)
            for u in range(2):
                sp.dma_start(xin[:, u, :], x2[u * P:(u + 1) * P, :]).then_inc(LDX[u], 16)
            sp.dma_start(wo[:, :, :], w_out[0].rearrange("(k p) n -> p k n", p=P)).then_inc(ld_wo, 16)
            sp.dma_start(wr[:, :, 0:NG], w_router_group[0].rearrange("(p k) n -> p k n", p=P)).then_inc(ld_wo, 16)
            sp.dma_start(wr[:, :, NG:], w_router_expert[0].rearrange("(p k) n -> p k n", p=P)).then_inc(ld_wo, 16)
            sp.wait_ge(pool_const, 6)
            sp.dma_start(table_v, rows[:, :, :]).then_inc(st_tab, 16)
            for dst in (out, ffn_in):
                for half in range(2):
                    sp.dma_start(dst[S:, half * HALF:(half + 1) * HALF], h2[:, HALF:]).then_inc(st_zero, 16)

            def body(t, u, main, nxt, ahead):
                if not main:
                    return
                if ahead:
                    sp.wait_ge(pe_mixT, t + 1)
                    sp.dma_start(hn[:, :], x2[bass.ds((t + 2) * P, P), :]).then_inc(ld_xn, 16)
                sp.wait_ge(dve_h, t + 1)
                sp.dma_start(out[bass.ds(t * P, P), :] if not isinstance(t, int) else out[t * P:t * P + P, :],
                             xin[:, u, :]).then_inc(st_h, 16)
                sp.wait_ge(dve_hn2, t + 1)
                sp.dma_start(ffn_in[bass.ds(t * P, P), :] if not isinstance(t, int)
                             else ffn_in[t * P:t * P + P, :], h2[:, :]).then_inc(st_h2, 16)
                if ahead:
                    sp.wait_ge(st_h, 16 * t + 16)
                    sp.wait_ge(act_ssh, t + 1)
                    sp.dma_start(xin[:, u, :], x2[bass.ds((t + 2) * P, P), :]).then_inc(LDX[u], 16)
            tiles(sp, body)
            wg = w_gate[0].rearrange("e (p k) n -> e p k n", p=P)
            wu = w_up[0].rearrange("e (p k) n -> e p k n", p=P)
            wd = w_down[0].rearrange("e (c p) n -> e p c n", p=P)

            def load_piece(e, i):
                ei = slice(e, e + 1) if isinstance(e, int) else bass.ds(e, 1)
                dst = slot[i]
                if i < 2 * FC:
                    j, w = i // 2, (wg, wu)[i % 2]
                    dst, src = dst.rearrange("p (k n) -> p k n", k=2), w[ei, :, 2 * j:2 * j + 2, :].rearrange(
                        "e p k n -> (e p) k n")
                else:
                    src = wd[ei, :, i - 2 * FC, :].rearrange("e p n -> (e p) n")
                sp.dma_start(dst, src).then_inc(ld_slot[i], 16)

            sp.wait_ge(pe_om, TILES)
            for i in range(PIECES):
                if i == 2:
                    sp.wait_ge(dve_hn, TILES)
                if i == 3:
                    sp.wait_ge(st_h, 16 * (TILES - 1))
                if i == 4:
                    sp.wait_ge(pe_u, TILES)
                if i == 6:
                    sp.wait_ge(dve_hn2, TILES)
                    sp.wait_ge(act_ssh, TILES)
                    sp.wait_ge(st_h, 16 * TILES)
                if i == 8:
                    sp.wait_ge(pe_h2T, TILES)
                    sp.wait_ge(st_h2, 16 * TILES)
                if i == 10:
                    sp.wait_ge(dve_L1, TILES)
                load_piece(0, i)
            sp.wait_ge(st_rows, 16 * 2 * TILES)
            sp.dma_start(rows[:, :, :], table_v).then_inc(ld_rows, 16)
            sp.wait_ge(pe_mx, 1)
            with sp.Fori(1, NE) as e:
                for i in range(PIECES):
                    sp.wait_ge(*lo_ready(e - 1, i))
                    load_piece(e, i)

        @block.gpsimd
        def _(pool):
            chain = Chain(pool, pool_chain)
            chain(pool.memset(ident[:, :], 0.0))
            chain(pool.affine_select(out=ident[:, :], in_=ident[:, :], compare_op=ALU.not_equal, fill=1.0,
                                     base=0, pattern=[[-1, P]], channel_multiplier=1))
            chain(pool.memset(flip, 0.0))
            chain(pool.affine_select(out=flip, in_=flip, compare_op=ALU.not_equal, fill=1.0,
                                     base=1 - P, pattern=[[1, P]], channel_multiplier=1))
            chain(pool.memset(tri[:, :], 0.0))
            chain(pool.affine_select(out=tri[:, :], in_=tri[:, :], compare_op=ALU.is_ge, fill=NEG,
                                     base=0, pattern=[[1, P]], channel_multiplier=-1))
            pool.memset(mhalf[:, :], -0.5).then_inc(pool_const, 1)
            chain(pool.memset(selh[:, :, :], 0.0))
            chain(pool.affine_select(out=selh[:, :, :], in_=selh[:, :, :], compare_op=ALU.not_equal, fill=1.0,
                                     base=0, pattern=[[-1, MH], [0, P]], channel_multiplier=1))
            chain(pool.memset(selp[:, :, :], 0.0))
            sv = selp[:, :, :].rearrange("h c (a b) -> h c a b", a=2)
            chain(pool.affine_select(out=sv, in_=sv, compare_op=ALU.not_equal, fill=1.0, base=0,
                                     pattern=[[-2, PAIRS], [-1, 2], [0, P // 2]], channel_multiplier=1))
            pool.memset(warm[:, :], 0.0)
            pool.memset(ones_s[:, :], 1.0).then_inc(pool_const, 1)
            pool.memset(brow[:, :], NEG).then_inc(pool_const, 1)
            chain(pool.memset(rows[:, :, 1], 0))
            pool.iota(rows[:, :, 0], pattern=[[0, TCOLS]], base=S, channel_multiplier=1).then_inc(pool_const, 1)
            pool.memset(h2[:, HALF:], 0.0).then_inc(pool_const, 1)
            pool.iota(ints[:, 0:NI], pattern=[[1, NI]], base=0, channel_multiplier=0)
            pool.iota(ints[:, NI:], pattern=[[P, TILES]], base=0, channel_multiplier=1)
            for e, n in ((eps_d, D), (eps_hd, HD), (eps_dv, DV)):
                pool.memset(e[:, :], n * EPS)
            for z in (GT[:, :], gt[:, :], mprev[:, :], Cst[:, :, :], kTw[:, 1, :], vw[:, 1, :],
                      cin[:, :, 0:TAPS - 1]):
                chain(pool.memset(z, 0.0))
            chain(pool.memset(pbias[:, :], NEG))
            pool.memset(vm[:, :, :, DV:VE], 1.0).then_inc(pool_const, 1)

            def pwait(sem, value):
                pool.wait_ge(sem, value)
                if not isinstance(value, int):
                    ticks.append(len(ticks))
                    pool.tensor_tensor(tick[:, len(ticks):len(ticks) + 1], mhalf[0:1, 0:1], mhalf[0:1, 0:1], ALU.mult)
            ticks = []

            def rsqrt(root, ss, done, add):
                chain(pool.tensor_tensor(root, ss, add[:, 0:root.shape[1]], ALU.add))
                pool.tensor_tensor(root, root, mhalf[:, 0:root.shape[1]], ALU.pow).then_inc(done, 1)

            def scatter_rows(a, b, n):
                pool.wait_ge(dve_pay, n)
                for t in range(a, b):
                    for c in range(2):
                        pool.indirect_dma_start(
                            out=table, out_offset=bass.IndirectOffsetOnAxis(
                                ap=desti[:, t, c:c + 1].bitcast(U32), axis=0),
                            in_=pay[:, t, c, :], in_offset=None).then_inc(st_rows, 16)

            def body(t, u, main, nxt, ahead):
                if nxt:
                    pool.wait_ge(dve_sqk, t + 2)
                    rsqrt(rqk[:, :], ssqk[:, :], pool_rqk, eps_hd)
                if main:
                    pool.wait_ge(dve_hss, t + 1)
                    rsqrt(hrs[:, :], hss[:, :], pool_rhm, eps_dv)
                if ahead:
                    pool.wait_ge(act_ssx, t + 3)
                    rsqrt(rsx[:, :], ssx[:, :], pool_rx, eps_d)
                if nxt and not main:
                    pool.wait_ge(dve_const, 1)
                    pool.wait_ge(ld_wo, 48)
                    for c in range(MW // P):
                        ins = pool.tensor_tensor(wo[:, AW // P + c, :], wo[:, AW // P + c, :],
                                                 gml[:, c:c + 1].to_broadcast([P, D]), ALU.mult)
                    ins.then_inc(pool_wo, 1)
                if main:
                    pool.wait_ge(act_ssh, t + 1)
                    rsqrt(rsh[:, :], ssh[:, :], pool_rh, eps_d)
                if main and not nxt:
                    pool.wait_ge(st_tab, 16)
                    scatter_rows(0, TILES - 1, 1)
            tiles(pool, body, chain, 4)

            scatter_rows(TILES - 1, TILES, 2)
            pool.wait_ge(st_rows, 16 * 2 * TILES)

            def gather():
                pool.indirect_dma_start(
                    out=xg[:, :], out_offset=None, in_=ffn_in,
                    in_offset=bass.IndirectOffsetOnAxis(ap=row_g[:, 0:1].bitcast(U32), axis=0)).then_inc(ld_g, 16)

            def scatter_add():
                pool.indirect_dma_start(
                    out=out, out_offset=bass.IndirectOffsetOnAxis(ap=row_s[:, 0:1].bitcast(U32), axis=0),
                    in_=yb[:, :], in_offset=None, compute_op=ALU.add).then_inc(st_y, 16)

            def pick(dst, t):
                at = tabi[0:1, ROWS + t:ROWS + t + 1] if isinstance(t, int) else tabi[0:1, bass.ds(t + ROWS, 1)]
                col = pool.value_load(at, min_val=0, max_val=TCOLS - 1)
                pool.tensor_copy(dst[:, :], rows[:, bass.ds(col, 1), 0:1].rearrange(
                    "p a c -> p (a c)")).then_inc(pool_rowg, 1)

            pool.wait_ge(st_h2, 16 * TILES)
            pool.wait_ge(pe_h2T, TILES)
            pool.wait_ge(ld_rows, 16)
            pool.tensor_copy(row_g[:, :], rows[:, 0, 0:1]).then_inc(pool_rowg, 1)
            pool.wait_ge(pool_rowg, 1)
            gather()
            pool.wait_ge(dve_tab, 1)
            pool.wait_ge(ld_g, 16)
            pick(row_g, 1)
            pool.wait_ge(pool_rowg, 2)
            pool.wait_ge(pe_mx, 1)
            gather()
            pool.wait_ge(st_h, 16 * TILES)

            def tile(t, split):
                pwait(ld_g, 16 * t + 32)
                pick(row_g, t + 2)
                pwait(pool_rowg, 2 * t + 3)
                pwait(pe_mx, t + 2)
                gather()
                split(VP, 2 * FC)
                pwait(act_y, t + 1)
                pwait(dve_y, t + 1)
                pick(row_s, t)
                pwait(pool_rowg, 2 * t + 4)
                scatter_add()
                split(2 * FC, PIECES)

            def inner_tiles(e):
                first = pool.value_load(tabi[0:1, FIRST + e:FIRST + e + 1] if isinstance(e, int) else
                                        tabi[0:1, bass.ds(e + FIRST, 1)], min_val=0, max_val=MAXT - 1)
                last = pool.value_load(tabi[0:1, LAST + e:LAST + e + 1] if isinstance(e, int) else
                                       tabi[0:1, bass.ds(e + LAST, 1)], min_val=0, max_val=MAXT - 1)
                with pool.If(first < last):
                    with pool.Fori(first, last) as t:
                        tile(t, lambda a, b: None)
                return last

            with pool.Fori(0, NE - 1) as e:
                last = inner_tiles(e)

                def split(a, b):
                    for i in range(a, b):
                        pool.wait_ge(act_hi, e * PIECES + (PIECES + i + 1))
                        at = slice(order(i) * PW, order(i) * PW + PW)
                        pool.tensor_tensor(wlo[:, at], slot[i], whi[:, at].bitcast(F32),
                                           ALU.subtract).then_inc(lo_ready(e + 1, i)[0], 1)
                tile(last, split)
            end = inner_tiles(NE - 1)
            tile(end, lambda a, b: None)
            pwait(st_y, 16 * end + 16)
            pwait(ld_g, 16 * end + 48)

        @block.scalar
        def _(act):
            chain = Chain(act, act_chain)

            def cp(dst, src):
                return act.activation(dst, src, ACT.Copy)

            def route_exp(count, n):
                act.wait_ge(dve_rt, n)
                act.activation(route_e[:, 0:count * (NG + 1)], route_e[:, 0:count * (NG + 1)],
                               ACT.Exp).then_inc(act_rt, 1)

            def exps(t, g, nm_done, done):
                act.wait_ge(nm_done, t + 1)
                for j in range(G):
                    h = g * G + j
                    act.activation(pr[:, j, :], lg[:, j, :], ACT.Exp, bias=anm[:, h:h + 1],
                                   accum_out=asum[:, h:h + 1])
                act.activation(aes[:, g * G:g * G + G], aes[:, g * G:g * G + G], ACT.Exp).then_inc(done, 1)

            def body(t, u, main, nxt, ahead):
                v = 1 - u
                if nxt:
                    act.wait_ge(pe_hnT, t + 2)
                    wait(act, pe_om, t + 1)
                    cp(hnT[:, 0:4, :].rearrange("p a b -> p (a b)"), T0[:, :]).then_inc(act_hnT, 1)
                if main:
                    act.wait_ge(pe_qkT, t + 1)
                    wait(act, pe_s1, t)
                    cp(qT[:, :, :].rearrange("p a b -> p (a b)"), S0[:, :]).then_inc(act_qT, 1)
                    act.wait_ge(act_kvg, t + 1)
                    wait(act, pe_o, t)
                    cp(vw[:, u, :], kvg[:, KVW:2 * KVW]).then_inc(act_v, 1)
                    act.wait_ge(dve_az, t + 1)
                    chain(act.activation(gfz[32:32 + MH, 1, :], gfz[32:32 + MH, 0, :], ACT.Exp, scale=-1.0))
                    act.activation(gfz[32:32 + MH, 1, :], gfz[32:32 + MH, 1, :], ACT.Ln, bias=1.0).then_inc(act_ln, 1)
                if nxt:
                    act.wait_ge(pe_kvg, t + 2)
                    wait(act, dve_qkn, t + 1)
                    if main:
                        act.wait_ge(act_v, t + 1)
                    cp(kvg[:, :], J0[:, 0:KVG])
                    act.activation(sqk[:, 0:KVW], J0[:, 0:KVW], ACT.Square).then_inc(act_kvg, 1)
                if main:
                    act.wait_ge(dve_ca, t + 1)
                    act.activation(gbm[:, 3, :], gbm[:, 2, :], ACT.Exp, bias=mprev[:, :])
                    act.activation(GT[32:32 + MH, :], GT[0:MH, :], ACT.Exp, bias=gbm[:, 2, P - 1:P])
                    act.activation(GT[64:64 + MH, :], gbm[:, 1, :], ACT.Exp, scale=-1.0).then_inc(act_g, 1)
                    exps(t, 0, dve_nm0, act_p0)
                if nxt:
                    act.wait_ge(pe_q, t + 2)
                    cp(q_sb[:, :], J1[:, :])
                    act.activation(sqk[:, KVW:], J1[:, :], ACT.Square).then_inc(act_q, 1)
                if main:
                    act.wait_ge(pe_pT0, t + 1)
                    cp(PT[:, 0:2, :, :].rearrange("p a b c -> p (a b c)"), T0[:, :]).then_inc(act_pT0, 1)
                    act.wait_ge(dve_darg, t + 1)
                    act.wait_ge(dve_gT, t + 1)
                    for h in range(MH):
                        ins = act.activation(dmat[:, h, :], darg[:, h, :], ACT.Exp, bias=gT[:, h:h + 1])
                    ins.then_inc(act_D, 1)
                    exps(t, 1, dve_nm1, act_p1)
                    act.wait_ge(pe_pT1, t + 1)
                    cp(PT[:, 0:2, :, :].rearrange("p a b c -> p (a b c)"), T0[:, :]).then_inc(act_pT1, 1)
                if nxt:
                    act.wait_ge(pe_cin, t + 2)
                    wait(act, dve_cy, t + 1)
                    cp(cin[:, :, TAPS - 1:], J0[:, :].rearrange("p (a b) -> p a b", a=CC)).then_inc(act_cin, 1)
                if main:
                    act.wait_ge(dve_den, t + 1)
                    wait(act, act_ssh, t)
                    for h in range(MH):
                        c = h // 2
                        ins = act.activation(junk[:, h * DV:(h + 1) * DV], (S0, S1)[h % 2][:, c * VE:c * VE + DV],
                                             ACT.Square, accum_out=hsn[:, h:h + 1])
                    ins.then_inc(act_ssn, 1)
                if nxt:
                    act.wait_ge(pe_vm, t + 2)
                    cp(vm[:, v, :, 0:DV], J1[:, :].rearrange("p (a b) -> p a b", a=MH)).then_inc(act_vm, 1)
                if main:
                    act.wait_ge(pe_mixT, t + 1)
                    wait(act, pe_r, t)
                    cp(mixT[:, 0:4, :].rearrange("p a b -> p (a b)"), T0[:, :]).then_inc(act_mixT, 1)
                if main and not nxt:
                    route_exp(TILES - 1, 1)
                if ahead:
                    act.wait_ge(ld_xn, 16 * (t + 3))
                    wait(act, dve_hn, t + 2)
                    if main:
                        act.wait_ge(act_ssn, t + 1)
                    act.activation(junk, hn[:, :], ACT.Square, accum_out=ssx[:, :]).then_inc(act_ssx, 1)
                if nxt:
                    act.wait_ge(dve_cy, t + 2)
                    wait(act, dve_qg, t)
                    wait(act, pe_st, t)
                    for c in range(CC):
                        ins = act.activation(qk[:, v, c, :], cy[:, c, :], ACT.Silu, bias=cb[:, c:c + 1])
                    ins.then_inc(act_qk, 1)
                if main:
                    act.wait_ge(dve_h, t + 1)
                    if ahead:
                        act.wait_ge(act_ssx, t + 3)
                    act.activation(junk, xin[:, u, :], ACT.Square, accum_out=ssh[:, :]).then_inc(act_ssh, 1)
                    act.wait_ge(pe_h2T, t + 1)
                    cp(h2T[:, 0:4, :].rearrange("p a b -> p (a b)"), T0[:, :]).then_inc(act_h2T, 1)
                if nxt:
                    act.wait_ge(pe_om, t + 2)
                    wait(act, dve_mix, t + 1)
                    act.activation(osg, J0[:, :], ACT.Sigmoid).then_inc(act_om, 1)
            tiles(act, body, chain, 1)

            sg = cy[:, :, :].rearrange("p a b -> p (a b)")
            HF = FF // 2

            def silu(t, half):
                act.wait_ge(pe_gup, (FC + 1) * t + (1 if half == 0 else FC + 1))
                wait(act, dve_mh, 2 * t)
                act.activation(sg[:, half * HF:(half + 1) * HF], (J0, J1)[half][:, 0:HF], ACT.Silu).then_inc(act_silu, 1)

            def rows_hi(t):
                act.wait_ge(pe_mx, t + 1)
                if not (isinstance(t, int) and t == 0):
                    act.wait_ge(pe_gup, (FC + 1) * t)
                for b in range(2):
                    cp(mxh[:, 4 * b:4 * b + 4, :].rearrange("p a b -> p (a b)"), TB[b][:, :]).then_inc(act_mx, 1)

            def hidden_hi(t, half):
                act.wait_ge(pe_hT, 2 * t + half + 1)
                wait(act, pe_dnp, FC * t)
                cp(mhh[:, 2 * half:2 * half + 2, :].rearrange("p a b -> p (a b)"),
                   (S0, X0)[half][:, 0:HF]).then_inc(act_hT, 1)

            def weigh(t):
                act.wait_ge(pe_dnp, FC * (t + 1))
                act.wait_ge(dve_wt, t + 1)
                act.wait_ge(st_y, 16 * t)
                act.activation(yb[:, 0:HALF], S1[:, :], ACT.Copy, scale=wt_t[:, 0:1]).then_inc(act_y, 1)

            def split_hi(e, i, last):
                act.wait_ge(ld_slot[i], e * 16 + 16)
                if last is not None:
                    sem, n = split_free(i)
                    act.wait_ge(sem, last * (FC + 1) + n + 1 if i < 2 * FC else last * FC + n)
                at = order(i) * PW
                cp(whi[:, at:at + PW], slot[i]).then_inc(act_hi, 1)

            route_exp(1, 2)
            act.wait_ge(pe_y1, TILES)
            for i in range(PIECES):
                split_hi(0, i, None)
            act.wait_ge(dve_tab, 1)
            rows_hi(0)

            def tile(t, split):
                act.activation(warm[:, 0:1], warm[:, 1:2], ACT.Silu)
                silu(t, 0)
                split(0, 2)
                hidden_hi(t, 0)
                split(2, 3)
                silu(t, 1)
                hidden_hi(t, 1)
                rows_hi(t + 1)
                split(3, 2 * FC)
                weigh(t)
                split(2 * FC, PIECES)

            def inner_tiles(e):
                first = act.value_load(tabi[0:1, FIRST + e:FIRST + e + 1] if isinstance(e, int) else
                                       tabi[0:1, bass.ds(e + FIRST, 1)], min_val=0, max_val=MAXT - 1)
                last = act.value_load(tabi[0:1, LAST + e:LAST + e + 1] if isinstance(e, int) else
                                      tabi[0:1, bass.ds(e + LAST, 1)], min_val=0, max_val=MAXT - 1)
                with act.If(first < last):
                    with act.Fori(first, last) as t:
                        tile(t, lambda a, b: None)
                return last

            with act.Fori(0, NE - 1) as e:
                last = inner_tiles(e)

                def split(a, b):
                    for i in range(a, b):
                        split_hi(e + 1, i, last)
                tile(last, split)
            tile(inner_tiles(NE - 1), lambda a, b: None)

        @block.tensor
        def _(pe):
            def transposes(src, dst):
                for b in range(2):
                    for i in range(4):
                        ins = pe.transpose(TB[b][:, i * P:(i + 1) * P], src[:, (4 * b + i) * P:(4 * b + i + 1) * P],
                                           ident[:, :])
                ins.then_inc(dst, 1)

            def project(bank, c0, n, done, w_ready, w_count, t):
                wait(pe, w_ready, w_count)
                for k in range(KC):
                    ins = pe.matmul(bank[:, 0:n], hnT[:, k, :], wi[:, k, c0:c0 + n], start=(k == 0),
                                    stop=(k == KC - 1))
                ins.then_inc(done, 1)

            pe.wait_ge(ld_rb, 32)
            pe.matmul(X0[0:HEADS, 0:P], rbt[:, 0:HEADS], rbt[:, HEADS:], start=True, stop=True).then_inc(pe_brow, 1)
            pe.wait_ge(pool_const, 6)

            def positions(count, n):
                pe.wait_ge(dve_M, n)
                if n > 1:
                    pe.wait_ge(dve_pay, n - 1)
                pe.matmul(S0[:, 0:count * NE], strict, Mall[:, 0:count * NE], start=True, stop=True)
                pe.matmul(S1[:, 0:count * NE], onesm, Mall[:, 0:count * NE], start=True, stop=True).then_inc(pe_pos, 1)

            def body(t, u, main, nxt, ahead):
                v = 1 - u
                if nxt:
                    pe.wait_ge(dve_hn, t + 2)
                    transposes(hn, pe_hnT)
                if main:
                    pe.wait_ge(dve_qkn, t + 1)
                    pe.wait_ge(dve_bias, 1)
                    qf = qn[:, :, :, :].rearrange("p j g d -> p j (g d)")
                    for j in range(G):
                        pe.transpose(S0[:, j * P:(j + 1) * P], qf[:, j, :], ident[:, :])
                    pe.transpose(S1[:, 0:P], kn[:, :, :].rearrange("p g d -> p (g d)"), ident[:, :])
                    pe.transpose(S1[0:64, P:2 * P], gt[:, :], ident[:, :]).then_inc(pe_qkT, 1)

                def scores(g, done):
                    for j in range(G):
                        b = (S0, S1)[j // 2]
                        for w, slot in ((0, v), (1, u)):
                            c = (j % 2) * 2 * P + w * P
                            ins = pe.matmul(b[:, c:c + P], qT[64 * g:64 * g + 64, j, :],
                                            kTw[64 * g:64 * g + 64, slot, :], start=True, stop=True)
                    ins.then_inc(done, 1)

                def probs_T(done):
                    for j in range(G):
                        for w in range(2):
                            c = (j % 2) * 2 * P + w * P
                            ins = pe.transpose(TB[j // 2][:, c:c + P], pr[:, j, w * P:(w + 1) * P], ident[:, :])
                    ins.then_inc(done, 1)

                def values(g, done):
                    for j in range(G):
                        h = g * G + j
                        for w, slot in ((0, v), (1, u)):
                            ins = pe.matmul(O0[:, h * HD:(h + 1) * HD], PT[:, j, w, :],
                                            vw[:, slot, g * HD:(g + 1) * HD], start=(w == 0), stop=(w == 1))
                    if done is not None:
                        ins.then_inc(done, 1)

                def conv_channels(cs):
                    for c in cs:
                        for k in range(KC):
                            ins = pe.matmul(J0[:, c * P:(c + 1) * P], wi[:, k, c_cv + c * P:c_cv + (c + 1) * P],
                                            hnT[:, k, :], start=(k == 0), stop=(k == KC - 1))
                    return ins

                if nxt:
                    pe.wait_ge(act_hnT, t + 2)
                    pe.wait_ge(dve_hnT, t + 2)
                    wait(pe, act_om, t + 1)
                    project(J0, 0, KVG, pe_kvg, ld_w0, 32, t)
                if main:
                    pe.wait_ge(act_qT, t + 1)
                    pe.wait_ge(dve_kg, t + 1)
                    scores(0, pe_s0)
                if nxt:
                    wait(pe, dve_h, t)
                    project(J1, c_q, AW, pe_q, ld_w1, 16, t)
                if main:
                    pe.wait_ge(act_qk, t + 1)
                    wait(pe, dve_rl, t)
                    for c in range(PAIRS):
                        pe.transpose(X0[:, P + c * P:P + (c + 1) * P], qk[:, u, PAIRS + c, :], ident[:, :])
                    pe.wait_ge(act_g, t + 1)
                    pe.transpose(X0[:, 0:P], GT[:, :], ident[:, :])
                    for h in range(MH):
                        pe.matmul(T0[:, h * P:(h + 1) * P], selh[:, h, :], gbm[:, 2, :], start=True, stop=True)
                    for c in range(PAIRS):
                        ins = pe.matmul(T1[:, c * P:(c + 1) * P], selp[:, c, :], gbm[:, 3, :], start=True, stop=True)
                    ins.then_inc(pe_g, 1)
                    pe.wait_ge(dve_L0, t + 1)
                    scores(1, pe_s1)
                    pe.wait_ge(act_p0, t + 1)
                    pe.wait_ge(dve_darg, t + 1)
                    pe.wait_ge(dve_qg, t + 1)
                    probs_T(pe_pT0)
                if nxt:
                    wait(pe, ld_w2, 16)
                    pe.wait_ge(act_kvg, t + 2)
                    ins = conv_channels(range(CC - 1) if main else range(CC))
                if main:
                    pe.wait_ge(act_v, t + 1)
                    pe.wait_ge(act_pT0, t + 1)
                    pe.wait_ge(dve_pT0, t + 1)
                    wait(pe, dve_att, t)
                    values(0, pe_pv0)
                    pe.wait_ge(act_p1, t + 1)
                    probs_T(pe_pT1)
                    pe.wait_ge(dve_L1, t + 1)
                    for h in range(MH):
                        r, c = 64 * (h % 2), h // 2
                        st_ins = pe.matmul((S0, S1)[h % 2][:, c * P:(c + 1) * P], qk[r:r + 64, u, PAIRS + c, :],
                                           qk[r:r + 64, u, c, :], start=True, stop=True)
                    st_ins.then_inc(pe_st, 1)
                    if nxt:
                        ins = conv_channels([CC - 1])
                if nxt:
                    ins.then_inc(pe_cin, 1)
                if main:
                    pe.wait_ge(act_pT1, t + 1)
                    pe.wait_ge(dve_pT1, t + 1)
                    values(1, pe_o)
                    pe.wait_ge(dve_sd, t + 1)
                    pe.wait_ge(act_vm, t + 1)
                    wait(pe, dve_C, t)
                    for h in range(MH):
                        r, c = 64 * (h % 2), h // 2
                        o = (S0, S1)[h % 2][:, c * VE:(c + 1) * VE]
                        pe.matmul(o, sd[:, h, :], vm[:, u, h, :], start=True, stop=False)
                        ins = pe.matmul(o, qg[r:r + 64, c, :], Cst[r:r + 64, c, :], start=False, stop=True)
                    ins.then_inc(pe_h, 1)
                    pe.wait_ge(dve_kw, t + 1)
                    pe.wait_ge(dve_gT, t + 1)
                    for h in range(MH):
                        r, c = 64 * (h % 2), h // 2
                        ins = pe.matmul(X0[r:r + 64, c * VE:(c + 1) * VE], kw[:, h, :], vm[:, u, h, :],
                                        start=True, stop=True)
                    ins.then_inc(pe_u, 1)
                if nxt:
                    pe.wait_ge(act_q, t + 2)
                    project(J1, c_vm, MW, pe_vm, ld_w3, 16, t)
                if not main and nxt:
                    pe.wait_ge(dve_brow, 1)
                    pe.wait_ge(ld_bias, 16)
                    for b, bank in enumerate((S0, S1, O0, X0)):
                        ins = pe.matmul(bank[:, :], flip, bias[:, 2 * b:2 * b + 2, :].rearrange("p h k -> p (h k)"),
                                        start=True, stop=True)
                    ins.then_inc(pe_bias, 1)
                if main:
                    pe.wait_ge(dve_mix, t + 1)
                    transposes(mix, pe_mixT)
                    pe.wait_ge(act_mixT, t + 1)
                    pe.wait_ge(dve_mixT, t + 1)
                    pe.wait_ge(pool_wo, 1)
                    pe.wait_ge(act_cin, t + 1 + (1 if nxt else 0))
                    for half, (b, done) in enumerate(((J0, pe_y0), (J1, pe_y1))):
                        if half:
                            pe.wait_ge(act_vm, t + 1 + (1 if nxt else 0))
                            if not nxt:
                                positions(TILES - 1, 1)
                        for k in range(KC):
                            ins = pe.matmul(b[:, :], mixT[:, k, :], wo[:, k, half * HALF:(half + 1) * HALF],
                                            start=(k == 0), stop=(k == KC - 1))
                        ins.then_inc(done, 1)
                if nxt:
                    if main:
                        pe.wait_ge(dve_h0, t + 1)
                    else:
                        pe.wait_ge(act_cin, 1)
                    project(J0, c_om, MW, pe_om, ld_w4, 16, t)
                if main:
                    pe.wait_ge(dve_hn2, t + 1)
                    transposes(h2, pe_h2T)
                    pe.wait_ge(act_h2T, t + 1)
                    pe.wait_ge(dve_h2T, t + 1)
                    pe.wait_ge(dve_C, t + 1)
                    for k in range(KC):
                        ins = pe.matmul(X0[:, 0:NG + NE], h2T[:, k, :], wr[:, k, :], start=(k == 0),
                                        stop=(k == KC - 1))
                    ins.then_inc(pe_r, 1)
            tiles(pe, body)

            positions(1, 2)

            pe.wait_ge(dve_tab, 1)
            HF = FF // 2
            gu_hi, lo_a = (w[:, 0:2 * FC * PW].rearrange("p (g k n) -> p g k n", g=2, k=KC)
                            for w in (whi, wlo))
            dn_hi, lo_b = (w[:, 2 * FC * PW:].rearrange("p (c n) -> p c n", c=FC)
                            for w in (whi, wlo))

            def three(out_, ah, al, bh, bl, start, stop):
                pe.matmul(out_, ah, bh, start=start, stop=False)
                pe.matmul(out_, ah, bl, start=False, stop=False)
                return pe.matmul(out_, al, bh, start=False, stop=stop)

            def rows_T(t):
                pe.wait_ge(ld_g, 16 * (t + 1))
                wait(pe, dve_mx, 2 * t)
                transposes(xg, pe_mx)

            def hidden_T(t, half):
                pe.wait_ge(dve_mh, 2 * t + half + 1)
                if half == 0:
                    wait(pe, dve_hT, 2 * t)
                for c in range(2):
                    ins = pe.transpose((S0, X0)[half][:, c * P:(c + 1) * P],
                                       mh[:, half * HF + c * P:half * HF + (c + 1) * P], ident[:, :])
                ins.then_inc(pe_hT, 1)

            def tile(t, e):
                pe.wait_ge(dve_mx, 2 * t + 2)
                wait(pe, dve_mh, 2 * t)
                for half, bank in enumerate((J0, J1)):
                    cols = slice(half * HF, (half + 1) * HF)
                    for k in range(KC):
                        if half == 0 and k % 2 == 0:
                            for i in (k, k + 1):
                                pe.wait_ge(*lo_ready(e, i))
                        ins = three(bank[:, :], mxh[:, k, :], mxl[:, k, :], gu_hi[:, :, k, cols], lo_a[:, :, k, cols],
                                    k == 0, k == KC - 1)
                        if half == 1 and k % 2 == 1:
                            ins.then_inc(pe_gup, 1)
                        if half == 1 and k == KC // 2 - 1:
                            hidden_T(t, 0)
                    if half == 0:
                        ins.then_inc(pe_gup, 1)
                rows_T(t + 1)
                hidden_T(t, 1)
                wait(pe, act_y, t)
                wait(pe, dve_y, t)
                for c in range(FC):
                    if c % 2 == 0:
                        pe.wait_ge(dve_hT, 2 * t + c // 2 + 1)
                    pe.wait_ge(*lo_ready(e, 2 * FC + c))
                    for half, b in enumerate((S1, O0)):
                        cols = slice(half * HALF, (half + 1) * HALF)
                        ins = three(b[:, :], mhh[:, c, :], mhl[:, c, :], dn_hi[:, c, cols], lo_b[:, c, cols],
                                    c == 0, c == FC - 1)
                    ins.then_inc(pe_dnp, 1)

            def expert(e):
                first = pe.value_load(tabi[0:1, bass.ds(e + FIRST, 1)], min_val=0, max_val=MAXT - 1)
                last = pe.value_load(tabi[0:1, bass.ds(e + LAST, 1)], min_val=0, max_val=MAXT - 1)
                with pe.Fori(first, last + 1) as t:
                    tile(t, e)

            rows_T(0)
            with pe.Fori(0, NE) as e:
                expert(e)

        @block.vector
        def _(dve):
            chain = Chain(dve, dve_chain)
            dve.wait_ge(pool_const, 6)
            dve.wait_ge(pe_brow, 1)
            dve.tensor_copy(brow[:, P:2 * P], X0[0:HEADS, 0:P]).then_inc(dve_brow, 1)
            dve.wait_ge(ld_gn, 16)
            chain(dve.tensor_scalar(gmix[:, :], gmix[:, :], float(D) ** 0.5, None, ALU.mult))

            class Space:
                def __init__(self, bufs):
                    self.bufs, self.i, self.at = bufs, 0, 0

                def __call__(self, n):
                    if self.at + n > self.bufs[self.i].shape[1]:
                        self.i, self.at = self.i + 1, 0
                    self.at += n
                    return self.bufs[self.i][:, self.at - n:self.at]

            new = Space([lg[:, :, :].rearrange("p a b -> p (a b)"), hnT[:, :, :].rearrange("p a b -> p (a b)")])

            def tt(out_, a, b, op):
                chain(dve.tensor_tensor(out_, a, b, op))

            def route(a, b, n):
                T_ = b - a

                def first_max(vals, w):
                    mx, idx = new(T_), new(T_)
                    chain(dve.tensor_reduce(mx, vals, AX, ALU.max))
                    oh = new(T_ * w).rearrange("p (t n) -> p t n", n=w)
                    bc = lambda v: v.unsqueeze(2).to_broadcast([P, T_, w])
                    tt(oh, vals, bc(mx), ALU.is_equal)
                    io, iom = (f[:, 0:w].unsqueeze(1).to_broadcast([P, T_, w]) for f in (iota_f[:, :], iota_m[:, :]))
                    chain(dve.scalar_tensor_tensor(oh, oh, -1.0e4, io, ALU.mult, ALU.add))
                    chain(dve.tensor_reduce(idx, oh, AX, ALU.min))
                    tt(oh, iom, bc(idx), ALU.is_equal)
                    return oh, mx

                if n == 1:
                    chain(dve.tensor_copy(iota_f[:, :], ints[:, 0:NI]))
                    chain(dve.tensor_scalar(iota_m[:, :], iota_f[:, 0:NG], -1.0e4, None, ALU.add))
                    chain(dve.tensor_scalar(strict, tri[:, :], -0.5, None, ALU.is_gt))
                    dve.tensor_tensor(strict, strict, ident[:, :], ALU.subtract)
                    dve.memset(onesm, 1.0)
                    chain(dve.memset(off_e[:, :], 0.0))
                gl = rl[:, a:b, 0:NG]
                ohg, gmx = first_max(gl, NG)
                tt(route_e[:, 0:T_ * NG].rearrange("p (t n) -> p t n", n=NG), gl,
                   gmx.unsqueeze(2).to_broadcast([P, T_, NG]), ALU.subtract)
                el = rl[:, a:b, NG:].rearrange("p t (g e) -> p t g e", g=NG)
                prod = new(T_ * NE).rearrange("p (t g e) -> p t g e", g=NG, e=EPG)
                tt(prod, el, ohg.unsqueeze(3).to_broadcast([P, T_, NG, EPG]), ALU.mult)
                ein = new(T_ * EPG).rearrange("p (t e) -> p t e", e=EPG)
                chain(dve.tensor_reduce(ein, prod.rearrange("p t g e -> p t e g"), AX, ALU.add))
                oh1, m1 = first_max(ein, EPG)
                e2 = new(T_ * EPG).rearrange("p (t e) -> p t e", e=EPG)
                chain(dve.scalar_tensor_tensor(e2, oh1, -3.0e38, ein, ALU.mult, ALU.add))
                oh2, m2 = first_max(e2, EPG)
                dve.tensor_tensor(route_e[:, T_ * NG:T_ * (NG + 1)], m2, m1, ALU.subtract).then_inc(dve_rt, 1)
                full = []
                for oh in (oh1, oh2):
                    full.append(new(T_ * NE))
                    tt(full[-1].rearrange("p (t g e) -> p t g e", g=NG, e=EPG),
                       ohg.unsqueeze(3).to_broadcast([P, T_, NG, EPG]),
                       oh.unsqueeze(2).to_broadcast([P, T_, NG, EPG]), ALU.mult)
                dve.tensor_tensor(Mall[:, 0:T_ * NE], full[0], full[1], ALU.add).then_inc(dve_M, 1)
                dve.wait_ge(act_rt, n)
                gs, wt = new(T_), new(2 * T_).rearrange("p (t c) -> p t c", c=2)
                chain(dve.tensor_reduce(gs, route_e[:, 0:T_ * NG].rearrange("p (t n) -> p t n", n=NG), AX, ALU.add))
                e21, dn = route_e[:, T_ * NG:T_ * (NG + 1)], new(T_)
                chain(dve.scalar_tensor_tensor(dn, e21, 1.0, gs, ALU.add, ALU.mult))
                chain(dve.reciprocal(dn, dn))
                dve.tensor_copy(wt[:, :, 0], dn)
                tt(wt[:, :, 1], dn, e21, ALU.mult)
                dve.tensor_copy(pay[:, a:b, :, 1].bitcast(F32), wt)
                for c in range(2):
                    ins = dve.tensor_copy(pay[:, a:b, c, 0], ints[:, NI + a:NI + b])
                chain(ins)
                dve.wait_ge(pe_pos, n)
                MC = T_ * NE
                pos, dst = new(MC), new(2 * T_).rearrange("p (t c) -> p t c", c=2)
                for t in range(T_):
                    tt(off_e[:, a + t + 1, :], off_e[:, a + t, :], S1[:, t * NE:(t + 1) * NE], ALU.add)
                p3 = pos.rearrange("p (t e) -> p t e", e=NE)
                tt(p3, S0[:, 0:MC].rearrange("p (t e) -> p t e", e=NE), off_e[:, a:b, :], ALU.add)
                chain(dve.scalar_tensor_tensor(p3, iota_f[:, 0:NE].unsqueeze(1).to_broadcast([P, T_, NE]), float(S), p3,
                                               ALU.mult, ALU.add))
                for c in range(2):
                    tt(full[c], full[c], pos, ALU.mult)
                    chain(dve.tensor_reduce(dst[:, :, c], full[c].rearrange("p (t e) -> p t e", e=NE), AX, ALU.add))
                q = new(2 * T_).rearrange("p (t c) -> p t c", c=2)
                chain(dve.tensor_scalar(q, dst, 1.0 / P, -0.5 + 0.5 / P, ALU.mult, ALU.add))
                chain(dve.tensor_scalar(q, q, 1.5 * 2.0 ** 23, None, ALU.add))
                dve.tensor_scalar(dst, dst, float(TCOLS), None, ALU.mult)
                chain(dve.tensor_scalar(q, q, -1.5 * 2.0 ** 23, None, ALU.add))
                chain(dve.scalar_tensor_tensor(dst, q, -float(P * TCOLS - 1), dst, ALU.mult, ALU.add))
                dve.tensor_copy(desti[:, a:b, :], dst).then_inc(dve_pay, 1)

            def logits(t, g, s_done, l_done, nm_done):
                hs = slice(g * G, g * G + G)
                dve.wait_ge(s_done, t + 1)
                for b, S_ in enumerate((S0, S1)):
                    sv = S_[:, :].rearrange("p (j w k) -> p j w k", j=2, w=2)
                    lv = lg[:, 2 * b:2 * b + 2, :].rearrange("p j (w k) -> p j w k", w=2)
                    bv = bias[:, g * G + 2 * b:g * G + 2 * b + 2, :].rearrange("p j (w k) -> p j w k", w=2)
                    dve.scalar_tensor_tensor(lv[:, :, 0, :], sv[:, :, 0, :], pbias[:, :], bv[:, :, 0, :],
                                             ALU.add, ALU.add)
                    ins = dve.tensor_tensor(lv[:, :, 1, :], sv[:, :, 1, :], bv[:, :, 1, :], ALU.add)
                ins.then_inc(l_done, 1)
                dve.wait_ge(l_done, t + 1)
                chain(dve.tensor_reduce(amx[:, hs], lg[:, :, :], AX, ALU.max))
                chain(dve.tensor_tensor(amx[:, hs], amx[:, hs], sink[:, hs], ALU.max))
                chain(dve.tensor_scalar(anm[:, hs], amx[:, hs], -1.0, None, ALU.mult))
                dve.tensor_tensor(aes[:, hs], sink[:, hs], anm[:, hs], ALU.add).then_inc(nm_done, 1)

            def body(t, u, main, nxt, ahead):
                v = 1 - u
                if nxt:
                    dve.wait_ge(pe_hnT, t + 2)
                    wait(dve, pe_om, t + 1)
                    dve.tensor_copy(hnT[:, 4:8, :].rearrange("p a b -> p (a b)"), T1[:, :]).then_inc(dve_hnT, 1)
                if nxt and not main:
                    dve.wait_ge(ld_c, 16 * (10 + TAPS))
                    dve.tensor_scalar(gffn[:, :], gffn[:, :], float(D) ** 0.5, None, ALU.mult)
                    dve.tensor_scalar(gml[:, :], gml[:, :], float(DV) ** 0.5, None, ALU.mult)
                    dve.tensor_scalar(gk[:, :], gk[:, :], float(HD) ** 0.5, None, ALU.mult).then_inc(dve_const, 1)
                    dve.wait_ge(dve_const, 1)
                if main:
                    dve.wait_ge(pe_qkT, t + 1)
                    wait(dve, pe_s1, t)
                    dve.tensor_copy(kTw[:, u, :], S1[:, 0:P])
                    dve.tensor_scalar(giz[:, :], S1[0:MH, P:2 * P], gb[0:MH, :], None, ALU.add)
                    ins = dve.tensor_scalar(gfz[32:32 + MH, 2, :], S1[32:32 + MH, P:2 * P], gb[32:32 + MH, :], None,
                                            ALU.add)
                    ins.then_inc(dve_kg, 1)
                    dve.wait_ge(dve_kg, t + 1)
                    dve.scalar_tensor_tensor(gfz[32:32 + MH, 0, :], gfz[32:32 + MH, 2, :], -1.0,
                                             gfz[32:32 + MH, 2, :], ALU.mult, ALU.max).then_inc(dve_az, 1)
                    dve.wait_ge(act_ln, t + 1)
                    chain(dve.tensor_scalar(gfz[32:32 + MH, 2, :], gfz[32:32 + MH, 2, :], 0.0, None, ALU.min))
                    chain(dve.tensor_tensor(glf[:, :], gfz[32:32 + MH, 2, :], gfz[32:32 + MH, 1, :], ALU.subtract))
                    dve.tensor_tensor_scan(gbm[:, 0, :], ones_s[:, :], glf[:, :], 0.0, ALU.mult, ALU.add)
                    chain(dve.tensor_tensor_scan(gbm[:, 1, :], glf[:, :], giz[:, :], mprev[:, :], ALU.add, ALU.max))
                    wait(dve, pe_g, t)
                    dve.tensor_tensor(gbm[:, 2, :], gbm[:, 0, :], gbm[:, 1, :], ALU.subtract)
                    dve.tensor_tensor(GT[0:MH, :], giz[:, :], gbm[:, 0, :], ALU.subtract).then_inc(dve_ca, 1)
                    wait(dve, pe_pT1, t)
                    logits(t, 0, pe_s0, dve_L0, dve_nm0)
                    dve.wait_ge(pe_g, t + 1)
                    wait(dve, pe_h, t)
                    dve.tensor_tensor(darg[:, :, :], T0[:, :].rearrange("p (h s) -> p h s", h=MH),
                                      tri[:, :].unsqueeze(1).to_broadcast([P, MH, P]), ALU.add).then_inc(dve_darg, 1)
                    dve.wait_ge(act_qk, t + 1)
                    dve.tensor_tensor(qg[:, :, :], qk[:, u, 0:PAIRS, :],
                                      T1[:, 0:PAIRS * P].rearrange("p (c s) -> p c s", c=PAIRS), ALU.mult)
                    dve.tensor_copy(dec[:, :], T1[:, P - 1:PAIRS * P:P]).then_inc(dve_qg, 1)
                    dve.tensor_copy(gT[:, :], X0[:, 0:68]).then_inc(dve_gT, 1)
                    dve.wait_ge(act_g, t + 1)
                    dve.tensor_copy(mprev[:, :], gbm[:, 1, P - 1:P])
                    dve.wait_ge(pe_pT0, t + 1)
                    dve.tensor_copy(PT[:, 2:4, :, :].rearrange("p a b c -> p (a b c)"), T1[:, :]).then_inc(dve_pT0, 1)
                    logits(t, 1, pe_s1, dve_L1, dve_nm1)
                    dve.memset(pbias[:, :], 0.0)
                    dve.wait_ge(dve_gT, t + 1)
                    dve.scalar_tensor_tensor(
                        kw[:, :, :], X0[:, P:P + MH * DQK].rearrange("p (h d) -> p h d", h=MH), float(DQK) ** -0.5,
                        gT[:, 32:32 + MH].unsqueeze(2).to_broadcast([P, MH, DQK]), ALU.mult,
                        ALU.mult).then_inc(dve_kw, 1)
                if nxt:
                    dve.wait_ge(act_kvg, t + 2)
                    dve.wait_ge(act_q, t + 2)
                    dve.tensor_reduce(ssqk[:, :], sqk[:, :].rearrange("p (h d) -> p h d", d=HD), AX,
                                      ALU.add).then_inc(dve_sqk, 1)
                    dve.tensor_copy(gt[:, 0:MH], kvg[:, 2 * KVW:2 * KVW + MH])
                    dve.tensor_copy(gt[:, 32:32 + MH], kvg[:, 2 * KVW + MH:KVG])
                    q8 = q_sb[:, :].rearrange("p (h d) -> p h d", d=HD)
                    k2 = kvg[:, 0:KVW].rearrange("p (g d) -> p g d", g=KVH)
                    dve.tensor_tensor(q8, q8, gq[:, :].unsqueeze(1).to_broadcast([P, HEADS, HD]), ALU.mult)
                    chain(dve.tensor_tensor(k2, k2, gk[:, :].unsqueeze(1).to_broadcast([P, KVH, HD]), ALU.mult))
                    dve.wait_ge(pool_rqk, t + 2)
                    qv = qn[:, :, :, :].rearrange("p j g d -> p g j d")
                    for g in range(KVH):
                        dve.tensor_tensor(qv[:, g, :, :],
                                          q_sb[:, g * G * HD:(g + 1) * G * HD].rearrange("p (j d) -> p j d", j=G),
                                          rqk[:, KVH + g * G:KVH + (g + 1) * G].unsqueeze(2).to_broadcast([P, G, HD]),
                                          ALU.mult)
                    dve.tensor_tensor(kn[:, :, :], k2, rqk[:, 0:KVH].unsqueeze(2).to_broadcast([P, KVH, HD]),
                                      ALU.mult).then_inc(dve_qkn, 1)
                if main:
                    dve.wait_ge(pe_pT1, t + 1)
                    dve.tensor_copy(PT[:, 2:4, :, :].rearrange("p a b c -> p (a b c)"), T1[:, :]).then_inc(dve_pT1, 1)
                    dve.wait_ge(pe_st, t + 1)
                    dve.wait_ge(act_D, t + 1)
                    for b, S_ in enumerate((S0, S1)):
                        ins = dve.scalar_tensor_tensor(
                            sd[:, b::2, :], S_[:, 0:PAIRS * P].rearrange("p (c s) -> p c s", c=PAIRS),
                            float(DQK) ** -0.5, dmat[:, b::2, :], ALU.mult, ALU.mult)
                    ins.then_inc(dve_sd, 1)
                    dve.wait_ge(pe_o, t + 1)
                    dve.wait_ge(act_p1, t + 1)
                    chain(dve.tensor_tensor(arc[:, :], asum[:, :], aes[:, :], ALU.add))
                    chain(dve.reciprocal(arc[:, :], arc[:, :]))
                    dve.tensor_tensor(mix[:, 0:AW].rearrange("p (h d) -> p h d", h=HEADS),
                                      O0[:, :].rearrange("p (h d) -> p h d", h=HEADS),
                                      arc[:, :].unsqueeze(2).to_broadcast([P, HEADS, HD]), ALU.mult)\
                        .then_inc(dve_att, 1)
                    dve.wait_ge(pe_h, t + 1)
                    for b, S_ in enumerate((S0, S1)):
                        hv = S_[:, 0:PAIRS * VE].rearrange("p (c e) -> p c e", c=PAIRS)
                        ins = dve.tensor_copy(hrr[:, b::2], hv[:, :, DV])
                    ins.then_inc(dve_den, 1)
                    dve.wait_ge(dve_den, t + 1)
                    chain(dve.tensor_tensor(hden[:, :], hrr[:, :], gT[:, 64:64 + MH], ALU.max))
                    chain(dve.scalar_tensor_tensor(hden[:, :], hrr[:, :], -1.0, hden[:, :], ALU.mult, ALU.max))
                    chain(dve.reciprocal(hden[:, :], hden[:, :]))
                    chain(dve.tensor_tensor(hd2[:, :], hden[:, :], hden[:, :], ALU.mult))
                    dve.wait_ge(act_ssn, t + 1)
                    dve.tensor_tensor(hss[:, :], hsn[:, :], hd2[:, :], ALU.mult).then_inc(dve_hss, 1)
                    dve.wait_ge(pe_u, t + 1)
                    for c in range(PAIRS):
                        ins = dve.scalar_tensor_tensor(Cst[:, c, :], Cst[:, c, :], dec[:, c:c + 1],
                                                       X0[:, c * VE:(c + 1) * VE], ALU.mult, ALU.add)
                    ins.then_inc(dve_C, 1)
                    dve.wait_ge(pool_rhm, t + 1)
                    dve.wait_ge(act_om, t + 1)
                    chain(dve.tensor_tensor(hrr[:, :], hden[:, :], hrs[:, :], ALU.mult))
                    for h in range(MH):
                        c = h // 2
                        ins = dve.scalar_tensor_tensor(
                            mix[:, AW + h * DV:AW + (h + 1) * DV], (S0, S1)[h % 2][:, c * VE:c * VE + DV],
                            hrr[:, h:h + 1], osg[:, h * DV:(h + 1) * DV], ALU.mult, ALU.mult)
                    ins.then_inc(dve_mix, 1)
                    dve.wait_ge(pe_mixT, t + 1)
                    wait(dve, pe_r, t)
                    dve.tensor_copy(mixT[:, 4:8, :].rearrange("p a b -> p (a b)"), T1[:, :]).then_inc(dve_mixT, 1)
                if main and not nxt:
                    dve.wait_ge(dve_rl, TILES - 1)
                    route(0, TILES - 1, 1)
                if nxt:
                    dve.wait_ge(act_cin, t + 2)
                    wait(dve, act_qk, t + 1)
                    for c in range(CC):
                        ins = dve.tensor_scalar(cy[:, c, :], cin[:, c, 0:P], cw[:, 0, c:c + 1], None, ALU.mult)
                    chain(ins)
                    for k in range(1, TAPS):
                        for c in range(CC):
                            ins = dve.scalar_tensor_tensor(cy[:, c, :], cin[:, c, k:k + P], cw[:, k, c:c + 1],
                                                           cy[:, c, :], ALU.mult, ALU.add)
                        chain(ins)
                    dve.tensor_copy(cin[:, :, 0:TAPS - 1], cin[:, :, P:P + TAPS - 1]).then_inc(dve_cy, 1)
                if nxt and not main:
                    dve.wait_ge(pe_bias, 1)
                    for b, bank in enumerate((S0, S1, O0, X0)):
                        ins = dve.tensor_copy(bias[:, 2 * b:2 * b + 2, :].rearrange("p h k -> p (h k)"), bank[:, :])
                    ins.then_inc(dve_bias, 1)
                if main:
                    dve.wait_ge(LDX[u], 8 * t + (16 - 8 * u))
                    dve.wait_ge(pe_y0, t + 1)
                    dve.tensor_tensor(xin[:, u, 0:HALF], J0[:, :], xin[:, u, 0:HALF], ALU.add).then_inc(dve_h0, 1)
                if ahead:
                    dve.wait_ge(pool_rx, t + 3)
                    dve.scalar_tensor_tensor(hn[:, :], hn[:, :], rsx[:, :], gmix[:, :], ALU.mult,
                                             ALU.mult).then_inc(dve_hn, 1)
                if main:
                    dve.wait_ge(pe_y1, t + 1)
                    dve.tensor_tensor(xin[:, u, HALF:], J1[:, :], xin[:, u, HALF:], ALU.add).then_inc(dve_h, 1)
                    dve.wait_ge(pool_rh, t + 1)
                    dve.wait_ge(dve_h, t + 1)
                    wait(dve, st_h2, 16 * t)
                    dve.wait_ge(st_zero, 64)
                    hv = h2[:, :].rearrange("q (k p) -> q p k", k=KC)
                    dve.scalar_tensor_tensor(hv, xin[:, u, :].rearrange("q (p k) -> q p k", k=KC), rsh[:, :],
                                             gffn[:, :].rearrange("q (p k) -> q p k", k=KC), ALU.mult,
                                             ALU.mult).then_inc(dve_hn2, 1)
                    dve.wait_ge(pe_h2T, t + 1)
                    dve.tensor_copy(h2T[:, 4:8, :].rearrange("p a b -> p (a b)"), T1[:, :]).then_inc(dve_h2T, 1)
                    dve.wait_ge(pe_r, t + 1)
                    ti = slice(t, t + 1) if isinstance(t, int) else bass.ds(t, 1)
                    dve.tensor_tensor(rl[:, ti, :].rearrange("p t n -> p (t n)"), X0[:, 0:NG + NE], rbias[:, :],
                                      ALU.add).then_inc(dve_rl, 1)
            tiles(dve, body, chain, 21)

            dve.wait_ge(dve_rl, TILES)
            route(TILES - 1, TILES, 2)
            one = slice(0, 1)
            T_ = TILES
            cnt = off_e[one, T_, :]
            cmp = new(NE * (T_ - 1))[one, :].rearrange("p (e k) -> p e k", e=NE)
            thr = new(T_ - 1)[one, :]
            chain(dve.tensor_scalar(thr, iota_f[one, 1:T_], float(P), None, ALU.mult))
            tt(cmp, cnt.unsqueeze(2).to_broadcast([1, NE, T_ - 1]), thr.unsqueeze(1).to_broadcast([1, NE, T_ - 1]),
               ALU.is_gt)
            te, cum = new(NE)[one, :], new(NE)[one, :]
            chain(dve.tensor_reduce(te, cmp, AX, ALU.add))
            chain(dve.tensor_scalar(te, te, 1.0, None, ALU.add))
            on = new(NE)[one, :]
            chain(dve.memset(on, 1.0))
            chain(dve.tensor_tensor_scan(cum, on, te, 0.0, ALU.mult, ALU.add))
            NTL = NI
            big = new(NTL * NE)[one, :].rearrange("p (t e) -> p t e", e=NE)
            et, fs = new(NTL)[one, :], new(NTL)[one, :]
            tt(big, cum.unsqueeze(1).to_broadcast([1, NTL, NE]),
               iota_f[one, 0:NTL].unsqueeze(2).to_broadcast([1, NTL, NE]), ALU.is_le)
            chain(dve.tensor_reduce(et, big, AX, ALU.add))
            tt(big, big, te.unsqueeze(1).to_broadcast([1, NTL, NE]), ALU.mult)
            chain(dve.tensor_reduce(fs, big, AX, ALU.add))
            chain(dve.tensor_scalar(et, et, float(S // P), None, ALU.mult))
            tt(et, et, iota_f[one, 0:NTL], ALU.add)
            tt(et, et, fs, ALU.subtract)
            chain(dve.tensor_scalar(et, et, float(TCOLS - 1), None, ALU.min))
            chain(dve.tensor_copy(tabi[:, ROWS:ROWS + NTL], et))
            chain(dve.tensor_tensor(tabi[:, FIRST:FIRST + NE], cum, te, ALU.subtract))
            dve.tensor_scalar(tabi[:, LAST:LAST + NE], cum, -1.0, None, ALU.add).then_inc(dve_tab, 1)

            sg = cy[:, :, :].rearrange("p a b -> p (a b)")
            HF = FF // 2

            def hidden(t, half):
                cols = slice(half * HF, (half + 1) * HF)
                dve.wait_ge(act_silu, 2 * t + half + 1)
                wait(dve, pe_hT, 2 * t)
                dve.tensor_tensor(mh[:, cols], sg[:, cols], (J0, J1)[half][:, HF:], ALU.mult).then_inc(dve_mh, 1)

            def rows_lo(t):
                for b in range(2):
                    dve.wait_ge(act_mx, 2 * t + b + 1)
                    at = slice(4 * b, 4 * b + 4)
                    dve.tensor_tensor(mxl[:, at, :].rearrange("p a b -> p (a b)"), TB[b][:, :],
                                      mxh[:, at, :].bitcast(F32).rearrange("p a b -> p (a b)"), ALU.subtract).then_inc(dve_mx, 1)

            def hidden_lo(t, half):
                dve.wait_ge(act_hT, 2 * t + half + 1)
                at = slice(2 * half, 2 * half + 2)
                dve.tensor_tensor(mhl[:, at, :].rearrange("p a b -> p (a b)"), (S0, X0)[half][:, 0:HF],
                                  mhh[:, at, :].bitcast(F32).rearrange("p a b -> p (a b)"), ALU.subtract).then_inc(dve_hT, 1)

            def weigh(t):
                dve.wait_ge(pe_dnp, FC * (t + 1))
                dve.wait_ge(dve_wt, t + 1)
                dve.wait_ge(st_y, 16 * t)
                dve.tensor_scalar(yb[:, HALF:], O0[:, :], wt_t[:, 0:1], None, ALU.mult).then_inc(dve_y, 1)

            def split_lo(e, i):
                dve.wait_ge(act_hi, e * PIECES + (i + 1))
                at = slice(order(i) * PW, order(i) * PW + PW)
                dve.tensor_tensor(wlo[:, at], slot[i], whi[:, at].bitcast(F32),
                                  ALU.subtract).then_inc(lo_ready(e, i)[0], 1)

            def tile(t, split):
                wait(dve, act_y, t)
                wait(dve, dve_y, t)
                col = dve.value_load(tabi[0:1, bass.ds(t + ROWS, 1)], min_val=0, max_val=TCOLS - 1)
                dve.tensor_copy(wt_t[:, 0:1], rows[:, bass.ds(col, 1), 1:2].rearrange("p a c -> p (a c)")
                                .bitcast(F32)).then_inc(dve_wt, 1)
                hidden(t, 0)
                split(0, 1)
                hidden_lo(t, 0)
                split(1, 2)
                hidden(t, 1)
                hidden_lo(t, 1)
                rows_lo(t + 1)
                split(2, VP)
                weigh(t)

            def inner_tiles(e):
                first = dve.value_load(tabi[0:1, FIRST + e:FIRST + e + 1] if isinstance(e, int) else
                                       tabi[0:1, bass.ds(e + FIRST, 1)], min_val=0, max_val=MAXT - 1)
                last = dve.value_load(tabi[0:1, LAST + e:LAST + e + 1] if isinstance(e, int) else
                                      tabi[0:1, bass.ds(e + LAST, 1)], min_val=0, max_val=MAXT - 1)
                with dve.If(first < last):
                    with dve.Fori(first, last) as t:
                        tile(t, lambda a, b: None)
                return last

            for i in range(VP):
                split_lo(0, i)
            rows_lo(0)
            for i in range(VP, PIECES):
                split_lo(0, i)
            dve.wait_ge(ld_rows, 16)
            with dve.Fori(0, NE - 1) as e:
                last = inner_tiles(e)

                def split(a, b):
                    for i in range(a, b):
                        split_lo(e + 1, i)
                tile(last, split)
            tile(inner_tiles(NE - 1), lambda a, b: None)


_INS = ["x", "rel_bias", "norm_mix_g", "w_in", "q_norm_g", "k_norm_g", "attn_sink", "conv_w", "conv_b", "gate_b",
        "mlstm_norm_g", "w_out", "norm_ffn_g", "w_router_group", "b_router_group", "w_router_expert",
        "b_router_expert", "w_gate", "w_up", "w_down"]


def bucket_one_hot(buckets, window):
    import math
    import numpy as np
    exact = buckets // 2
    m = np.zeros((buckets, window), np.float32)
    for dist in range(window):
        b = dist if dist < exact else min(buckets - 1, exact + int(
            math.log(dist / exact) / math.log(window / exact) * (buckets - exact)))
        m[b, window - 1 - dist] = 1.0
    return m


def kernel(**inputs):
    import numpy as _np
    import concourse.bacc as _bacc
    from concourse import mybir as _mybir
    from concourse.bass_utils import run_bass_kernel_spmd as _run

    nc = _bacc.Bacc("TRN2", target_bir_lowering=False, num_devices=1)
    arrays, args = {}, []
    for name in _INS:
        a = _np.ascontiguousarray(inputs[name])
        arrays[f"in_{name}_dram"] = a
        args.append(nc.dram_tensor(f"in_{name}_dram", a.shape, _mybir.dt.from_np(a.dtype), kind="ExternalInput").ap())
    a = bucket_one_hot(inputs["rel_bias"].shape[0], 128)
    arrays["bucket_dram"] = a
    args.append(nc.dram_tensor("bucket_dram", a.shape, _mybir.dt.float32, kind="ExternalInput").ap())
    _, seq, width = inputs["x"].shape
    args.append(nc.dram_tensor("out_0_dram", (seq + 128, width), _mybir.dt.float32, kind="ExternalOutput").ap())
    hymba_layer_program(nc, *args)
    r = _run(nc, [arrays], core_ids=[0])
    return r.results[0]["out_0_dram"][:seq].reshape(1, seq, width)
```

```python
import concourse.bass as bass
from concourse import mybir
from contextlib import ExitStack


def hymba_layer_program(nc, x, rel_bias, norm_mix_g, w_in, q_norm_g, k_norm_g, attn_sink, conv_w, conv_b,
                        gate_b, mlstm_norm_g, w_out, norm_ffn_g, w_router_group, b_router_group,
                        w_router_expert, b_router_expert, w_gate, w_up, w_down, bucket_onehot, out):
    F32 = mybir.dt.float32
    I32 = mybir.dt.int32
    U32 = mybir.dt.uint32
    F32R = mybir.dt.float32r
    ALU = mybir.AluOpType
    ACT = mybir.ActivationFunctionType
    AX = mybir.AxisListType.X

    P = 128
    S, D = x.shape[1], x.shape[2]
    TILES = S // P
    KC = D // P
    HEADS, HD = attn_sink.shape[1], q_norm_g.shape[1]
    KVH = 2
    G = HEADS // KVH
    AW = HEADS * HD
    KVW = KVH * HD
    MH = gate_b.shape[1] // 2
    CH = conv_w.shape[2]
    TAPS = conv_w.shape[1]
    CC = CH // P
    DQK = CH // 2 // MH
    MW = mlstm_norm_g.shape[1]
    DV = MW // MH
    VE = DV + 1
    PAIRS = MH // 2
    NG = w_router_group.shape[2]
    NE = w_router_expert.shape[2]
    EPG = NE // NG
    FF = w_gate.shape[3]
    FC = FF // P
    HALF = D // 2
    EPS = 1e-6
    NEG = -1.0e30
    NBK = rel_bias.shape[0]
    RLEN = 3 * P
    MAXT = 2 * S // P + NE
    TCOLS = NE * S // P + 2
    OUTR = S + P

    x2 = x.rearrange("b s d -> (b s) d")
    ctx = ExitStack()
    with ctx:
        def sb(name, shape, dt=F32):
            return ctx.enter_context(nc.sbuf_tensor(name, shape, dt))

        def pb(name):
            return ctx.enter_context(nc.psum_tensor(name, [P, 512], F32))

        def sems(names):
            return [ctx.enter_context(nc.semaphore(n)) for n in names.split()]

        bias_rows = nc.dram_tensor("bias_rows", (HEADS, RLEN), F32, kind="Internal").ap()
        mix_rows = nc.dram_tensor("mix_rows", (S, D), F32, kind="Internal").ap()
        ffn_in = nc.dram_tensor("ffn_in", (OUTR, D), F32, kind="Internal").ap()
        table = nc.dram_tensor("table", (P * TCOLS, 2), I32, kind="Internal").ap()
        table_v = table.rearrange("(p a) c -> p a c", p=P)

        KVG = 2 * KVW + 2 * MH
        NIN = w_in.shape[2]
        NRES = KVG + CH
        PIECES, PW = 3 * FC, 2 * FF
        VP = 2 * FC
        OUTP = D // P
        whi, wlo = sb("w_high", [P, PIECES * PW], F32R), sb("w_low", [P, PIECES * PW], F32R)
        mxh, mxl = sb("rows_high", [P, KC, P], F32R), sb("rows_low", [P, KC, P], F32R)
        MX = [(mxh, mxl), tuple(w[:, OUTP * PW:(OUTP + 1) * PW].rearrange("p (k n) -> p k n", k=KC)
                                for w in (whi, wlo))]
        hnT = sb("hnT", [P, KC, P])
        h2T = hnT
        wres = sb("w_res", [P, KC * NRES])
        wi = wres[:, :].rearrange("p (k n) -> p k n", k=KC)
        overlaid = ExitStack()

        def sb1(name, shape):
            return overlaid.enter_context(nc.sbuf_tensor(name, shape, F32))

        qT = sb1("qT", [P, G, P])
        osgT = sb1("osg", [P, FC, P])
        osg = osgT[:, :, :].rearrange("p a b -> p (a b)")
        qn = sb1("qn", [P, G, KVH, HD])
        kn = sb1("kn", [P, KVH, HD])
        gt = sb1("gt", [P, 64])
        kTw = sb1("kTw", [P, 2, P])
        vw = sb1("vw", [P, 2, KVW])
        overlaid.close()
        mhh, mhl = sb("hidden_high", [P, FC, P], F32R), sb("hidden_low", [P, FC, P], F32R)
        slot_b = sb("slot_b", [P, G * P + KVW + 64 + 2 * P + 2 * KVW])
        wr = sb("wr", [P, KC, NG + NE])
        ident = sb("ident", [P, P])
        tri = sb("tri", [P, P])
        selh = sb("selh", [MH, MH, P])
        selp = sb("selp", [MH, PAIRS, P])
        gmix = sb("gmix", [P, D])
        gffn = gmix
        gq = sb("gq", [P, HD])
        gk = sb("gk", [P, HD])
        sink = sb("sink", [P, HEADS])
        cw = sb("cw", [P, TAPS, CC])
        cb = sb("cb", [P, CC])
        gb = sb("gb", [64, 1])
        gml = sb("gml", [P, MW // P])
        bias = sb("bias", [P, HEADS, 2 * P])
        rbt = sb("rbt", [NBK, HEADS + P])
        rbias = sb("rbias", [P, NG + NE])
        mhalf = sb("mhalf", [P, 16])
        eps_d, eps_hd, eps_dv = (sb(f"eps_{n}", [P, 16]) for n in ("d", "hd", "dv"))
        tick = sb("tick", [1, 32])
        ones_s = sb("ones_s", [MH, P])
        warm = sb("warm", [1, 2])
        xin = bias[:, :, :].rearrange("p h k -> p (h k)").rearrange("p (u d) -> p u d", u=2)
        ssx = sb("ssx", [P, 1])
        rsx = sb("rsx", [P, 1])
        hn = sb("hn", [P, D])
        kvg = sb("kvg", [P, KVG])
        q_sb = sb("q_sb", [P, AW])
        sqk = sb("sqk", [P, KVW + AW])
        ssqk = sb("ssqk", [P, KVH + HEADS])
        rqk = sb("rqk", [P, KVH + HEADS])
        lg = sb("lg", [P, G, 2 * P])
        pr = lg
        PT = sb("PT", [P, G, 2, P])
        junk = PT[:, :, :, :].rearrange("p a b c -> p (a b c)")
        amx = sb("amx", [P, HEADS])
        anm = sb("anm", [P, HEADS])
        aes = sb("aes", [P, HEADS])
        asum = sb("asum", [P, HEADS])
        arc = sb("arc", [P, HEADS])
        pbias = sb("pbias", [P, 1])
        cin = sb("cin", [P, CC, TAPS - 1 + P])
        cy = sb("cy", [P, CC, P])
        qk = sb("qk", [P, CC, P])
        vm = sb("vm", [P, MH, VE])
        giz = sb("giz", [MH, P])
        gfz = sb("gfz", [64, 3, P])
        glf = sb("glf", [MH, P])
        gbm = sb("gbm", [MH, 4, P])
        mprev = sb("mprev", [MH, 1])
        GT = sb("GT", [P, P])
        gT = sb("gT", [P, 68])
        darg = sb("darg", [P, MH, P])
        flip = darg[:, 0, :]
        dmat = sd = darg
        qg = sb("qg", [P, PAIRS, P])
        dec = sb("dec", [P, PAIRS])
        kw = sb("kw", [P, MH, DQK])
        Cst = sb("Cst", [P, PAIRS, VE])
        hden, hd2, hrr, hsn = (sb(f"h_{n}", [P, MH]) for n in ("den", "den_sq", "scale", "num_sq"))
        hss = sb("hss", [P, MH])
        hrs = sb("hrs", [P, MH])
        ssh = sb("ssh", [P, 1])
        rsh = sb("rsh", [P, 1])
        h2 = sb("h2", [P, D])
        mix = h2
        brow = osg[0:HEADS, 0:RLEN]
        rl = sb("rl", [P, TILES, NG + NE])

        pay = sb("pay", [P, TILES, 2, 2], I32)
        desti = sb("desti", [P, TILES, 2], I32)
        xg = hn
        yb = lg[:, :, :].rearrange("p a b -> p (a b)")
        NI = MAXT + 2
        FIRST, LAST, ROWS = 0, NE, 2 * NE
        tabi = sb("tabi", [1, 2 * NE + NI], I32)
        rows = sb("rows", [P, TCOLS, 2], I32)
        row_g, row_s = sb("row_g", [P, 1], I32), sb("row_s", [P, 1], I32)
        wt_t = sb("wt_t", [P, 2], F32)
        pieces_of = lambda b, n: [b[:, i * PW:(i + 1) * PW] for i in range(n)]
        slot = [*pieces_of(wres, 6), slot_b[:, 0:PW], junk, gffn[:, :], xin[:, 0, :], xin[:, 1, :], h2[:, :]]
        slot_in = [*pieces_of(bias[:, :, :].rearrange("p h k -> p (h k)"), 2), h2[:, :], junk] * 2 + [h2[:, :], junk] * 2
        slot_out = [*pieces_of(wres, 6), gmix[:, :], wres[:, 0:PW]]
        ints = sb("ints", [P, NI + TILES], I32)
        route_e = sb("route_e", [P, TILES * (NG + 1)])
        iota_f, iota_m = sb("iota_f", [P, NI]), sb("iota_m", [P, NG])
        off_e = sb("off_e", [P, TILES + 1, NE])
        Mall = sqk[:, 0:TILES * NE]
        onesm = kvg[:, 0:P]
        strict = darg[:, 0, :]
        mh = q_sb

        T0, T1, J0, J1, S0, S1, O0, X0 = [pb(f"bank_{n}") for n in "t0 t1 j0 j1 s0 s1 o0 x0".split()]
        TB = [T0, T1]

        (ld_xn, ld_x0, ld_x1, ld_gn, ld_gf, ld_mix, st_mix, ld_w0, ld_w2, ld_wr, ld_c, ld_rb, ld_bias, st_brow, st_h, st_h2,
         st_tab, st_zero) = sems("ld_xnorm ld_x0 ld_x1 ld_gain ld_gain_ffn ld_mix st_mix ld_wkvg ld_wconv ld_wrouter ld_consts ld_relbias "
                                 "ld_bias st_brow st_h st_ffn st_table st_zero")
        LDX = [ld_x0, ld_x1]
        (pool_const, pe_brow, dve_brow, pe_bias, dve_bias) = sems("pool_const pe_brow dve_brow pe_bias dve_bias")
        (pe_qkT, pe_hnT, pe_s0, pe_s1, pe_kvg, pe_g, pe_pT0, pe_pT1, pe_q, pe_pv0, pe_o, pe_cin, pe_st,
         pe_vm, pe_h, pe_u, pe_om, pe_mixT, pe_y0, pe_y1, pe_h2T, pe_r) = sems(
            "pe_qkT pe_hnT pe_s0 pe_s1 pe_kvg pe_g pe_pT0 pe_pT1 pe_q pe_pv0 pe_o pe_cin pe_st "
            "pe_vm pe_h pe_u pe_om pe_mixT pe_y0 pe_y1 pe_h2T pe_r")
        (act_v, act_qT, act_ssx, act_ln, act_hnT, act_p0, act_g, act_kvg, act_pT0, act_D, act_p1, act_q,
         act_pT1, act_cin, act_vm, act_mixT, act_qk, act_om, act_ssh, act_h2T, act_ssn) = sems(
            "act_v act_qT act_ssx act_ln act_hnT act_p0 act_g act_kvg act_pT0 act_D act_p1 act_q "
            "act_pT1 act_cin act_vm act_mixT act_qk act_om act_ssh act_h2T act_ssn")
        (dve_kg, dve_az, dve_hn, dve_nm0, dve_L0, dve_L1, dve_nm1, dve_ca, dve_hnT, dve_gT, dve_darg, dve_qg,
         dve_pT0, dve_pT1, dve_kw, dve_att, dve_sd, dve_qkn, dve_C, dve_mix, dve_mixT, dve_h,
         dve_h0, dve_hn2, dve_h2T, dve_rl, dve_cy, dve_sqk, dve_hss) = sems(
            "dve_kg dve_az dve_hn dve_nm0 dve_L0 dve_L1 dve_nm1 dve_ca dve_hnT dve_gT dve_darg dve_qg "
            "dve_pT0 dve_pT1 dve_kw dve_att dve_sd dve_qkn dve_C dve_mix dve_mixT dve_h "
            "dve_h0 dve_hn2 dve_h2T dve_rl dve_cy dve_sqk dve_hss")
        (pool_rx, pool_rqk, pool_rhm, pool_rh, dve_const, dve_den) = sems("pool_rx pool_rqk pool_rhm pool_rh dve_const dve_den")
        (dve_chain, act_chain, pool_chain) = sems("dve_chain act_chain pool_chain")
        (dve_M, pe_pos, dve_pay, st_rows, dve_tab, dve_exps, act_exps) = sems(
            "dve_masks pe_positions dve_payload st_rows dve_tables dve_exponents act_exponentials")
        (hi0, lo0, act_hnh, dve_hnl) = sems("hi_proj lo_proj act_hn_high dve_hn_low")
        ld_piece = sems(" ".join(f"ld_piece{j}" for j in range(PIECES)))
        (ld_rows, ld_g, st_y, act_hi, lo_a, lo_b, pe_mx, pe_gup, pe_hT, pe_dnp, act_silu, act_mx, act_hT, act_y,
         dve_mh, dve_mx, dve_hT, dve_y, pool_rowg, dve_wt) = sems(
            "ld_rows ld_gathered st_y act_hi lo_a lo_b pe_mx pe_gateup pe_hT pe_down act_silu act_mx act_hT act_y "
            "dve_mh dve_mx dve_hT dve_y pool_rowg dve_wt")

        block = ctx.enter_context(nc.Block())

        def wait(eng, sem, value):
            if not (isinstance(value, int) and value <= 0):
                eng.wait_ge(sem, value)

        class Chain:

            def __init__(self, eng, sem):
                self.eng, self.sem, self.base, self.n, self.start = eng, sem, 0, 0, 0
                self.wait = eng.wait_ge

            def begin_tiles(self):
                self.start = self.base + self.n

            def at(self, base):
                self.base, self.n = self.start + base, 0

            def __call__(self, ins):
                self.n += 1
                ins.then_inc(self.sem, 1)
                self.wait(self.sem, self.base + self.n)

        def tiles(eng, body, chain=None, per_tile=0):
            base = 0

            def one(t, u, main, nxt, ahead, at):
                if chain is not None:
                    chain.at(at)
                body(t, u, main, nxt, ahead)
                return 0 if chain is None else chain.n
            if chain is not None:
                chain.begin_tiles()
            base += one(-2, 0, False, False, True, base)
            base += one(-1, 1, False, True, True, base)
            with eng.Fori(0, (TILES - 2) // 2) as pair:
                for u in range(2):
                    t = 2 * pair + u
                    n = one(t, u, True, True, True, t * per_tile + base)
                    assert n == per_tile, n
            base += (TILES - 2) * per_tile
            base += one(TILES - 2, 0, True, True, False, base)
            one(TILES - 1, 1, True, False, False, base)

        def tiles2(eng, body, chain=None, per_tile=0):
            if chain is not None:
                chain.begin_tiles()

            def one(t, u, first, last):
                if chain is not None:
                    chain.at(t * per_tile)
                body(t, u, first, last)
            one(0, 0, True, False)
            with eng.Fori(0, (TILES - 2) // 2) as pair:
                one(2 * pair + 1, 1, False, False)
                one(2 * pair + 2, 0, False, False)
            one(TILES - 1, (TILES - 1) % 2, False, True)

        def order(i):
            return (i % 2) * FC + i // 2 if i < 2 * FC else i

        def lo_ready(e, i):
            return (lo_a, e * VP + (i + 1)) if i < VP else (lo_b, e * (PIECES - VP) + (i - VP + 1))

        def split_free(i):
            return (pe_gup, i // 2 + 1) if i < 2 * FC else (pe_dnp, i - 2 * FC + 1)

        @block.sync
        def _(sp):
            w_v = w_in[0].rearrange("(k p) n -> p k n", p=P)
            a0 = AW + 2 * KVW

            def load_in(i):
                c0, j = (0, a0 + CH, a0 + CH + MW)[i // FC], i % FC
                sp.dma_start(slot_in[i].rearrange("p (k n) -> p k n", k=2),
                             w_v[:, 2 * j:2 * j + 2, c0:c0 + FF]).then_inc(ld_piece[i], 16)

            sp.dma_start(hn[:, :], x2[0:P, :]).then_inc(ld_xn, 16)
            sp.dma_start(gmix[:, :], norm_mix_g[0, :].partition_broadcast(P)).then_inc(ld_gn, 16)
            sp.dma_start(rbt[:, 0:HEADS], rel_bias).then_inc(ld_rb, 16)
            sp.dma_start(rbt[:, HEADS:], bucket_onehot).then_inc(ld_rb, 16)
            sp.dma_start(wi[:, :, 0:2 * KVW], w_v[:, :, AW:a0]).then_inc(ld_w0, 16)
            sp.dma_start(wi[:, :, 2 * KVW:KVG], w_v[:, :, NIN - 2 * MH:NIN]).then_inc(ld_w0, 16)
            for i in range(4):
                load_in(i)
            for src, dst in ((q_norm_g[0, :].partition_broadcast(P), gq[:, :]),
                             (k_norm_g[0, :].partition_broadcast(P), gk[:, :]),
                             (attn_sink[0, :].partition_broadcast(P), sink[:, :]),
                             (mlstm_norm_g[0].rearrange("(c p) -> p c", p=P), gml[:, :]),
                             (b_router_group[0, :].partition_broadcast(P), rbias[:, 0:NG]),
                             (b_router_expert[0, :].partition_broadcast(P), rbias[:, NG:]),
                             *((conv_w[0, k].rearrange("(c p) -> p c", p=P), cw[:, k, :]) for k in range(TAPS)),
                             (conv_b[0].rearrange("(c p) -> p c", p=P), cb[:, :]),
                             (gate_b[0, 0:MH].rearrange("(h o) -> h o", o=1), gb[0:MH, :]),
                             (gate_b[0, MH:].rearrange("(h o) -> h o", o=1), gb[32:32 + MH, :])):
                with nc.allow_non_contiguous_dma("small constants"):
                    sp.dma_start(dst, src).then_inc(ld_c, 16)
            sp.wait_ge(dve_brow, 1)
            sp.dma_start(bias_rows, brow[:, :]).then_inc(st_brow, 16)
            sp.wait_ge(pool_const, 6)
            for dst in (out, ffn_in):
                for half in range(2):
                    sp.dma_start(dst[S:, half * HALF:(half + 1) * HALF],
                                 cy[:, :, :].rearrange("p a b -> p (a b)")).then_inc(st_zero, 16)
            sp.dma_start(table_v, rows[:, :, :]).then_inc(st_tab, 16)
            sp.wait_ge(pe_hnT, 1)
            sp.dma_start(hn[:, :], x2[P:2 * P, :]).then_inc(ld_xn, 16)
            sp.dma_start(wi[:, :, KVG:], w_v[:, :, a0:a0 + CH]).then_inc(ld_w2, 16)
            for i in range(4, 8):
                sp.wait_ge(lo0, i - 3)
                load_in(i)
            sp.wait_ge(st_brow, 16)
            sp.wait_ge(lo0, 6)
            sp.dma_start(bias[:, :, :], bass.AP(tensor=bias_rows.tensor, offset=0,
                                                ap=[[1, P], [RLEN, HEADS], [1, 2 * P]])).then_inc(ld_bias, 16)
            for i in range(8, 12):
                sp.wait_ge(lo0, 7 + (i - 8))
                load_in(i)
            sp.dma_start(wr[:, :, 0:NG], w_router_group[0].rearrange("(p k) n -> p k n", p=P)).then_inc(ld_wr, 16)
            sp.dma_start(wr[:, :, NG:], w_router_expert[0].rearrange("(p k) n -> p k n", p=P)).then_inc(ld_wr, 16)

            def rows_of(dram, t):
                return dram[t * P:t * P + P, :] if isinstance(t, int) else dram[bass.ds(t * P, P), :]

            def load_out(i):
                sp.dma_start(slot_out[i], w_out[0, i * P:(i + 1) * P, :]).then_inc(ld_piece[i], 16)

            def load_mix(t):
                sp.wait_ge(st_mix, 16 * t + 16)
                if not (isinstance(t, int) and t == 0):
                    sp.wait_ge(pe_mixT, t)
                sp.dma_start(hn[:, :], rows_of(mix_rows, t)).then_inc(ld_mix, 16)

            def body(t, u, main, nxt, ahead):
                if main and not nxt:
                    sp.wait_ge(pe_hnT, TILES)
                    load_mix(0)
                    sp.wait_ge(pe_cin, TILES)
                    sp.wait_ge(dve_hn, TILES)
                    for i in range(OUTP):
                        if i == OUTP - 1:
                            sp.wait_ge(lo0, PIECES + 1)
                        load_out(i)
                if main and ahead:
                    sp.wait_ge(pe_hnT, t + 2)
                    sp.dma_start(hn[:, :], rows_of(x2, t + 2)).then_inc(ld_xn, 16)
                if main:
                    sp.wait_ge(dve_mix, t + 1)
                    sp.dma_start(rows_of(mix_rows, t), mix[:, :]).then_inc(st_mix, 16)
            tiles(sp, body)

            sp.wait_ge(dve_L1, TILES)
            sp.dma_start(xin[:, 0, :], x2[0:P, :]).then_inc(LDX[0], 16)
            sp.wait_ge(lo0, PIECES + OUTP)
            sp.dma_start(gffn[:, :], norm_ffn_g[0, :].partition_broadcast(P)).then_inc(ld_gf, 16)

            wg = w_gate[0].rearrange("e (p k) n -> e p k n", p=P)
            wu = w_up[0].rearrange("e (p k) n -> e p k n", p=P)
            wd = w_down[0].rearrange("e (c p) n -> e p c n", p=P)

            def load_piece(e, i):
                ei = slice(e, e + 1) if isinstance(e, int) else bass.ds(e, 1)
                dst = slot[i]
                if i < 2 * FC:
                    j, w = i // 2, (wg, wu)[i % 2]
                    dst, src = dst.rearrange("p (k n) -> p k n", k=2), w[ei, :, 2 * j:2 * j + 2, :].rearrange(
                        "e p k n -> (e p) k n")
                else:
                    src = wd[ei, :, i - 2 * FC, :].rearrange("e p n -> (e p) n")
                sp.dma_start(dst, src).then_inc(ld_piece[i], 16)

            def store_ffn_in(t):
                sp.wait_ge(dve_hn2, t + 1)
                sp.dma_start(rows_of(ffn_in, t), h2[:, :]).then_inc(st_h2, 16)

            def body2(t, u, first, last):
                if not last:
                    load_mix(t + 1)
                if not first:
                    store_ffn_in(t - 1)
                if not last:
                    if not first:
                        sp.wait_ge(st_h, 16 * t)
                        sp.wait_ge(dve_hn2, t)
                        sp.wait_ge(act_ssh, t)
                    sp.dma_start(xin[:, 1 - u, :], rows_of(x2, t + 1)).then_inc(LDX[1 - u], 16)
                if last:
                    for i in range(7):
                        load_piece(0, i)
                sp.wait_ge(dve_h, t + 1)
                sp.dma_start(rows_of(out, t), xin[:, u, :]).then_inc(st_h, 16)
            tiles2(sp, body2)
            store_ffn_in(TILES - 1)
            sp.wait_ge(act_ssh, TILES)
            load_piece(0, 7)
            sp.wait_ge(dve_hn2, TILES)
            load_piece(0, 8)
            sp.wait_ge(st_h, 16 * TILES)
            load_piece(0, 9)
            load_piece(0, 10)
            sp.wait_ge(pe_h2T, TILES)
            sp.wait_ge(st_h2, 16 * TILES)
            load_piece(0, 11)
            sp.wait_ge(st_rows, 16 * 2 * TILES)
            sp.dma_start(rows[:, :, :], table_v).then_inc(ld_rows, 16)
            sp.wait_ge(pe_mx, 1)
            with sp.Fori(1, NE) as e:
                for i in range(PIECES):
                    sp.wait_ge(*lo_ready(e - 1, i))
                    load_piece(e, i)

        @block.gpsimd
        def _(pool):
            chain = Chain(pool, pool_chain)
            chain(pool.memset(ident[:, :], 0.0))
            chain(pool.affine_select(out=ident[:, :], in_=ident[:, :], compare_op=ALU.not_equal, fill=1.0,
                                     base=0, pattern=[[-1, P]], channel_multiplier=1))
            chain(pool.memset(flip, 0.0))
            chain(pool.affine_select(out=flip, in_=flip, compare_op=ALU.not_equal, fill=1.0,
                                     base=1 - P, pattern=[[1, P]], channel_multiplier=1))
            chain(pool.memset(tri[:, :], 0.0))
            chain(pool.affine_select(out=tri[:, :], in_=tri[:, :], compare_op=ALU.is_ge, fill=NEG,
                                     base=0, pattern=[[1, P]], channel_multiplier=-1))
            pool.memset(mhalf[:, :], -0.5).then_inc(pool_const, 1)
            chain(pool.memset(selh[:, :, :], 0.0))
            chain(pool.affine_select(out=selh[:, :, :], in_=selh[:, :, :], compare_op=ALU.not_equal, fill=1.0,
                                     base=0, pattern=[[-1, MH], [0, P]], channel_multiplier=1))
            chain(pool.memset(selp[:, :, :], 0.0))
            sv = selp[:, :, :].rearrange("h c (a b) -> h c a b", a=2)
            chain(pool.affine_select(out=sv, in_=sv, compare_op=ALU.not_equal, fill=1.0, base=0,
                                     pattern=[[-2, PAIRS], [-1, 2], [0, P // 2]], channel_multiplier=1))
            pool.memset(warm[:, :], 0.0)
            pool.memset(ones_s[:, :], 1.0).then_inc(pool_const, 1)
            pool.memset(brow[:, :], NEG).then_inc(pool_const, 1)
            chain(pool.memset(rows[:, :, 1], 0))
            pool.iota(rows[:, :, 0], pattern=[[0, TCOLS]], base=S, channel_multiplier=1).then_inc(pool_const, 1)
            pool.memset(cy[:, :, :], 0.0).then_inc(pool_const, 1)
            pool.iota(ints[:, 0:NI], pattern=[[1, NI]], base=0, channel_multiplier=0)
            pool.iota(ints[:, NI:], pattern=[[P, TILES]], base=0, channel_multiplier=1)
            for e, n in ((eps_d, D), (eps_hd, HD), (eps_dv, DV)):
                pool.memset(e[:, :], n * EPS)
            for z in (GT[:, :], gt[:, :], mprev[:, :], Cst[:, :, :], kTw[:, 1, :], vw[:, 1, :],
                      cin[:, :, 0:TAPS - 1]):
                chain(pool.memset(z, 0.0))
            chain(pool.memset(pbias[:, :], NEG))
            pool.memset(vm[:, :, DV:VE], 1.0).then_inc(pool_const, 1)

            def pwait(sem, value):
                pool.wait_ge(sem, value)
                if not isinstance(value, int):
                    ticks.append(len(ticks))
                    pool.tensor_tensor(tick[:, len(ticks):len(ticks) + 1], mhalf[0:1, 0:1], mhalf[0:1, 0:1], ALU.mult)
            ticks = []

            def rsqrt(root, ss, done, add):
                chain(pool.tensor_tensor(root, ss, add[:, 0:root.shape[1]], ALU.add))
                pool.tensor_tensor(root, root, mhalf[:, 0:root.shape[1]], ALU.pow).then_inc(done, 1)

            def scatter_rows(a, b, n):
                pool.wait_ge(dve_pay, n)
                for t in range(a, b):
                    for c in range(2):
                        pool.indirect_dma_start(
                            out=table, out_offset=bass.IndirectOffsetOnAxis(
                                ap=desti[:, t, c:c + 1].bitcast(U32), axis=0),
                            in_=pay[:, t, c, :], in_offset=None).then_inc(st_rows, 16)

            def body(t, u, main, nxt, ahead):
                if nxt:
                    pool.wait_ge(dve_sqk, t + 2)
                    rsqrt(rqk[:, :], ssqk[:, :], pool_rqk, eps_hd)
                if main:
                    pool.wait_ge(dve_hss, t + 1)
                    rsqrt(hrs[:, :], hss[:, :], pool_rhm, eps_dv)
                if ahead:
                    pool.wait_ge(act_ssx, t + 3)
                    rsqrt(rsx[:, :], ssx[:, :], pool_rx, eps_d)
            tiles(pool, body, chain, 3)

            def body2(t, u, first, last):
                pool.wait_ge(act_ssh, t + 1)
                rsqrt(rsh[:, :], ssh[:, :], pool_rh, eps_d)
                if last:
                    pool.wait_ge(st_tab, 16)
                    scatter_rows(0, TILES - 2, 1)
            tiles2(pool, body2, chain, 1)

            scatter_rows(TILES - 2, TILES, 2)
            pool.wait_ge(st_rows, 16 * 2 * TILES)

            def gather():
                pool.indirect_dma_start(
                    out=xg[:, :], out_offset=None, in_=ffn_in,
                    in_offset=bass.IndirectOffsetOnAxis(ap=row_g[:, 0:1].bitcast(U32), axis=0)).then_inc(ld_g, 16)

            def scatter_add():
                pool.indirect_dma_start(
                    out=out, out_offset=bass.IndirectOffsetOnAxis(ap=row_s[:, 0:1].bitcast(U32), axis=0),
                    in_=yb[:, :], in_offset=None, compute_op=ALU.add).then_inc(st_y, 16)

            def pick(dst, t):
                at = tabi[0:1, ROWS + t:ROWS + t + 1] if isinstance(t, int) else tabi[0:1, bass.ds(t + ROWS, 1)]
                col = pool.value_load(at, min_val=0, max_val=TCOLS - 1)
                pool.tensor_copy(dst[:, :], rows[:, bass.ds(col, 1), 0:1].rearrange(
                    "p a c -> p (a c)")).then_inc(pool_rowg, 1)

            pool.wait_ge(st_h2, 16 * TILES)
            pool.wait_ge(pe_h2T, TILES)
            pool.wait_ge(ld_rows, 16)
            pool.tensor_copy(row_g[:, :], rows[:, 0, 0:1]).then_inc(pool_rowg, 1)
            pool.wait_ge(pool_rowg, 1)
            gather()
            pool.wait_ge(dve_tab, 1)
            pool.wait_ge(ld_g, 16)
            pick(row_g, 1)
            pool.wait_ge(pool_rowg, 2)
            pool.wait_ge(pe_mx, 1)
            gather()
            pool.wait_ge(st_h, 16 * TILES)

            def tile(t, split):
                pwait(ld_g, 16 * t + 32)
                pick(row_g, t + 2)
                pwait(pool_rowg, 2 * t + 3)
                pwait(pe_mx, t + 2)
                gather()
                split(VP, 2 * FC)
                pwait(act_y, t + 1)
                pwait(dve_y, t + 1)
                pick(row_s, t)
                pwait(pool_rowg, 2 * t + 4)
                scatter_add()
                split(2 * FC, PIECES)

            def inner_tiles(e):
                first = pool.value_load(tabi[0:1, FIRST + e:FIRST + e + 1] if isinstance(e, int) else
                                        tabi[0:1, bass.ds(e + FIRST, 1)], min_val=0, max_val=MAXT - 1)
                last = pool.value_load(tabi[0:1, LAST + e:LAST + e + 1] if isinstance(e, int) else
                                       tabi[0:1, bass.ds(e + LAST, 1)], min_val=0, max_val=MAXT - 1)
                with pool.If(first < last):
                    with pool.Fori(first, last) as t:
                        tile(t, lambda a, b: None)
                return last

            with pool.Fori(0, NE - 1) as e:
                last = inner_tiles(e)

                def split(a, b):
                    for i in range(a, b):
                        pool.wait_ge(act_hi, e * PIECES + (PIECES + i + 1))
                        at = slice(order(i) * PW, order(i) * PW + PW)
                        pool.tensor_tensor(wlo[:, at], slot[i], whi[:, at].bitcast(F32),
                                           ALU.subtract).then_inc(lo_ready(e + 1, i)[0], 1)
                tile(last, split)
            end = inner_tiles(NE - 1)
            tile(end, lambda a, b: None)
            pwait(st_y, 16 * end + 16)
            pwait(ld_g, 16 * end + 48)

        @block.scalar
        def _(act):
            chain = Chain(act, act_chain)

            def cp(dst, src):
                return act.activation(dst, src, ACT.Copy)

            def hn_high(t):
                act.wait_ge(act_hnT, t + 2)
                act.wait_ge(dve_hnT, t + 2)
                cp(mxh[:, :, :], hnT[:, :, :]).then_inc(act_hnh, 1)

            def in_high(i):
                act.wait_ge(ld_piece[i], 16)
                cp(whi[:, i * PW:(i + 1) * PW], slot_in[i]).then_inc(hi0, 1)

            def out_high(i):
                act.wait_ge(ld_piece[i], 32)
                act.wait_ge(pe_om, TILES)
                act.activation(whi[:, i * PW:(i + 1) * PW], slot_out[i], ACT.Copy,
                               scale=gml[:, i - AW // P:i - AW // P + 1] if i >= AW // P else 1.0).then_inc(hi0, 1)

            def mix_high(t, u):
                act.wait_ge(pe_mixT, t + 1)
                for b in range(2):
                    cp(MX[u][0][:, 4 * b:4 * b + 4, :].rearrange("p a b -> p (a b)"), TB[b][:, :]).then_inc(act_mixT, 1)

            def route_exp(count, n):
                act.wait_ge(dve_exps, n)
                act.activation(route_e[:, 0:count * (NG + 1)], route_e[:, 0:count * (NG + 1)],
                               ACT.Exp).then_inc(act_exps, 1)

            def exps(t, g, nm_done, done):
                act.wait_ge(nm_done, t + 1)
                for j in range(G):
                    h = g * G + j
                    act.activation(pr[:, j, :], lg[:, j, :], ACT.Exp, bias=anm[:, h:h + 1],
                                   accum_out=asum[:, h:h + 1])
                act.activation(aes[:, g * G:g * G + G], aes[:, g * G:g * G + G], ACT.Exp).then_inc(done, 1)

            def body(t, u, main, nxt, ahead):
                v = 1 - u
                if nxt:
                    act.wait_ge(pe_hnT, t + 2)
                    wait(act, pe_om, t + 1)
                    cp(hnT[:, 0:4, :].rearrange("p a b -> p (a b)"), T0[:, :]).then_inc(act_hnT, 1)
                    if not main:
                        hn_high(t)
                if main:
                    act.wait_ge(pe_qkT, t + 1)
                    wait(act, pe_s1, t)
                    cp(qT[:, :, :].rearrange("p a b -> p (a b)"), S0[:, :]).then_inc(act_qT, 1)
                    if nxt:
                        hn_high(t)
                    if not nxt:
                        act.wait_ge(pe_om, TILES)
                        mix_high(0, 0)
                    act.wait_ge(act_kvg, t + 1)
                    wait(act, pe_o, t)
                    cp(vw[:, u, :], kvg[:, KVW:2 * KVW]).then_inc(act_v, 1)
                    act.wait_ge(dve_az, t + 1)
                    chain(act.activation(gfz[32:32 + MH, 1, :], gfz[32:32 + MH, 0, :], ACT.Exp, scale=-1.0))
                    act.activation(gfz[32:32 + MH, 1, :], gfz[32:32 + MH, 1, :], ACT.Ln, bias=1.0).then_inc(act_ln, 1)
                    if not nxt:
                        for i in range(4):
                            out_high(i)
                if nxt:
                    act.wait_ge(pe_kvg, t + 2)
                    wait(act, dve_qkn, t + 1)
                    if main:
                        act.wait_ge(act_v, t + 1)
                    cp(kvg[:, :], J0[:, 0:KVG])
                    act.activation(sqk[:, 0:KVW], J0[:, 0:KVW], ACT.Square).then_inc(act_kvg, 1)
                    if not main:
                        for i in range(8):
                            in_high(i)
                if main:
                    act.wait_ge(dve_ca, t + 1)
                    act.activation(gbm[:, 3, :], gbm[:, 2, :], ACT.Exp, bias=mprev[:, :])
                    act.activation(GT[32:32 + MH, :], GT[0:MH, :], ACT.Exp, bias=gbm[:, 2, P - 1:P])
                    act.activation(GT[64:64 + MH, :], gbm[:, 1, :], ACT.Exp, scale=-1.0).then_inc(act_g, 1)
                    exps(t, 0, dve_nm0, act_p0)
                    if not nxt:
                        for i in range(4, OUTP):
                            out_high(i)
                if nxt:
                    act.wait_ge(pe_q, t + 2)
                    cp(q_sb[:, :], J1[:, :])
                    act.activation(sqk[:, KVW:], J1[:, :], ACT.Square).then_inc(act_q, 1)
                if main:
                    act.wait_ge(pe_pT0, t + 1)
                    cp(PT[:, 0:2, :, :].rearrange("p a b c -> p (a b c)"), T0[:, :]).then_inc(act_pT0, 1)
                    act.wait_ge(dve_darg, t + 1)
                    act.wait_ge(dve_gT, t + 1)
                    for h in range(MH):
                        ins = act.activation(dmat[:, h, :], darg[:, h, :], ACT.Exp, bias=gT[:, h:h + 1])
                    ins.then_inc(act_D, 1)
                    exps(t, 1, dve_nm1, act_p1)
                    act.wait_ge(pe_pT1, t + 1)
                    cp(PT[:, 0:2, :, :].rearrange("p a b c -> p (a b c)"), T0[:, :]).then_inc(act_pT1, 1)
                if nxt:
                    act.wait_ge(pe_cin, t + 2)
                    wait(act, dve_cy, t + 1)
                    cp(cin[:, :, TAPS - 1:], J0[:, :].rearrange("p (a b) -> p a b", a=CC)).then_inc(act_cin, 1)
                if main:
                    act.wait_ge(dve_den, t + 1)
                    wait(act, act_ssx, t + 2 if nxt else t + 1)
                    for h in range(MH):
                        c = h // 2
                        ins = act.activation(junk[:, h * DV:(h + 1) * DV], (S0, S1)[h % 2][:, c * VE:c * VE + DV],
                                             ACT.Square, accum_out=hsn[:, h:h + 1])
                    ins.then_inc(act_ssn, 1)
                if nxt:
                    act.wait_ge(pe_vm, t + 2)
                    wait(act, pe_u, t + 1)
                    cp(vm[:, :, 0:DV], J1[:, :].rearrange("p (a b) -> p a b", a=MH)).then_inc(act_vm, 1)
                if ahead:
                    act.wait_ge(ld_xn, 16 * (t + 3))
                    wait(act, dve_hn, t + 2)
                    if main:
                        act.wait_ge(act_ssn, t + 1)
                    act.activation(junk if main else lg[:, :, :].rearrange("p a b -> p (a b)"), hn[:, :], ACT.Square,
                                   accum_out=ssx[:, :]).then_inc(act_ssx, 1)
                if nxt and not main:
                    for i in range(8, PIECES):
                        in_high(i)
                if nxt:
                    act.wait_ge(dve_cy, t + 2)
                    wait(act, dve_qg, t + 1)
                    wait(act, pe_st, t + 1)
                    for c in range(CC):
                        ins = act.activation(qk[:, c, :], cy[:, c, :], ACT.Silu, bias=cb[:, c:c + 1])
                    ins.then_inc(act_qk, 1)
                if nxt:
                    act.wait_ge(pe_om, t + 2)
                    wait(act, dve_mix, t + 1)
                    act.activation(osg, J0[:, :], ACT.Sigmoid).then_inc(act_om, 1)
            tiles(act, body, chain, 1)

            def h2T_half(t):
                act.wait_ge(pe_h2T, t + 1)
                cp(h2T[:, 0:4, :].rearrange("p a b -> p (a b)"), S0[:, :]).then_inc(act_h2T, 1)

            def body2(t, u, first, last):
                if last:
                    route_exp(TILES - 2, 1)
                if not first:
                    h2T_half(t - 1)
                if not last:
                    mix_high(t + 1, 1 - u)
                act.wait_ge(dve_h, t + 1)
                act.activation(junk, xin[:, u, :], ACT.Square, accum_out=ssh[:, :]).then_inc(act_ssh, 1)

            tiles2(act, body2)
            h2T_half(TILES - 1)

            sg = cy[:, :, :].rearrange("p a b -> p (a b)")
            HF = FF // 2

            def silu(t, half):
                act.wait_ge(pe_gup, (FC + 1) * t + (1 if half == 0 else FC + 1))
                wait(act, dve_mh, 2 * t)
                act.activation(sg[:, half * HF:(half + 1) * HF], (J0, J1)[half][:, 0:HF], ACT.Silu).then_inc(act_silu, 1)

            def rows_hi(t):
                act.wait_ge(pe_mx, t + 1)
                if not (isinstance(t, int) and t == 0):
                    act.wait_ge(pe_gup, (FC + 1) * t)
                for b in range(2):
                    cp(mxh[:, 4 * b:4 * b + 4, :].rearrange("p a b -> p (a b)"), TB[b][:, :]).then_inc(act_mx, 1)

            def hidden_hi(t, half):
                act.wait_ge(pe_hT, 2 * t + half + 1)
                wait(act, pe_dnp, FC * t)
                cp(mhh[:, 2 * half:2 * half + 2, :].rearrange("p a b -> p (a b)"),
                   (S0, X0)[half][:, 0:HF]).then_inc(act_hT, 1)

            def weigh(t):
                act.wait_ge(pe_dnp, FC * (t + 1))
                act.wait_ge(dve_wt, t + 1)
                act.wait_ge(st_y, 16 * t)
                act.activation(yb[:, 0:HALF], S1[:, :], ACT.Copy, scale=wt_t[:, 0:1]).then_inc(act_y, 1)

            def split_hi(e, i, last):
                act.wait_ge(ld_piece[i], e * 16 + (48 if i < OUTP else 32))
                if last is not None:
                    sem, n = split_free(i)
                    act.wait_ge(sem, last * (FC + 1) + n + 1 if i < 2 * FC else last * FC + n)
                at = order(i) * PW
                cp(whi[:, at:at + PW], slot[i]).then_inc(act_hi, 1)

            route_exp(2, 2)
            act.wait_ge(pe_y1, TILES)
            for i in range(PIECES):
                split_hi(0, i, None)
            act.wait_ge(dve_tab, 1)
            rows_hi(0)

            def tile(t, split):
                act.activation(warm[:, 0:1], warm[:, 1:2], ACT.Silu)
                silu(t, 0)
                split(0, 2)
                hidden_hi(t, 0)
                split(2, 3)
                silu(t, 1)
                hidden_hi(t, 1)
                rows_hi(t + 1)
                split(3, 2 * FC)
                weigh(t)
                split(2 * FC, PIECES)

            def inner_tiles(e):
                first = act.value_load(tabi[0:1, FIRST + e:FIRST + e + 1] if isinstance(e, int) else
                                       tabi[0:1, bass.ds(e + FIRST, 1)], min_val=0, max_val=MAXT - 1)
                last = act.value_load(tabi[0:1, LAST + e:LAST + e + 1] if isinstance(e, int) else
                                      tabi[0:1, bass.ds(e + LAST, 1)], min_val=0, max_val=MAXT - 1)
                with act.If(first < last):
                    with act.Fori(first, last) as t:
                        tile(t, lambda a, b: None)
                return last

            with act.Fori(0, NE - 1) as e:
                last = inner_tiles(e)

                def split(a, b):
                    for i in range(a, b):
                        split_hi(e + 1, i, last)
                tile(last, split)
            tile(inner_tiles(NE - 1), lambda a, b: None)

        @block.tensor
        def _(pe):
            def transposes(src, dst):
                for b in range(2):
                    for i in range(4):
                        ins = pe.transpose(TB[b][:, i * P:(i + 1) * P], src[:, (4 * b + i) * P:(4 * b + i + 1) * P],
                                           ident[:, :])
                ins.then_inc(dst, 1)

            def three(out_, ah, al, bh, bl, start, stop):
                pe.matmul(out_, ah, bh, start=start, stop=False)
                pe.matmul(out_, ah, bl, start=False, stop=False)
                return pe.matmul(out_, al, bh, start=False, stop=stop)

            def project(bank, group, done, main):
                w_h, w_l = (w[:, group * FC * PW:(group + 1) * FC * PW].rearrange("p (k n) -> p k n", k=KC)
                            for w in (whi, wlo))
                for k in range(KC):
                    if not main and k % 2 == 0:
                        pe.wait_ge(lo0, group * FC + k // 2 + 1)
                    ins = three(bank[:, :], mxh[:, k, :], mxl[:, k, :], w_h[:, k, :], w_l[:, k, :], k == 0, k == KC - 1)
                ins.then_inc(done, 1)

            pe.wait_ge(ld_rb, 32)
            pe.matmul(X0[0:HEADS, 0:P], rbt[:, 0:HEADS], rbt[:, HEADS:], start=True, stop=True).then_inc(pe_brow, 1)
            pe.wait_ge(pool_const, 6)

            wo_h, wo_l = (w[:, 0:OUTP * PW].rearrange("p (k n) -> p k n", k=KC) for w in (whi, wlo))

            def mix_T(t):
                pe.wait_ge(ld_mix, 16 * (t + 1))
                transposes(hn, pe_mixT)

            def project_out(t, u, half):
                b, done, read = ((J0, pe_y0, dve_h0), (J1, pe_y1, dve_h))[half]
                if half == 0:
                    pe.wait_ge(dve_mixT, 2 * t + 2)
                if isinstance(t, int) and t == 0:
                    pe.wait_ge(lo0, PIECES + OUTP)
                    pe.wait_ge((act_om, act_vm)[half], TILES)
                wait(pe, read, t)
                cols = slice(half * HALF, (half + 1) * HALF)
                for k in range(KC):
                    ins = three(b[:, :], MX[u][0][:, k, :], MX[u][1][:, k, :], wo_h[:, k, cols], wo_l[:, k, cols],
                                k == 0, k == KC - 1)
                ins.then_inc(done, 1)

            def positions(count, n):
                pe.wait_ge(dve_M, n)
                if n > 1:
                    pe.wait_ge(dve_pay, n - 1)
                pe.matmul(O0[:, 0:count * NE], strict, Mall[:, 0:count * NE], start=True, stop=True)
                pe.matmul(O0[:, 2 * P:2 * P + count * NE], onesm, Mall[:, 0:count * NE], start=True,
                          stop=True).then_inc(pe_pos, 1)

            def body(t, u, main, nxt, ahead):
                v = 1 - u
                if nxt:
                    pe.wait_ge(dve_hn, t + 2)
                    transposes(hn, pe_hnT)
                if main and not nxt:
                    mix_T(0)
                if main:
                    wait(pe, dve_mix, t)
                    pe.wait_ge(dve_qkn, t + 1)
                    pe.wait_ge(dve_bias, 1)
                    qf = qn[:, :, :, :].rearrange("p j g d -> p j (g d)")
                    for j in range(G):
                        pe.transpose(S0[:, j * P:(j + 1) * P], qf[:, j, :], ident[:, :])
                    pe.transpose(S1[:, 0:P], kn[:, :, :].rearrange("p g d -> p (g d)"), ident[:, :])
                    pe.transpose(S1[0:64, P:2 * P], gt[:, :], ident[:, :]).then_inc(pe_qkT, 1)

                def scores(g, done):
                    for j in range(G):
                        b = (S0, S1)[j // 2]
                        for w, slot in ((0, v), (1, u)):
                            c = (j % 2) * 2 * P + w * P
                            ins = pe.matmul(b[:, c:c + P], qT[64 * g:64 * g + 64, j, :],
                                            kTw[64 * g:64 * g + 64, slot, :], start=True, stop=True)
                    ins.then_inc(done, 1)

                def probs_T(done):
                    for j in range(G):
                        for w in range(2):
                            c = (j % 2) * 2 * P + w * P
                            ins = pe.transpose(TB[j // 2][:, c:c + P], pr[:, j, w * P:(w + 1) * P], ident[:, :])
                    ins.then_inc(done, 1)

                def values(g, done):
                    for j in range(G):
                        h = g * G + j
                        for w, slot in ((0, v), (1, u)):
                            ins = pe.matmul(O0[:, h * HD:(h + 1) * HD], PT[:, j, w, :],
                                            vw[:, slot, g * HD:(g + 1) * HD], start=(w == 0), stop=(w == 1))
                    if done is not None:
                        ins.then_inc(done, 1)

                def conv_channels(cs):
                    for c in cs:
                        for k in range(KC):
                            ins = pe.matmul(J0[:, c * P:(c + 1) * P], wi[:, k, KVG + c * P:KVG + (c + 1) * P],
                                            hnT[:, k, :], start=(k == 0), stop=(k == KC - 1))
                    return ins

                if nxt:
                    pe.wait_ge(act_hnT, t + 2)
                    pe.wait_ge(dve_hnT, t + 2)
                    wait(pe, act_om, t + 1)
                    if not main:
                        pe.wait_ge(ld_w0, 32)
                    for k in range(KC):
                        ins = pe.matmul(J0[:, 0:KVG], hnT[:, k, :], wi[:, k, 0:KVG], start=(k == 0), stop=(k == KC - 1))
                    ins.then_inc(pe_kvg, 1)
                if main:
                    pe.wait_ge(act_qT, t + 1)
                    pe.wait_ge(dve_kg, t + 1)
                    scores(0, pe_s0)
                if nxt:
                    wait(pe, act_vm, t + 1)
                    pe.wait_ge(dve_hnl, t + 2)
                    project(J1, 0, pe_q, main)
                if main:
                    pe.wait_ge(act_qk, t + 1)
                    wait(pe, dve_C, t)
                    for c in range(PAIRS):
                        pe.transpose(X0[:, P + c * P:P + (c + 1) * P], qk[:, PAIRS + c, :], ident[:, :])
                    pe.wait_ge(act_g, t + 1)
                    if not nxt:
                        pe.wait_ge(dve_mixT, 2)
                    pe.transpose(X0[:, 0:P], GT[:, :], ident[:, :])
                    for h in range(MH):
                        pe.matmul(T0[:, h * P:(h + 1) * P], selh[:, h, :], gbm[:, 2, :], start=True, stop=True)
                    for c in range(PAIRS):
                        ins = pe.matmul(T1[:, c * P:(c + 1) * P], selp[:, c, :], gbm[:, 3, :], start=True, stop=True)
                    ins.then_inc(pe_g, 1)
                    pe.wait_ge(dve_L0, t + 1)
                    scores(1, pe_s1)
                    pe.wait_ge(act_p0, t + 1)
                    pe.wait_ge(dve_darg, t + 1)
                    pe.wait_ge(dve_qg, t + 1)
                    probs_T(pe_pT0)
                if nxt:
                    wait(pe, ld_w2, 16)
                    pe.wait_ge(act_kvg, t + 2)
                    ins = conv_channels(range(CC - 1) if main else range(CC))
                if main:
                    pe.wait_ge(act_v, t + 1)
                    pe.wait_ge(act_pT0, t + 1)
                    pe.wait_ge(dve_pT0, t + 1)
                    wait(pe, dve_att, t)
                    values(0, pe_pv0)
                    pe.wait_ge(act_p1, t + 1)
                    probs_T(pe_pT1)
                    pe.wait_ge(dve_L1, t + 1)
                    for h in range(MH):
                        r, c = 64 * (h % 2), h // 2
                        st_ins = pe.matmul((S0, S1)[h % 2][:, c * P:(c + 1) * P], qk[r:r + 64, PAIRS + c, :],
                                           qk[r:r + 64, c, :], start=True, stop=True)
                    st_ins.then_inc(pe_st, 1)
                    if nxt:
                        ins = conv_channels([CC - 1])
                    else:
                        project_out(0, 0, 0)
                if nxt:
                    ins.then_inc(pe_cin, 1)
                if main:
                    pe.wait_ge(act_pT1, t + 1)
                    pe.wait_ge(dve_pT1, t + 1)
                    values(1, pe_o)
                    pe.wait_ge(dve_sd, t + 1)
                    pe.wait_ge(act_vm, t + 1)
                    wait(pe, dve_C, t)
                    for h in range(MH):
                        r, c = 64 * (h % 2), h // 2
                        o = (S0, S1)[h % 2][:, c * VE:(c + 1) * VE]
                        pe.matmul(o, sd[:, h, :], vm[:, h, :], start=True, stop=False)
                        ins = pe.matmul(o, qg[r:r + 64, c, :], Cst[r:r + 64, c, :], start=False, stop=True)
                    ins.then_inc(pe_h, 1)
                    pe.wait_ge(dve_kw, t + 1)
                    pe.wait_ge(dve_gT, t + 1)
                    for h in range(MH):
                        r, c = 64 * (h % 2), h // 2
                        ins = pe.matmul(X0[r:r + 64, c * VE:(c + 1) * VE], kw[:, h, :], vm[:, h, :],
                                        start=True, stop=True)
                    ins.then_inc(pe_u, 1)
                if nxt:
                    pe.wait_ge(act_q, t + 2)
                    project(J1, 1, pe_vm, main)
                else:
                    if main:
                        project_out(0, 0, 1)
                if not main and nxt:
                    pe.wait_ge(dve_brow, 1)
                    pe.wait_ge(ld_bias, 16)
                    for b, bank in enumerate((S0, S1, O0, X0)):
                        ins = pe.matmul(bank[:, :], flip, bias[:, 2 * b:2 * b + 2, :].rearrange("p h k -> p (h k)"),
                                        start=True, stop=True)
                    ins.then_inc(pe_bias, 1)
                if nxt:
                    pe.wait_ge(act_cin, t + 2)
                    project(J0, 2, pe_om, main)
            tiles(pe, body)

            def h2_T(t):
                pe.wait_ge(dve_hn2, t + 1)
                wait(pe, act_h2T, t)
                wait(pe, dve_h2T, t)
                for b, bank in enumerate((S0, S1)):
                    for i in range(4):
                        ins = pe.transpose(bank[:, i * P:(i + 1) * P], h2[:, (4 * b + i) * P:(4 * b + i + 1) * P],
                                           ident[:, :])
                ins.then_inc(pe_h2T, 1)

            def router(t):
                pe.wait_ge(act_h2T, t + 1)
                pe.wait_ge(dve_h2T, t + 1)
                wait(pe, dve_rl, t)
                for k in range(KC):
                    ins = pe.matmul(X0[:, 0:NG + NE], h2T[:, k, :], wr[:, k, :], start=(k == 0), stop=(k == KC - 1))
                ins.then_inc(pe_r, 1)

            def body2(t, u, first, last):
                if not first:
                    project_out(t, u, 0)
                if not first:
                    h2_T(t - 1)
                if not last:
                    mix_T(t + 1)
                if not first:
                    project_out(t, u, 1)
                if last:
                    positions(TILES - 2, 1)
                if not first:
                    router(t - 1)

            pe.wait_ge(dve_mix, TILES)
            pe.wait_ge(dve_C, TILES)
            pe.wait_ge(ld_wr, 32)
            tiles2(pe, body2)
            h2_T(TILES - 1)
            router(TILES - 1)
            positions(2, 2)

            pe.wait_ge(dve_tab, 1)
            HF = FF // 2
            gu_hi, lo_a = (w[:, 0:2 * FC * PW].rearrange("p (g k n) -> p g k n", g=2, k=KC)
                            for w in (whi, wlo))
            dn_hi, lo_b = (w[:, 2 * FC * PW:].rearrange("p (c n) -> p c n", c=FC)
                            for w in (whi, wlo))

            def rows_T(t):
                pe.wait_ge(ld_g, 16 * (t + 1))
                wait(pe, dve_mx, 2 * t)
                transposes(xg, pe_mx)

            def hidden_T(t, half):
                pe.wait_ge(dve_mh, 2 * t + half + 1)
                if half == 0:
                    wait(pe, dve_hT, 2 * t)
                for c in range(2):
                    ins = pe.transpose((S0, X0)[half][:, c * P:(c + 1) * P],
                                       mh[:, half * HF + c * P:half * HF + (c + 1) * P], ident[:, :])
                ins.then_inc(pe_hT, 1)

            def tile(t, e):
                pe.wait_ge(dve_mx, 2 * t + 2)
                wait(pe, dve_mh, 2 * t)
                for half, bank in enumerate((J0, J1)):
                    cols = slice(half * HF, (half + 1) * HF)
                    for k in range(KC):
                        if half == 0 and k % 2 == 0:
                            for i in (k, k + 1):
                                pe.wait_ge(*lo_ready(e, i))
                        ins = three(bank[:, :], mxh[:, k, :], mxl[:, k, :], gu_hi[:, :, k, cols], lo_a[:, :, k, cols],
                                    k == 0, k == KC - 1)
                        if half == 1 and k % 2 == 1:
                            ins.then_inc(pe_gup, 1)
                        if half == 1 and k == KC // 2 - 1:
                            hidden_T(t, 0)
                    if half == 0:
                        ins.then_inc(pe_gup, 1)
                rows_T(t + 1)
                hidden_T(t, 1)
                wait(pe, act_y, t)
                wait(pe, dve_y, t)
                for c in range(FC):
                    if c % 2 == 0:
                        pe.wait_ge(dve_hT, 2 * t + c // 2 + 1)
                    pe.wait_ge(*lo_ready(e, 2 * FC + c))
                    for half, b in enumerate((S1, O0)):
                        cols = slice(half * HALF, (half + 1) * HALF)
                        ins = three(b[:, :], mhh[:, c, :], mhl[:, c, :], dn_hi[:, c, cols], lo_b[:, c, cols],
                                    c == 0, c == FC - 1)
                    ins.then_inc(pe_dnp, 1)

            def expert(e):
                first = pe.value_load(tabi[0:1, bass.ds(e + FIRST, 1)], min_val=0, max_val=MAXT - 1)
                last = pe.value_load(tabi[0:1, bass.ds(e + LAST, 1)], min_val=0, max_val=MAXT - 1)
                with pe.Fori(first, last + 1) as t:
                    tile(t, e)

            rows_T(0)
            with pe.Fori(0, NE) as e:
                expert(e)

        @block.vector
        def _(dve):
            chain = Chain(dve, dve_chain)
            dve.wait_ge(pool_const, 6)
            dve.wait_ge(pe_brow, 1)
            dve.tensor_copy(brow[:, P:2 * P], X0[0:HEADS, 0:P]).then_inc(dve_brow, 1)
            dve.wait_ge(ld_gn, 16)
            chain(dve.tensor_scalar(gmix[:, :], gmix[:, :], float(D) ** 0.5, None, ALU.mult))

            class Space:
                def __init__(self, bufs):
                    self.bufs, self.i, self.at = bufs, 0, 0

                def __call__(self, n):
                    while self.at + n > self.bufs[self.i].shape[1]:
                        self.i, self.at = self.i + 1, 0
                    self.at += n
                    return self.bufs[self.i][:, self.at - n:self.at]

            new = Space([lg[:, :, :].rearrange("p a b -> p (a b)"), vm[:, :, :].rearrange("p a b -> p (a b)"),
                         qk[:, :, :].rearrange("p a b -> p (a b)"), hnT[:, :, :].rearrange("p a b -> p (a b)")])

            def tt(out_, a, b, op):
                chain(dve.tensor_tensor(out_, a, b, op))

            def route(a, b, n):
                T_ = b - a

                def first_max(vals, w):
                    mx, idx = new(T_), new(T_)
                    chain(dve.tensor_reduce(mx, vals, AX, ALU.max))
                    oh = new(T_ * w).rearrange("p (t n) -> p t n", n=w)
                    bc = lambda v: v.unsqueeze(2).to_broadcast([P, T_, w])
                    tt(oh, vals, bc(mx), ALU.is_equal)
                    io, iom = (f[:, 0:w].unsqueeze(1).to_broadcast([P, T_, w]) for f in (iota_f[:, :], iota_m[:, :]))
                    chain(dve.scalar_tensor_tensor(oh, oh, -1.0e4, io, ALU.mult, ALU.add))
                    chain(dve.tensor_reduce(idx, oh, AX, ALU.min))
                    tt(oh, iom, bc(idx), ALU.is_equal)
                    return oh, mx

                if n == 1:
                    chain(dve.tensor_copy(iota_f[:, :], ints[:, 0:NI]))
                    chain(dve.tensor_scalar(iota_m[:, :], iota_f[:, 0:NG], -1.0e4, None, ALU.add))
                    chain(dve.tensor_scalar(strict, tri[:, :], -0.5, None, ALU.is_gt))
                    dve.tensor_tensor(strict, strict, ident[:, :], ALU.subtract)
                    dve.memset(onesm, 1.0)
                    chain(dve.memset(off_e[:, :], 0.0))
                gl = rl[:, a:b, 0:NG]
                ohg, gmx = first_max(gl, NG)
                tt(route_e[:, 0:T_ * NG].rearrange("p (t n) -> p t n", n=NG), gl,
                   gmx.unsqueeze(2).to_broadcast([P, T_, NG]), ALU.subtract)
                el = rl[:, a:b, NG:].rearrange("p t (g e) -> p t g e", g=NG)
                prod = new(T_ * NE).rearrange("p (t g e) -> p t g e", g=NG, e=EPG)
                tt(prod, el, ohg.unsqueeze(3).to_broadcast([P, T_, NG, EPG]), ALU.mult)
                ein = new(T_ * EPG).rearrange("p (t e) -> p t e", e=EPG)
                chain(dve.tensor_reduce(ein, prod.rearrange("p t g e -> p t e g"), AX, ALU.add))
                oh1, m1 = first_max(ein, EPG)
                e2 = new(T_ * EPG).rearrange("p (t e) -> p t e", e=EPG)
                chain(dve.scalar_tensor_tensor(e2, oh1, -3.0e38, ein, ALU.mult, ALU.add))
                oh2, m2 = first_max(e2, EPG)
                dve.tensor_tensor(route_e[:, T_ * NG:T_ * (NG + 1)], m2, m1, ALU.subtract).then_inc(dve_exps, 1)
                full = []
                for oh in (oh1, oh2):
                    full.append(new(T_ * NE))
                    tt(full[-1].rearrange("p (t g e) -> p t g e", g=NG, e=EPG),
                       ohg.unsqueeze(3).to_broadcast([P, T_, NG, EPG]),
                       oh.unsqueeze(2).to_broadcast([P, T_, NG, EPG]), ALU.mult)
                dve.tensor_tensor(Mall[:, 0:T_ * NE], full[0], full[1], ALU.add).then_inc(dve_M, 1)
                dve.wait_ge(act_exps, n)
                gs, wt = new(T_), new(2 * T_).rearrange("p (t c) -> p t c", c=2)
                chain(dve.tensor_reduce(gs, route_e[:, 0:T_ * NG].rearrange("p (t n) -> p t n", n=NG), AX, ALU.add))
                e21, dn = route_e[:, T_ * NG:T_ * (NG + 1)], new(T_)
                chain(dve.scalar_tensor_tensor(dn, e21, 1.0, gs, ALU.add, ALU.mult))
                chain(dve.reciprocal(dn, dn))
                dve.tensor_copy(wt[:, :, 0], dn)
                tt(wt[:, :, 1], dn, e21, ALU.mult)
                dve.tensor_copy(pay[:, a:b, :, 1].bitcast(F32), wt)
                for c in range(2):
                    ins = dve.tensor_copy(pay[:, a:b, c, 0], ints[:, NI + a:NI + b])
                chain(ins)
                dve.wait_ge(pe_pos, n)
                MC = T_ * NE
                pos, dst = new(MC), new(2 * T_).rearrange("p (t c) -> p t c", c=2)
                for t in range(T_):
                    tt(off_e[:, a + t + 1, :], off_e[:, a + t, :], O0[:, 2 * P + t * NE:2 * P + (t + 1) * NE], ALU.add)
                p3 = pos.rearrange("p (t e) -> p t e", e=NE)
                tt(p3, O0[:, 0:MC].rearrange("p (t e) -> p t e", e=NE), off_e[:, a:b, :], ALU.add)
                chain(dve.scalar_tensor_tensor(p3, iota_f[:, 0:NE].unsqueeze(1).to_broadcast([P, T_, NE]), float(S), p3,
                                               ALU.mult, ALU.add))
                for c in range(2):
                    tt(full[c], full[c], pos, ALU.mult)
                    chain(dve.tensor_reduce(dst[:, :, c], full[c].rearrange("p (t e) -> p t e", e=NE), AX, ALU.add))
                q = new(2 * T_).rearrange("p (t c) -> p t c", c=2)
                chain(dve.tensor_scalar(q, dst, 1.0 / P, -0.5 + 0.5 / P, ALU.mult, ALU.add))
                chain(dve.tensor_scalar(q, q, 1.5 * 2.0 ** 23, None, ALU.add))
                dve.tensor_scalar(dst, dst, float(TCOLS), None, ALU.mult)
                chain(dve.tensor_scalar(q, q, -1.5 * 2.0 ** 23, None, ALU.add))
                chain(dve.scalar_tensor_tensor(dst, q, -float(P * TCOLS - 1), dst, ALU.mult, ALU.add))
                dve.tensor_copy(desti[:, a:b, :], dst).then_inc(dve_pay, 1)

            def hn_low(t):
                dve.wait_ge(act_hnh, t + 2)
                dve.tensor_tensor(mxl[:, :, :], hnT[:, :, :], mxh[:, :, :].bitcast(F32), ALU.subtract)\
                    .then_inc(dve_hnl, 1)

            def mix_low(t, u):
                for b in range(2):
                    dve.wait_ge(act_mixT, 2 * t + b + 1)
                    dve.tensor_tensor(MX[u][1][:, 4 * b:4 * b + 4, :].rearrange("p a b -> p (a b)"), TB[b][:, :],
                                      MX[u][0][:, 4 * b:4 * b + 4, :].bitcast(F32).rearrange("p a b -> p (a b)"),
                                      ALU.subtract).then_inc(dve_mixT, 1)

            def in_low(i):
                dve.wait_ge(hi0, i + 1)
                at = slice(i * PW, (i + 1) * PW)
                dve.tensor_tensor(wlo[:, at], slot_in[i], whi[:, at].bitcast(F32), ALU.subtract).then_inc(lo0, 1)

            def out_low(i):
                dve.wait_ge(hi0, PIECES + i + 1)
                at = slice(i * PW, (i + 1) * PW)
                g = gml[:, i - AW // P:i - AW // P + 1] if i >= AW // P else 1.0
                dve.scalar_tensor_tensor(wlo[:, at], slot_out[i], g, whi[:, at].bitcast(F32), ALU.mult,
                                         ALU.subtract).then_inc(lo0, 1)

            def logits(t, g, s_done, l_done, nm_done):
                hs = slice(g * G, g * G + G)
                dve.wait_ge(s_done, t + 1)
                for b, S_ in enumerate((S0, S1)):
                    sv = S_[:, :].rearrange("p (j w k) -> p j w k", j=2, w=2)
                    lv = lg[:, 2 * b:2 * b + 2, :].rearrange("p j (w k) -> p j w k", w=2)
                    bv = bias[:, g * G + 2 * b:g * G + 2 * b + 2, :].rearrange("p j (w k) -> p j w k", w=2)
                    dve.scalar_tensor_tensor(lv[:, :, 0, :], sv[:, :, 0, :], pbias[:, :], bv[:, :, 0, :],
                                             ALU.add, ALU.add)
                    ins = dve.tensor_tensor(lv[:, :, 1, :], sv[:, :, 1, :], bv[:, :, 1, :], ALU.add)
                ins.then_inc(l_done, 1)
                dve.wait_ge(l_done, t + 1)
                chain(dve.tensor_reduce(amx[:, hs], lg[:, :, :], AX, ALU.max))
                chain(dve.tensor_tensor(amx[:, hs], amx[:, hs], sink[:, hs], ALU.max))
                chain(dve.tensor_scalar(anm[:, hs], amx[:, hs], -1.0, None, ALU.mult))
                dve.tensor_tensor(aes[:, hs], sink[:, hs], anm[:, hs], ALU.add).then_inc(nm_done, 1)

            def body(t, u, main, nxt, ahead):
                v = 1 - u
                if nxt:
                    dve.wait_ge(pe_hnT, t + 2)
                    wait(dve, pe_om, t + 1)
                    dve.tensor_copy(hnT[:, 4:8, :].rearrange("p a b -> p (a b)"), T1[:, :]).then_inc(dve_hnT, 1)
                    if not main:
                        hn_low(t)
                if nxt and not main:
                    dve.wait_ge(ld_c, 16 * (9 + TAPS))
                    dve.tensor_scalar(gml[:, :], gml[:, :], float(DV) ** 0.5, None, ALU.mult)
                    dve.tensor_scalar(gk[:, :], gk[:, :], float(HD) ** 0.5, None, ALU.mult).then_inc(dve_const, 1)
                    dve.wait_ge(dve_const, 1)
                    for i in range(8):
                        in_low(i)
                if main:
                    dve.wait_ge(pe_qkT, t + 1)
                    wait(dve, pe_s1, t)
                    dve.tensor_copy(kTw[:, u, :], S1[:, 0:P])
                    dve.tensor_scalar(giz[:, :], S1[0:MH, P:2 * P], gb[0:MH, :], None, ALU.add)
                    ins = dve.tensor_scalar(gfz[32:32 + MH, 2, :], S1[32:32 + MH, P:2 * P], gb[32:32 + MH, :], None,
                                            ALU.add)
                    ins.then_inc(dve_kg, 1)
                    dve.wait_ge(dve_kg, t + 1)
                    dve.scalar_tensor_tensor(gfz[32:32 + MH, 0, :], gfz[32:32 + MH, 2, :], -1.0,
                                             gfz[32:32 + MH, 2, :], ALU.mult, ALU.max).then_inc(dve_az, 1)
                    if nxt:
                        hn_low(t)
                    else:
                        mix_low(0, 0)
                    dve.wait_ge(act_ln, t + 1)
                    chain(dve.tensor_scalar(gfz[32:32 + MH, 2, :], gfz[32:32 + MH, 2, :], 0.0, None, ALU.min))
                    chain(dve.tensor_tensor(glf[:, :], gfz[32:32 + MH, 2, :], gfz[32:32 + MH, 1, :], ALU.subtract))
                    dve.tensor_tensor_scan(gbm[:, 0, :], ones_s[:, :], glf[:, :], 0.0, ALU.mult, ALU.add)
                    chain(dve.tensor_tensor_scan(gbm[:, 1, :], glf[:, :], giz[:, :], mprev[:, :], ALU.add, ALU.max))
                    wait(dve, pe_g, t)
                    dve.tensor_tensor(gbm[:, 2, :], gbm[:, 0, :], gbm[:, 1, :], ALU.subtract)
                    dve.tensor_tensor(GT[0:MH, :], giz[:, :], gbm[:, 0, :], ALU.subtract).then_inc(dve_ca, 1)
                    wait(dve, pe_pT1, t)
                    logits(t, 0, pe_s0, dve_L0, dve_nm0)
                    if not nxt:
                        for i in range(4):
                            out_low(i)
                    dve.wait_ge(pe_g, t + 1)
                    wait(dve, pe_h, t)
                    dve.tensor_tensor(darg[:, :, :], T0[:, :].rearrange("p (h s) -> p h s", h=MH),
                                      tri[:, :].unsqueeze(1).to_broadcast([P, MH, P]), ALU.add).then_inc(dve_darg, 1)
                    dve.wait_ge(act_qk, t + 1)
                    dve.tensor_tensor(qg[:, :, :], qk[:, 0:PAIRS, :],
                                      T1[:, 0:PAIRS * P].rearrange("p (c s) -> p c s", c=PAIRS), ALU.mult)
                    dve.tensor_copy(dec[:, :], T1[:, P - 1:PAIRS * P:P]).then_inc(dve_qg, 1)
                    dve.tensor_copy(gT[:, :], X0[:, 0:68]).then_inc(dve_gT, 1)
                    dve.wait_ge(act_g, t + 1)
                    dve.tensor_copy(mprev[:, :], gbm[:, 1, P - 1:P])
                    dve.wait_ge(pe_pT0, t + 1)
                    dve.tensor_copy(PT[:, 2:4, :, :].rearrange("p a b c -> p (a b c)"), T1[:, :]).then_inc(dve_pT0, 1)
                    logits(t, 1, pe_s1, dve_L1, dve_nm1)
                    dve.memset(pbias[:, :], 0.0)
                    dve.wait_ge(dve_gT, t + 1)
                    dve.scalar_tensor_tensor(
                        kw[:, :, :], X0[:, P:P + MH * DQK].rearrange("p (h d) -> p h d", h=MH), float(DQK) ** -0.5,
                        gT[:, 32:32 + MH].unsqueeze(2).to_broadcast([P, MH, DQK]), ALU.mult,
                        ALU.mult).then_inc(dve_kw, 1)
                if nxt:
                    dve.wait_ge(act_kvg, t + 2)
                    dve.wait_ge(act_q, t + 2)
                    dve.tensor_reduce(ssqk[:, :], sqk[:, :].rearrange("p (h d) -> p h d", d=HD), AX,
                                      ALU.add).then_inc(dve_sqk, 1)
                    dve.tensor_copy(gt[:, 0:MH], kvg[:, 2 * KVW:2 * KVW + MH])
                    dve.tensor_copy(gt[:, 32:32 + MH], kvg[:, 2 * KVW + MH:KVG])
                    q8 = q_sb[:, :].rearrange("p (h d) -> p h d", d=HD)
                    k2 = kvg[:, 0:KVW].rearrange("p (g d) -> p g d", g=KVH)
                    dve.tensor_tensor(q8, q8, gq[:, :].unsqueeze(1).to_broadcast([P, HEADS, HD]), ALU.mult)
                    chain(dve.tensor_tensor(k2, k2, gk[:, :].unsqueeze(1).to_broadcast([P, KVH, HD]), ALU.mult))
                    dve.wait_ge(pool_rqk, t + 2)
                    qv = qn[:, :, :, :].rearrange("p j g d -> p g j d")
                    for g in range(KVH):
                        dve.tensor_tensor(qv[:, g, :, :],
                                          q_sb[:, g * G * HD:(g + 1) * G * HD].rearrange("p (j d) -> p j d", j=G),
                                          rqk[:, KVH + g * G:KVH + (g + 1) * G].unsqueeze(2).to_broadcast([P, G, HD]),
                                          ALU.mult)
                    dve.tensor_tensor(kn[:, :, :], k2, rqk[:, 0:KVH].unsqueeze(2).to_broadcast([P, KVH, HD]),
                                      ALU.mult).then_inc(dve_qkn, 1)
                if main and not nxt:
                    for i in range(4, OUTP):
                        out_low(i)
                if main:
                    dve.wait_ge(pe_pT1, t + 1)
                    dve.tensor_copy(PT[:, 2:4, :, :].rearrange("p a b c -> p (a b c)"), T1[:, :]).then_inc(dve_pT1, 1)
                    dve.wait_ge(pe_st, t + 1)
                    dve.wait_ge(act_D, t + 1)
                    for b, S_ in enumerate((S0, S1)):
                        ins = dve.scalar_tensor_tensor(
                            sd[:, b::2, :], S_[:, 0:PAIRS * P].rearrange("p (c s) -> p c s", c=PAIRS),
                            float(DQK) ** -0.5, dmat[:, b::2, :], ALU.mult, ALU.mult)
                    ins.then_inc(dve_sd, 1)
                    dve.wait_ge(pe_o, t + 1)
                    dve.wait_ge(act_p1, t + 1)
                    chain(dve.tensor_tensor(arc[:, :], asum[:, :], aes[:, :], ALU.add))
                    chain(dve.reciprocal(arc[:, :], arc[:, :]))
                    wait(dve, st_mix, 16 * t)
                    dve.tensor_tensor(mix[:, 0:AW].rearrange("p (h d) -> p h d", h=HEADS),
                                      O0[:, :].rearrange("p (h d) -> p h d", h=HEADS),
                                      arc[:, :].unsqueeze(2).to_broadcast([P, HEADS, HD]), ALU.mult)\
                        .then_inc(dve_att, 1)
                    dve.wait_ge(pe_h, t + 1)
                    for b, S_ in enumerate((S0, S1)):
                        hv = S_[:, 0:PAIRS * VE].rearrange("p (c e) -> p c e", c=PAIRS)
                        ins = dve.tensor_copy(hrr[:, b::2], hv[:, :, DV])
                    ins.then_inc(dve_den, 1)
                    dve.wait_ge(dve_den, t + 1)
                    chain(dve.tensor_tensor(hden[:, :], hrr[:, :], gT[:, 64:64 + MH], ALU.max))
                    chain(dve.scalar_tensor_tensor(hden[:, :], hrr[:, :], -1.0, hden[:, :], ALU.mult, ALU.max))
                    chain(dve.reciprocal(hden[:, :], hden[:, :]))
                    chain(dve.tensor_tensor(hd2[:, :], hden[:, :], hden[:, :], ALU.mult))
                    dve.wait_ge(act_ssn, t + 1)
                    dve.tensor_tensor(hss[:, :], hsn[:, :], hd2[:, :], ALU.mult).then_inc(dve_hss, 1)
                    dve.wait_ge(pe_u, t + 1)
                    for c in range(PAIRS):
                        ins = dve.scalar_tensor_tensor(Cst[:, c, :], Cst[:, c, :], dec[:, c:c + 1],
                                                       X0[:, c * VE:(c + 1) * VE], ALU.mult, ALU.add)
                    ins.then_inc(dve_C, 1)
                    dve.wait_ge(pool_rhm, t + 1)
                    dve.wait_ge(act_om, t + 1)
                    chain(dve.tensor_tensor(hrr[:, :], hden[:, :], hrs[:, :], ALU.mult))
                    for h in range(MH):
                        c = h // 2
                        ins = dve.scalar_tensor_tensor(
                            mix[:, AW + h * DV:AW + (h + 1) * DV], (S0, S1)[h % 2][:, c * VE:c * VE + DV],
                            hrr[:, h:h + 1], osg[:, h * DV:(h + 1) * DV], ALU.mult, ALU.mult)
                    ins.then_inc(dve_mix, 1)
                if nxt:
                    dve.wait_ge(act_cin, t + 2)
                    wait(dve, act_qk, t + 1)
                    if not main:
                        dve.wait_ge(st_zero, 64)
                    for c in range(CC):
                        ins = dve.tensor_scalar(cy[:, c, :], cin[:, c, 0:P], cw[:, 0, c:c + 1], None, ALU.mult)
                    chain(ins)
                    for k in range(1, TAPS):
                        for c in range(CC):
                            ins = dve.scalar_tensor_tensor(cy[:, c, :], cin[:, c, k:k + P], cw[:, k, c:c + 1],
                                                           cy[:, c, :], ALU.mult, ALU.add)
                        chain(ins)
                    dve.tensor_copy(cin[:, :, 0:TAPS - 1], cin[:, :, P:P + TAPS - 1]).then_inc(dve_cy, 1)
                if nxt and not main:
                    dve.wait_ge(pe_bias, 1)
                    for b, bank in enumerate((S0, S1, O0, X0)):
                        ins = dve.tensor_copy(bias[:, 2 * b:2 * b + 2, :].rearrange("p h k -> p (h k)"), bank[:, :])
                    ins.then_inc(dve_bias, 1)
                    for i in range(8, PIECES):
                        in_low(i)
                if ahead:
                    dve.wait_ge(pool_rx, t + 3)
                    dve.scalar_tensor_tensor(hn[:, :], hn[:, :], rsx[:, :], gmix[:, :], ALU.mult,
                                             ALU.mult).then_inc(dve_hn, 1)
            tiles(dve, body, chain, 21)

            def h2T_half(t):
                dve.wait_ge(pe_h2T, t + 1)
                dve.tensor_copy(h2T[:, 4:8, :].rearrange("p a b -> p (a b)"), S1[:, :]).then_inc(dve_h2T, 1)

            def router_logits(t):
                dve.wait_ge(pe_r, t + 1)
                ti = slice(t, t + 1) if isinstance(t, int) else bass.ds(t, 1)
                dve.tensor_tensor(rl[:, ti, :].rearrange("p t n -> p (t n)"), X0[:, 0:NG + NE], rbias[:, :],
                                  ALU.add).then_inc(dve_rl, 1)

            def body2(t, u, first, last):
                if last:
                    dve.wait_ge(dve_rl, TILES - 2)
                    route(0, TILES - 2, 1)
                dve.wait_ge(LDX[u], 8 * t + (16 - 8 * u))
                dve.wait_ge(pe_y0, t + 1)
                dve.tensor_tensor(xin[:, u, 0:HALF], J0[:, :], xin[:, u, 0:HALF], ALU.add).then_inc(dve_h0, 1)
                if not first:
                    h2T_half(t - 1)
                if not last:
                    mix_low(t + 1, 1 - u)
                dve.wait_ge(pe_y1, t + 1)
                dve.tensor_tensor(xin[:, u, HALF:], J1[:, :], xin[:, u, HALF:], ALU.add).then_inc(dve_h, 1)
                dve.wait_ge(pool_rh, t + 1)
                dve.wait_ge(dve_h, t + 1)
                wait(dve, st_h2, 16 * t)
                hv = h2[:, :].rearrange("q (k p) -> q p k", k=KC)
                dve.scalar_tensor_tensor(hv, xin[:, u, :].rearrange("q (p k) -> q p k", k=KC), rsh[:, :],
                                         gffn[:, :].rearrange("q (p k) -> q p k", k=KC), ALU.mult,
                                         ALU.mult).then_inc(dve_hn2, 1)
                if not first:
                    router_logits(t - 1)

            dve.wait_ge(ld_gf, 16)
            chain(dve.tensor_scalar(gffn[:, :], gffn[:, :], float(D) ** 0.5, None, ALU.mult))
            dve.wait_ge(st_mix, 16 * TILES)
            tiles2(dve, body2)
            h2T_half(TILES - 1)
            router_logits(TILES - 1)

            dve.wait_ge(dve_rl, TILES)
            route(TILES - 2, TILES, 2)
            one = slice(0, 1)
            T_ = TILES
            cnt = off_e[one, T_, :]
            cmp = new(NE * (T_ - 1))[one, :].rearrange("p (e k) -> p e k", e=NE)
            thr = new(T_ - 1)[one, :]
            chain(dve.tensor_scalar(thr, iota_f[one, 1:T_], float(P), None, ALU.mult))
            tt(cmp, cnt.unsqueeze(2).to_broadcast([1, NE, T_ - 1]), thr.unsqueeze(1).to_broadcast([1, NE, T_ - 1]),
               ALU.is_gt)
            te, cum = new(NE)[one, :], new(NE)[one, :]
            chain(dve.tensor_reduce(te, cmp, AX, ALU.add))
            chain(dve.tensor_scalar(te, te, 1.0, None, ALU.add))
            on = new(NE)[one, :]
            chain(dve.memset(on, 1.0))
            chain(dve.tensor_tensor_scan(cum, on, te, 0.0, ALU.mult, ALU.add))
            NTL = NI
            big = new(NTL * NE)[one, :].rearrange("p (t e) -> p t e", e=NE)
            et, fs = new(NTL)[one, :], new(NTL)[one, :]
            tt(big, cum.unsqueeze(1).to_broadcast([1, NTL, NE]),
               iota_f[one, 0:NTL].unsqueeze(2).to_broadcast([1, NTL, NE]), ALU.is_le)
            chain(dve.tensor_reduce(et, big, AX, ALU.add))
            tt(big, big, te.unsqueeze(1).to_broadcast([1, NTL, NE]), ALU.mult)
            chain(dve.tensor_reduce(fs, big, AX, ALU.add))
            chain(dve.tensor_scalar(et, et, float(S // P), None, ALU.mult))
            tt(et, et, iota_f[one, 0:NTL], ALU.add)
            tt(et, et, fs, ALU.subtract)
            chain(dve.tensor_scalar(et, et, float(TCOLS - 1), None, ALU.min))
            chain(dve.tensor_copy(tabi[:, ROWS:ROWS + NTL], et))
            chain(dve.tensor_tensor(tabi[:, FIRST:FIRST + NE], cum, te, ALU.subtract))
            dve.tensor_scalar(tabi[:, LAST:LAST + NE], cum, -1.0, None, ALU.add).then_inc(dve_tab, 1)

            sg = cy[:, :, :].rearrange("p a b -> p (a b)")
            HF = FF // 2

            def hidden(t, half):
                cols = slice(half * HF, (half + 1) * HF)
                dve.wait_ge(act_silu, 2 * t + half + 1)
                wait(dve, pe_hT, 2 * t)
                dve.tensor_tensor(mh[:, cols], sg[:, cols], (J0, J1)[half][:, HF:], ALU.mult).then_inc(dve_mh, 1)

            def rows_lo(t):
                for b in range(2):
                    dve.wait_ge(act_mx, 2 * t + b + 1)
                    at = slice(4 * b, 4 * b + 4)
                    dve.tensor_tensor(mxl[:, at, :].rearrange("p a b -> p (a b)"), TB[b][:, :],
                                      mxh[:, at, :].bitcast(F32).rearrange("p a b -> p (a b)"), ALU.subtract).then_inc(dve_mx, 1)

            def hidden_lo(t, half):
                dve.wait_ge(act_hT, 2 * t + half + 1)
                at = slice(2 * half, 2 * half + 2)
                dve.tensor_tensor(mhl[:, at, :].rearrange("p a b -> p (a b)"), (S0, X0)[half][:, 0:HF],
                                  mhh[:, at, :].bitcast(F32).rearrange("p a b -> p (a b)"), ALU.subtract).then_inc(dve_hT, 1)

            def weigh(t):
                dve.wait_ge(pe_dnp, FC * (t + 1))
                dve.wait_ge(dve_wt, t + 1)
                dve.wait_ge(st_y, 16 * t)
                dve.tensor_scalar(yb[:, HALF:], O0[:, :], wt_t[:, 0:1], None, ALU.mult).then_inc(dve_y, 1)

            def split_lo(e, i):
                dve.wait_ge(act_hi, e * PIECES + (i + 1))
                at = slice(order(i) * PW, order(i) * PW + PW)
                dve.tensor_tensor(wlo[:, at], slot[i], whi[:, at].bitcast(F32),
                                  ALU.subtract).then_inc(lo_ready(e, i)[0], 1)

            def tile(t, split):
                wait(dve, act_y, t)
                wait(dve, dve_y, t)
                col = dve.value_load(tabi[0:1, bass.ds(t + ROWS, 1)], min_val=0, max_val=TCOLS - 1)
                dve.tensor_copy(wt_t[:, 0:1], rows[:, bass.ds(col, 1), 1:2].rearrange("p a c -> p (a c)")
                                .bitcast(F32)).then_inc(dve_wt, 1)
                hidden(t, 0)
                split(0, 1)
                hidden_lo(t, 0)
                split(1, 2)
                hidden(t, 1)
                hidden_lo(t, 1)
                rows_lo(t + 1)
                split(2, VP)
                weigh(t)

            def inner_tiles(e):
                first = dve.value_load(tabi[0:1, FIRST + e:FIRST + e + 1] if isinstance(e, int) else
                                       tabi[0:1, bass.ds(e + FIRST, 1)], min_val=0, max_val=MAXT - 1)
                last = dve.value_load(tabi[0:1, LAST + e:LAST + e + 1] if isinstance(e, int) else
                                      tabi[0:1, bass.ds(e + LAST, 1)], min_val=0, max_val=MAXT - 1)
                with dve.If(first < last):
                    with dve.Fori(first, last) as t:
                        tile(t, lambda a, b: None)
                return last

            for i in range(VP):
                split_lo(0, i)
            rows_lo(0)
            for i in range(VP, PIECES):
                split_lo(0, i)
            dve.wait_ge(ld_rows, 16)
            with dve.Fori(0, NE - 1) as e:
                last = inner_tiles(e)

                def split(a, b):
                    for i in range(a, b):
                        split_lo(e + 1, i)
                tile(last, split)
            tile(inner_tiles(NE - 1), lambda a, b: None)


_INS = ["x", "rel_bias", "norm_mix_g", "w_in", "q_norm_g", "k_norm_g", "attn_sink", "conv_w", "conv_b", "gate_b",
        "mlstm_norm_g", "w_out", "norm_ffn_g", "w_router_group", "b_router_group", "w_router_expert",
        "b_router_expert", "w_gate", "w_up", "w_down"]


def bucket_one_hot(buckets, window):
    import math
    import numpy as np
    exact = buckets // 2
    m = np.zeros((buckets, window), np.float32)
    for dist in range(window):
        b = dist if dist < exact else min(buckets - 1, exact + int(
            math.log(dist / exact) / math.log(window / exact) * (buckets - exact)))
        m[b, window - 1 - dist] = 1.0
    return m


def kernel(**inputs):
    import numpy as _np
    import concourse.bacc as _bacc
    from concourse import mybir as _mybir
    from concourse.bass_utils import run_bass_kernel_spmd as _run

    nc = _bacc.Bacc("TRN2", target_bir_lowering=False, num_devices=1)
    arrays, args = {}, []
    for name in _INS:
        a = _np.ascontiguousarray(inputs[name])
        arrays[f"in_{name}_dram"] = a
        args.append(nc.dram_tensor(f"in_{name}_dram", a.shape, _mybir.dt.from_np(a.dtype), kind="ExternalInput").ap())
    a = bucket_one_hot(inputs["rel_bias"].shape[0], 128)
    arrays["bucket_dram"] = a
    args.append(nc.dram_tensor("bucket_dram", a.shape, _mybir.dt.float32, kind="ExternalInput").ap())
    _, seq, width = inputs["x"].shape
    args.append(nc.dram_tensor("out_0_dram", (seq + 128, width), _mybir.dt.float32, kind="ExternalOutput").ap())
    hymba_layer_program(nc, *args)
    r = _run(nc, [arrays], core_ids=[0])
    return r.results[0]["out_0_dram"][:seq].reshape(1, seq, width)
```
